# Optimizing a Trainium2 kernel written in Bass

```python
import math
import jax, jax.numpy as jnp
from jax import lax
import numpy as np

D_MODEL = 1024
BATCH = 1
SEQ = 256
DEPTH = 2
DEC_BATCH = 8
DEC_SEQ = 1
PAST_LEN = 1024
PAGE_SIZE = 128

HEAD_DIM = 64
MIX_WIDTH = D_MODEL
MEM_HEADS = 4
MEM_LEN = 256
MEMQ = MEM_HEADS * HEAD_DIM
TOK_HEADS = (MIX_WIDTH - MEMQ) // HEAD_DIM
QA = TOK_HEADS * HEAD_DIM
NSA_KV_GROUPS = 3
NSA_HPG = TOK_HEADS // NSA_KV_GROUPS
KVW = NSA_KV_GROUPS * HEAD_DIM
CMP_LEN = 32
CMP_STRIDE = 16
CMP_RATIO = CMP_LEN // CMP_STRIDE
CMP_HID = 2 * HEAD_DIM
SEL_LEN = 64
SEL_TOPK = 16
WINDOW = 512
Q_BLOCK = 128
GATE_W = 3 * TOK_HEADS
NSA_COLS = (QA, KVW, KVW, KVW, KVW, KVW, KVW, GATE_W, MEMQ)
C_A = sum(NSA_COLS)
RWKV_HEADS = TOK_HEADS
RWKV_WIDTH = RWKV_HEADS * HEAD_DIM
DECAY_RANK = 64
ICLR_RANK = 64
GATE_RANK = 128
RWKV_GN_EPS = 64e-5
RWKV_COLS = (RWKV_WIDTH, RWKV_WIDTH, RWKV_WIDTH, DECAY_RANK, ICLR_RANK, GATE_RANK)
SHIFT_W = sum(RWKV_COLS)
B_COLS = (SHIFT_W, MEMQ)
C_B = sum(B_COLS)
N_GROUPS = 4
E_PER_GROUP = 8
N_EXPERTS = N_GROUPS * E_PER_GROUP
TOPK_FINE = 2
D_EXPERT = D_MODEL // 2
MOE_BLOCK = 64
N_A = (DEPTH + 1) // 2
N_B = DEPTH // 2
NEG = -1e30
BIG = 1e30

kernel_name = 'hybrid_nsa_rwkv7_hmoe_decode_step'

def rms_norm(x, g, eps=1e-6):
    xf = x.astype(jnp.float32)
    return xf * lax.rsqrt(jnp.mean(xf * xf, axis=-1, keepdims=True) + eps) * g

def masked_softmax(s, mask):
    s = jnp.where(mask, s.astype(jnp.float32), NEG)
    m = jnp.max(s, axis=-1, keepdims=True)
    e = jnp.where(mask, jnp.exp(s - m), 0.0)
    return e / jnp.maximum(jnp.sum(e, axis=-1, keepdims=True), 1e-30)

def alibi_slopes(n):
    return jnp.exp2(-8.0 * jnp.arange(1, n + 1, dtype=jnp.float32) / n)

def split_cols(p, widths):
    offs = np.cumsum((0,) + tuple(widths))
    return [p[..., int(offs[i]):int(offs[i + 1])] for i in range(len(widths))]

def nsa_project(h, w_in, q_gain, k_gain):
    B, T, _ = h.shape
    q, kc, vc, ks, vs, kw, vw, g, mq = split_cols(h @ w_in, NSA_COLS)
    hd = lambda z, n: z.reshape(B, T, n, HEAD_DIM)
    G = NSA_KV_GROUPS
    return (rms_norm(hd(q, TOK_HEADS), q_gain), hd(kc, G), hd(vc, G),
            rms_norm(hd(ks, G), k_gain[1]), hd(vs, G),
            rms_norm(hd(kw, G), k_gain[2]), hd(vw, G),
            jax.nn.sigmoid(g.astype(jnp.float32)).reshape(B, T, TOK_HEADS, 3), mq)

def nsa_compress(rows, pe, w1, b1, w2):
    B, L, G, Dh = rows.shape
    n_chunk = L // CMP_STRIDE
    n_cmp = n_chunk - CMP_RATIO + 1
    chunks = rows[:, :n_chunk * CMP_STRIDE].reshape(B, n_chunk, CMP_STRIDE, G, Dh)
    pe_r = pe.reshape(CMP_RATIO, CMP_STRIDE, 1, Dh)
    w1_r = w1.reshape(CMP_RATIO, CMP_STRIDE, Dh, CMP_HID)
    hid = b1
    for r in range(CMP_RATIO):
        hid = hid + jnp.einsum('bnlgd,ldf->bngf', chunks[:, r:r + n_cmp] + pe_r[r], w1_r[r])
    return jnp.einsum('bngf,fd->bngd', jax.nn.gelu(hid), w2)

def nsa_summaries(kc, vc, pe, w1, b1, w2, k_gain):
    ck = rms_norm(nsa_compress(kc, pe[0], w1[0], b1[0], w2[0]), k_gain)
    cv = nsa_compress(vc, pe[1], w1[1], b1[1], w2[1])
    c_end = jnp.arange(ck.shape[1]) * CMP_STRIDE + CMP_LEN - 1
    return ck, cv, c_end

def sel_blocks(rows):
    B, L, G, Dh = rows.shape
    ns = -(-L // SEL_LEN)
    rows = jnp.pad(rows, ((0, 0), (0, ns * SEL_LEN - L), (0, 0), (0, 0)))
    return rows.reshape(B, ns, SEL_LEN, G, Dh).transpose(0, 3, 1, 2, 4)

def cmp_sel_map(n_cmp, n_sel):
    c0 = jnp.arange(n_cmp) * CMP_STRIDE
    s0 = jnp.arange(n_sel) * SEL_LEN
    return ((c0[:, None] < s0[None, :] + SEL_LEN) & (c0[:, None] + CMP_LEN > s0[None, :])).astype(jnp.float32)

def nsa_block(q, gates, q_pos, ck, cv, c_end, ks_blk, vs_blk, kw, vw, kw_pos, cmp_to_sel):
    B, T, H, Dh = q.shape
    G = NSA_KV_GROUPS
    qg = (q.reshape(B, T, G, NSA_HPG, Dh) * (Dh ** -0.5)).astype(jnp.float32)
    slope = alibi_slopes(H).reshape(G, NSA_HPG)[None, :, None, :]
    t = q_pos
    s_c = jnp.einsum('btgjd,bngd->bgtjn', qg, ck)
    dist_c = t[:, None] - c_end[None, :]
    s_c = s_c - slope[..., None] * dist_c.astype(jnp.float32)[None, None, :, None, :]
    p_c = masked_softmax(s_c, (dist_c >= 0)[None, None, :, None, :])
    o_c = jnp.einsum('bgtjn,bngd->btgjd', p_c, cv)
    n_sel = ks_blk.shape[2]
    k_top = min(SEL_TOPK, n_sel)
    imp = jnp.einsum('bgtjn,ns->bgts', p_c, cmp_to_sel)
    blk = jnp.arange(n_sel)
    cur = (t // SEL_LEN)[:, None]
    forced = (blk == 0) | (blk == cur) | (blk == cur - 1)
    valid = blk * SEL_LEN <= t[:, None]
    score = jnp.where(valid, jnp.where(forced, BIG, imp), -BIG)
    _, idx = lax.top_k(score, k_top)
    bi = jnp.arange(B)[:, None, None, None]
    gi = jnp.arange(G)[None, :, None, None]
    k_sel = ks_blk[bi, gi, idx]
    v_sel = vs_blk[bi, gi, idx]
    s_s = jnp.einsum('btgjd,bgtnkd->bgtjnk', qg, k_sel)
    pos_s = idx[..., None] * SEL_LEN + jnp.arange(SEL_LEN)
    dist_s = t[None, None, :, None, None] - pos_s
    s_s = s_s - slope[..., None, None] * dist_s.astype(jnp.float32)[:, :, :, None]
    mask_s = (dist_s >= 0)[:, :, :, None]
    p_s = masked_softmax(s_s.reshape(B, G, T, NSA_HPG, -1), mask_s.reshape(B, G, T, 1, -1))
    o_s = jnp.einsum('bgtjnk,bgtnkd->btgjd', p_s.reshape(s_s.shape), v_sel)
    s_w = jnp.einsum('btgjd,bsgd->bgtjs', qg, kw)
    dist_w = t[:, None] - kw_pos[None, :]
    mask_w = (dist_w >= 0) & (dist_w <= WINDOW) & (kw_pos[None, :] >= 0)
    s_w = s_w - slope[..., None] * dist_w.astype(jnp.float32)[None, None, :, None, :]
    p_w = masked_softmax(s_w, mask_w[None, None, :, None, :])
    o_w = jnp.einsum('bgtjs,bsgd->btgjd', p_w, vw)
    gt = gates.reshape(B, T, G, NSA_HPG, 3)
    o = gt[..., 0:1] * o_c + gt[..., 1:2] * o_s + gt[..., 2:3] * o_w
    return o.reshape(B, T, H * Dh)

def nsa_prompt(q, kc, vc, ks, vs, kw, vw, gates, cmp_prm):
    B, S, H, Dh = q.shape
    ck, cv, c_end = nsa_summaries(kc, vc, *cmp_prm)
    ks_blk, vs_blk = sel_blocks(ks), sel_blocks(vs)
    cmp_to_sel = cmp_sel_map(ck.shape[1], ks_blk.shape[2])
    pad = ((0, 0), (WINDOW, 0), (0, 0), (0, 0))
    kw_pad, vw_pad = jnp.pad(kw, pad), jnp.pad(vw, pad)
    nqb = S // Q_BLOCK
    qb = q.reshape(B, nqb, Q_BLOCK, H, Dh).swapaxes(0, 1)
    gb = gates.reshape(B, nqb, Q_BLOCK, H, 3).swapaxes(0, 1)
    starts = jnp.arange(nqb) * Q_BLOCK

    def one(args):
        qi, gi, q0 = args
        kwi = lax.dynamic_slice_in_dim(kw_pad, q0, WINDOW + Q_BLOCK, axis=1)
        vwi = lax.dynamic_slice_in_dim(vw_pad, q0, WINDOW + Q_BLOCK, axis=1)
        kw_pos = q0 - WINDOW + jnp.arange(WINDOW + Q_BLOCK)
        return nsa_block(qi, gi, q0 + jnp.arange(Q_BLOCK), ck, cv, c_end,
                         ks_blk, vs_blk, kwi, vwi, kw_pos, cmp_to_sel)

    out = lax.map(one, (qb, gb, starts))
    return out.swapaxes(0, 1).reshape(B, S, H * Dh)

def nsa_sample(q, kc, vc, ks, vs, kw, vw, gates, pool_kc, pool_vc, pool_ks, pool_vs,
               win_k, win_v, page_table, cmp_prm):
    Bd, T = q.shape[:2]
    past = page_table.shape[1] * PAGE_SIZE

    def full(pool, new):
        old = pool[page_table].reshape(Bd, past, NSA_KV_GROUPS, HEAD_DIM)
        return jnp.concatenate([old, new], axis=1)

    ck, cv, c_end = nsa_summaries(full(pool_kc, kc), full(pool_vc, vc), *cmp_prm)
    ks_blk, vs_blk = sel_blocks(full(pool_ks, ks)), sel_blocks(full(pool_vs, vs))
    cmp_to_sel = cmp_sel_map(ck.shape[1], ks_blk.shape[2])
    wb = win_k.shape[1]
    kw_all = jnp.concatenate([win_k, kw], axis=1)
    vw_all = jnp.concatenate([win_v, vw], axis=1)
    kw_pos = past - wb + jnp.arange(wb + T)
    out = nsa_block(q, gates, past + jnp.arange(T), ck, cv, c_end, ks_blk, vs_blk,
                    kw_all, vw_all, kw_pos, cmp_to_sel)
    return out, kw_all[:, T:], vw_all[:, T:]

def rwkv_mix(Pr, shift_prev, S0, mu, w0, w_up, a0, a_up, g_up, k_k, k_a, r_k, ln_w, ln_b):
    B, T, _ = Pr.shape
    H, N = RWKV_HEADS, HEAD_DIM
    prev = jnp.concatenate([shift_prev[:, None, :].astype(Pr.dtype), Pr[:, :-1]], axis=1)
    X = Pr + mu * (prev - Pr)
    r, k, v, xw, xa, xg = split_cols(X, RWKV_COLS)
    w = -jax.nn.softplus(-(w0 + jnp.tanh(xw) @ w_up)) - 0.5
    a = jax.nn.sigmoid(a0 + xa @ a_up)
    g = jax.nn.sigmoid(xg) @ g_up
    heads = lambda z: z.astype(jnp.float32).reshape(B, T, H, N)
    kk = heads(k * k_k)
    kk = kk / jnp.maximum(jnp.linalg.norm(kk, axis=-1, keepdims=True), 1e-12)
    k = k * (1.0 + (a - 1.0) * k_a)
    r, k, v, a = heads(r), heads(k), heads(v), heads(a)
    decay = jnp.exp(-jnp.exp(heads(w)))

    def step(S, inp):
        r_t, d_t, k_t, v_t, kk_t, a_t = inp
        sa = jnp.einsum('bhvk,bhk->bhv', S, -kk_t)
        S = (S * d_t[:, :, None, :] + sa[..., None] * (kk_t * a_t)[:, :, None, :]
             + v_t[..., None] * k_t[:, :, None, :])
        return S, jnp.einsum('bhvk,bhk->bhv', S, r_t)

    xs = tuple(z.swapaxes(0, 1) for z in (r, decay, k, v, kk, a))
    S_T, y = lax.scan(step, S0.astype(jnp.float32), xs)
    y = y.swapaxes(0, 1)
    m = jnp.mean(y, axis=-1, keepdims=True)
    var = jnp.mean(jnp.square(y - m), axis=-1, keepdims=True)
    y = ((y - m) * lax.rsqrt(var + RWKV_GN_EPS)).reshape(B, T, H * N) * ln_w + ln_b
    bonus = (jnp.sum(r * k * r_k, axis=-1, keepdims=True) * v).reshape(B, T, H * N)
    return (y + bonus) * g, Pr[:, -1], S_T

def mem_kv(mem, g_norm, w_kv, g_k):
    B, M, _ = mem.shape
    kv = rms_norm(mem, g_norm) @ w_kv
    k = kv[..., :MEMQ].reshape(B, M, MEM_HEADS, HEAD_DIM)
    v = kv[..., MEMQ:].reshape(B, M, MEM_HEADS, HEAD_DIM)
    return rms_norm(k, g_k), v

def mem_attend(mq, km, vm, q_gain):
    B, T, _ = mq.shape
    q = rms_norm(mq.reshape(B, T, MEM_HEADS, HEAD_DIM), q_gain) * (HEAD_DIM ** -0.5)
    p = jax.nn.softmax(jnp.einsum('bthd,bmhd->bhtm', q, km).astype(jnp.float32), axis=-1)
    return jnp.einsum('bhtm,bmhd->bthd', p, vm).reshape(B, T, MEMQ)

def swiglu(x, wg, wu, wd):
    return (jax.nn.silu(x @ wg) * (x @ wu)) @ wd

def moe_dispatch(h, eidx, ew, w_gate, w_up, w_down):
    N, D = h.shape
    A = N * TOPK_FINE
    flat_e = eidx.reshape(A)
    order = jnp.argsort(flat_e)
    e_sorted = flat_e[order]
    tok_sorted = order // TOPK_FINE
    w_sorted = ew.reshape(A)[order]
    counts = jnp.bincount(flat_e, length=N_EXPERTS)
    padded = (counts + MOE_BLOCK - 1) // MOE_BLOCK * MOE_BLOCK
    pad_end = jnp.cumsum(padded)
    pad_start = pad_end - padded
    start = jnp.cumsum(counts) - counts
    dest = pad_start[e_sorted] + jnp.arange(A) - start[e_sorted]
    n_blocks = (A + N_EXPERTS * (MOE_BLOCK - 1)) // MOE_BLOCK
    buf = jnp.zeros((n_blocks * MOE_BLOCK, D), h.dtype).at[dest].set(h[tok_sorted])
    block_e = jnp.minimum(jnp.searchsorted(pad_end, jnp.arange(n_blocks) * MOE_BLOCK, side='right'),
                          N_EXPERTS - 1)

    def run(args):
        xb, e = args
        return swiglu(xb, w_gate[e], w_up[e], w_down[e])

    out = lax.map(run, (buf.reshape(n_blocks, MOE_BLOCK, D), block_e)).reshape(-1, D)
    y = out[dest] * w_sorted[:, None]
    return jax.ops.segment_sum(y, tok_sorted, num_segments=N)

def hier_moe(h, w_coarse, b_coarse, w_fine, b_fine, w_gate, w_up, w_down):
    N = h.shape[0]
    hf = h.astype(jnp.float32)
    lg = hf @ w_coarse + b_coarse
    grp = jnp.argmax(lg, axis=-1)
    p_grp = jnp.take_along_axis(jax.nn.softmax(lg, axis=-1), grp[:, None], axis=-1)
    lf = (hf @ w_fine + b_fine).reshape(N, N_GROUPS, E_PER_GROUP)
    lf = jnp.take_along_axis(lf, grp[:, None, None], axis=1)[:, 0]
    top_v, top_i = lax.top_k(lf, TOPK_FINE)
    ew = jax.nn.softmax(top_v, axis=-1) * p_grp
    eidx = (grp[:, None] * E_PER_GROUP + top_i).astype(jnp.int32)
    return moe_dispatch(h, eidx, ew, w_gate, w_up, w_down)

def setup_inputs(seed: int = 0) -> dict:
    key = jax.random.key(seed)
    keys = iter(jax.random.split(key, 64))

    def nrm(shape, scale=1.0):
        return jax.random.normal(next(keys), shape, jnp.float32) * scale

    def gain(shape):
        return 1.0 + nrm(shape, 0.02)

    D, G, Dh = D_MODEL, NSA_KV_GROUPS, HEAD_DIM
    n_pages = PAST_LEN // PAGE_SIZE
    n_used = DEC_BATCH * n_pages
    n_pool = n_used + (n_used + 3) // 4
    w_buf = min(WINDOW, PAST_LEN)
    page_table = jax.random.permutation(next(keys), n_pool)[:n_used].reshape(DEC_BATCH, n_pages).astype(jnp.int32)
    pool = (N_A, n_pool, PAGE_SIZE, G, Dh)
    return {
        'x_prompt': nrm((BATCH, SEQ, D)),
        'x_sample': nrm((DEC_BATCH, DEC_SEQ, D)),
        'cache_cmp_k': nrm(pool),
        'cache_cmp_v': nrm(pool),
        'cache_sel_k': nrm(pool),
        'cache_sel_v': nrm(pool),
        'cache_win_k': nrm((N_A, DEC_BATCH, w_buf, G, Dh)),
        'cache_win_v': nrm((N_A, DEC_BATCH, w_buf, G, Dh)),
        'cache_mem_k': nrm((DEPTH, DEC_BATCH, MEM_LEN, MEM_HEADS, Dh)),
        'cache_mem_v': nrm((DEPTH, DEC_BATCH, MEM_LEN, MEM_HEADS, Dh)),
        'state_rwkv': nrm((N_B, DEC_BATCH, RWKV_HEADS, Dh, Dh), 0.1),
        'state_shift': nrm((N_B, DEC_BATCH, SHIFT_W)),
        'page_table': page_table,
        'mem_prompt': nrm((BATCH, MEM_LEN, D)),
        'norm_mix': gain((DEPTH, D)),
        'norm_ffn': gain((DEPTH, D)),
        'norm_mem': gain((DEPTH, D)),
        'w_mem_kv': nrm((DEPTH, D, 2 * MEMQ), D ** -0.5),
        'mem_q_gain': gain((DEPTH, Dh)),
        'mem_k_gain': gain((DEPTH, Dh)),
        'w_in_a': nrm((N_A, D, C_A), D ** -0.5),
        'nsa_q_gain': gain((N_A, Dh)),
        'nsa_k_gain': gain((N_A, 3, Dh)),
        'cmp_pe': nrm((N_A, 2, CMP_LEN, Dh), 0.1),
        'cmp_w1': nrm((N_A, 2, CMP_LEN * Dh, CMP_HID), (CMP_LEN * Dh) ** -0.5),
        'cmp_b1': nrm((N_A, 2, CMP_HID), 0.01),
        'cmp_w2': nrm((N_A, 2, CMP_HID, Dh), CMP_HID ** -0.5),
        'w_in_b': nrm((N_B, D, C_B), D ** -0.5),
        'rwkv_mu': jax.random.uniform(next(keys), (N_B, SHIFT_W), jnp.float32),
        'rwkv_w0': -2.0 + nrm((N_B, RWKV_WIDTH), 0.5),
        'rwkv_w_up': nrm((N_B, DECAY_RANK, RWKV_WIDTH), 0.5 * DECAY_RANK ** -0.5),
        'rwkv_a0': nrm((N_B, RWKV_WIDTH), 0.1),
        'rwkv_a_up': nrm((N_B, ICLR_RANK, RWKV_WIDTH), 0.5 * ICLR_RANK ** -0.5),
        'rwkv_g_up': nrm((N_B, GATE_RANK, RWKV_WIDTH), GATE_RANK ** -0.5),
        'rwkv_k_k': 0.85 + nrm((N_B, RWKV_WIDTH), 0.05),
        'rwkv_k_a': 1.0 + nrm((N_B, RWKV_WIDTH), 0.05),
        'rwkv_r_k': nrm((N_B, RWKV_HEADS, Dh), 0.1),
        'rwkv_ln_w': gain((N_B, RWKV_WIDTH)),
        'rwkv_ln_b': nrm((N_B, RWKV_WIDTH), 0.01),
        'w_out': nrm((DEPTH, MIX_WIDTH, D), MIX_WIDTH ** -0.5),
        'moe_w_coarse': nrm((DEPTH, D, N_GROUPS), D ** -0.5),
        'moe_b_coarse': nrm((DEPTH, N_GROUPS), 0.01),
        'moe_w_fine': nrm((DEPTH, D, N_EXPERTS), D ** -0.5),
        'moe_b_fine': nrm((DEPTH, N_EXPERTS), 0.01),
        'moe_w_gate': nrm((DEPTH, N_EXPERTS, D, D_EXPERT), D ** -0.5),
        'moe_w_up': nrm((DEPTH, N_EXPERTS, D, D_EXPERT), D ** -0.5),
        'moe_w_down': nrm((DEPTH, N_EXPERTS, D_EXPERT, D), D_EXPERT ** -0.5),
    }

def reference(x_prompt, x_sample, cache_cmp_k, cache_cmp_v, cache_sel_k, cache_sel_v,
              cache_win_k, cache_win_v, cache_mem_k, cache_mem_v, state_rwkv, state_shift,
              page_table, mem_prompt,
              norm_mix, norm_ffn, norm_mem, w_mem_kv, mem_q_gain, mem_k_gain,
              w_in_a, nsa_q_gain, nsa_k_gain, cmp_pe, cmp_w1, cmp_b1, cmp_w2,
              w_in_b, rwkv_mu, rwkv_w0, rwkv_w_up, rwkv_a0, rwkv_a_up, rwkv_g_up,
              rwkv_k_k, rwkv_k_a, rwkv_r_k, rwkv_ln_w, rwkv_ln_b,
              w_out, moe_w_coarse, moe_b_coarse, moe_w_fine, moe_b_fine,
              moe_w_gate, moe_w_up, moe_w_down):
    xp, xs = x_prompt, x_sample
    B, S, _ = xp.shape
    Bd, T, _ = xs.shape
    pc_k, pc_v, ps_k, ps_v, pw_k, pw_v, pm_k, pm_v, pr_s, pr_x = ([] for _ in range(10))
    sc_k, sc_v, ss_k, ss_v, sw_k, sw_v, sr_s, sr_x = ([] for _ in range(8))
    for i in range(DEPTH):
        hp = rms_norm(xp, norm_mix[i])
        hs = rms_norm(xs, norm_mix[i])
        km_p, vm_p = mem_kv(mem_prompt, norm_mem[i], w_mem_kv[i], mem_k_gain[i])
        pm_k.append(km_p)
        pm_v.append(vm_p)
        if i % 2 == 0:
            ia = i // 2
            cmp_prm = (cmp_pe[ia], cmp_w1[ia], cmp_b1[ia], cmp_w2[ia], nsa_k_gain[ia, 0])
            q, kc, vc, ks, vs, kw, vw, gt, mq_p = nsa_project(hp, w_in_a[ia], nsa_q_gain[ia], nsa_k_gain[ia])
            mix_p = nsa_prompt(q, kc, vc, ks, vs, kw, vw, gt, cmp_prm)
            wl = min(WINDOW, S)
            pc_k.append(kc)
            pc_v.append(vc)
            ps_k.append(ks)
            ps_v.append(vs)
            pw_k.append(kw[:, S - wl:])
            pw_v.append(vw[:, S - wl:])
            q, kc, vc, ks, vs, kw, vw, gt, mq_s = nsa_project(hs, w_in_a[ia], nsa_q_gain[ia], nsa_k_gain[ia])
            mix_s, nwk, nwv = nsa_sample(q, kc, vc, ks, vs, kw, vw, gt,
                                         cache_cmp_k[ia], cache_cmp_v[ia], cache_sel_k[ia], cache_sel_v[ia],
                                         cache_win_k[ia], cache_win_v[ia], page_table, cmp_prm)
            sc_k.append(kc)
            sc_v.append(vc)
            ss_k.append(ks)
            ss_v.append(vs)
            sw_k.append(nwk)
            sw_v.append(nwv)
        else:
            ib = i // 2
            rw = (rwkv_mu[ib], rwkv_w0[ib], rwkv_w_up[ib], rwkv_a0[ib], rwkv_a_up[ib], rwkv_g_up[ib],
                  rwkv_k_k[ib], rwkv_k_a[ib], rwkv_r_k[ib], rwkv_ln_w[ib], rwkv_ln_b[ib])
            Pr, mq_p = split_cols(hp @ w_in_b[ib], B_COLS)
            mix_p, sh_p, st_p = rwkv_mix(Pr, jnp.zeros((B, SHIFT_W), Pr.dtype),
                                         jnp.zeros((B, RWKV_HEADS, HEAD_DIM, HEAD_DIM), jnp.float32), *rw)
            pr_s.append(st_p)
            pr_x.append(sh_p)
            Pr, mq_s = split_cols(hs @ w_in_b[ib], B_COLS)
            mix_s, sh_s, st_s = rwkv_mix(Pr, state_shift[ib], state_rwkv[ib], *rw)
            sr_s.append(st_s)
            sr_x.append(sh_s)
        mem_p = mem_attend(mq_p, km_p, vm_p, mem_q_gain[i])
        mem_s = mem_attend(mq_s, cache_mem_k[i], cache_mem_v[i], mem_q_gain[i])
        xp = xp + jnp.concatenate([mix_p, mem_p], axis=-1) @ w_out[i]
        xs = xs + jnp.concatenate([mix_s, mem_s], axis=-1) @ w_out[i]
        moe_prm = (moe_w_coarse[i], moe_b_coarse[i], moe_w_fine[i], moe_b_fine[i],
                   moe_w_gate[i], moe_w_up[i], moe_w_down[i])
        xp = xp + hier_moe(rms_norm(xp, norm_ffn[i]).reshape(B * S, -1), *moe_prm).reshape(B, S, -1)
        xs = xs + hier_moe(rms_norm(xs, norm_ffn[i]).reshape(Bd * T, -1), *moe_prm).reshape(Bd, T, -1)
    return (xp, xs,
            jnp.stack(pc_k), jnp.stack(pc_v), jnp.stack(ps_k), jnp.stack(ps_v),
            jnp.stack(pw_k), jnp.stack(pw_v), jnp.stack(pm_k), jnp.stack(pm_v),
            jnp.stack(pr_s), jnp.stack(pr_x),
            jnp.stack(sc_k), jnp.stack(sc_v), jnp.stack(ss_k), jnp.stack(ss_v),
            jnp.stack(sw_k), jnp.stack(sw_v), jnp.stack(sr_s), jnp.stack(sr_x))


_drawn_inputs = setup_inputs


def setup_inputs(seed=0):
    import zlib

    import numpy as np

    out = dict(_drawn_inputs(seed))
    spreads = {}
    factors = {'norm_mem': 2.833,
     'mem_q_gain': 4.843,
     'rwkv_ln_b': 15.685,
     'nsa_q_gain': 4.285,
     'nsa_k_gain': 2.945,
     'rwkv_k_k': 7.714,
     'moe_b_fine': 2.715,
     'cmp_b1': 5.796,
     'rwkv_ln_w': 6.304,
     'moe_b_coarse': 3.09}
    for name, (base, spread) in spreads.items():
        noise = np.random.default_rng([zlib.crc32(name.encode()), seed]).standard_normal(out[name].shape)
        drawn = base * np.exp(spread * noise) if base else spread * noise
        out[name] = __import__('jax').numpy.asarray(drawn.astype(out[name].dtype))
    for name, factor in factors.items():
        out[name] = (out[name] * factor).astype(out[name].dtype)
    return out
```

```python
from contextlib import ExitStack

import numpy as np
import concourse.bass as bass
from concourse import mybir

F32 = mybir.dt.float32
I32 = mybir.dt.int32
ALU = mybir.AluOpType
ACT = mybir.ActivationFunctionType
AX_X = mybir.AxisListType.X

P = 128
D = 1024
KD = D // P
SEQ, NB = 256, 8
NT = SEQ + NB
TILES = ((0, 128), (128, 128), (256, 8))
DH = 64
H, G, HG = 12, 3, 4
MH = 4
QA, KVW, MEMQ = H * DH, G * DH, MH * DH
GATES = 3 * H
C_A = QA + 6 * KVW + GATES + MEMQ
KV0 = QA
KVN = 6 * KVW + GATES
SHIFT_W = 3 * QA + 256
NCH = SHIFT_W // P
C_B = SHIFT_W + MEMQ
PAST, PAGE = 1024, 128
NPG = PAST // PAGE
SEL = 64
NSEL = PAST // SEL + 1
WIN = 512
NCS, NCP = 63, 15
RS = NB * H
CH = 64
NE, GE, NGRP = 32, 4, 8
FE = 512
SLOT = 32
OVER = (NT + SLOT - 1) // SLOT - 1
UNITS = 12
RING = 6
NEG = -1e30

SLOPES = np.exp2(-8.0 * np.arange(1, H + 1, dtype=np.float32) / H).astype(np.float32)


def constants():
    p = np.arange(P)
    t = np.arange(SEQ)
    f4 = lambda a: np.ascontiguousarray(a, dtype=np.float32)

    def rows(a):
        out = np.zeros((P, a.shape[1]), np.float32)
        out[: a.shape[0]] = a
        return out

    parts = {}
    parts["ident"] = np.eye(P)
    parts["headones"] = (p[:, None] // DH == p[None] // DH)
    parts["ones"] = np.ones((P, P))
    parts["before"] = p[:, None] < p[None]
    dist = np.stack([t[None] - (128 * i + p[:, None]) for i in range(2)], 1).astype(np.float64)
    parts["distp"] = np.where(dist <= 0, dist, NEG).reshape(P, -1)
    cend = np.arange(NCP) * 16 + 31
    dc = np.stack([cend[None] - (128 * i + p[:, None]) for i in range(2)], 1)
    cb = np.where(dc[:, :, None, :] <= 0, dc[:, :, None, :] * SLOPES[None, None, :, None], NEG)
    parts["cmpbias"] = cb.reshape(P, -1)
    parts["cmpmask"] = (dc <= 0).reshape(P, -1)
    parts["slope"] = rows(np.tile(SLOPES, NB)[:, None])
    parts["pos"] = np.tile(np.arange(PAST + 1) - float(PAST), (P, 1))
    parts["cpos"] = np.tile(np.arange(NCS) * 16 + 31 - float(PAST), (P, 1))
    c0, s0 = np.arange(NCS) * 16, np.arange(NSEL) * SEL
    parts["cmpsel"] = rows(((c0[:, None] < s0[None] + SEL) & (c0[:, None] + 32 > s0[None])))
    r = np.arange(RS)
    grp = (r // H) * G + (r % H) // HG
    parts["samegroup"] = rows(grp[:, None] == grp[None])
    parts["rowseq"] = rows(r[:, None] // H == np.arange(NB)[None])
    parts["blkno"] = np.tile(np.arange(1, NSEL - 2), (P, 1))
    i, q = (p % CH)[:, None], np.arange(CH)[None]
    same = lambda n: i // n == q // n
    parts["m_iu"] = (i < q)
    parts["m_ieu"] = (i <= q)
    parts["m16u"] = (i < q) & same(16)
    parts["m16l"] = (i > q) & same(16)
    parts["off32"] = (i > q) & same(32) & ~same(16)
    parts["off64"] = (i > q) & ~same(32)
    parts["ident64"] = (i == q)
    parts["slotno"] = np.tile(np.arange(SLOT * (OVER + 1)), (P, 1))
    parts["fold"] = (p % SLOT)[:, None] == np.arange(SLOT)[None]
    parts["order"] = np.tile(NE - np.arange(NE), (P, 1))
    parts["gorder"] = np.tile(4 - np.arange(4), (P, 1))
    parts["real"] = np.stack([np.ones(P), np.ones(P), p < NB], 1)
    at, cols, off = {}, [], 0
    for k, v in parts.items():
        v = f4(v)
        at[k] = (off, v.shape[1])
        cols.append(v)
        off += v.shape[1]
    return at, f4(np.concatenate(cols, 1))


class Count:

    def __init__(self):
        self.n, self.i, self.per = 0, None, 0

    def value(self, more=0):
        v = self.n + more
        return v if self.i is None else self.i * self.per + v

    def add(self, k):
        self.n += k
        return self.value()

    def loop(self, i, per):
        self.i, self.per, self.start = i, per, self.n

    def end(self, turns):
        assert self.n - self.start == self.per, (self.n - self.start, self.per)
        self.i, self.n = None, self.start + self.per * turns


class Banks:

    def __init__(self, banks):
        self.banks = banks
        self.claimed, self.taken = Count(), Count()

    def room(self):
        return self.claimed.value(1)

    def claim(self):
        self.claimed.add(1)
        return self.banks[(self.claimed.n - 1) % 4]

    def all_free(self):
        return self.claimed.value(4)

    def filled(self):
        return self.taken.value(1)

    def take(self):
        self.taken.add(1)
        return self.banks[(self.taken.n - 1) % 4]

    def emptied(self):
        return self.taken.value(4)


def build(nc, A, O, at):
    ctx = ExitStack()
    ctx.enter_context(nc.allow_non_contiguous_dma(reason="parameter columns and cut cache rows"))
    base0 = 16512
    names = iter(range(10 ** 6))

    cur = [base0]

    def keep(name, shape, dt=F32):
        t = nc.alloc_sbuf_tensor_at(name, [P] + list(shape), dt, offset=cur[0])
        cur[0] += (int(np.prod(shape)) * 4 + 31) // 32 * 32
        return t

    nconst = sum(w for _, w in at.values())
    CONST = keep("CONST", [nconst])
    C = lambda k, p=P: CONST[0:p, at[k][0]:at[k][0] + at[k][1]]
    X = keep("X", [3, D])
    XN = keep("XN", [3, D])
    HT = keep("HT", [KD, NT])
    MIXT = keep("MIXT", [KD, NT])
    PAR = keep("PAR", [120])
    ROWG = keep("ROWG", [4, DH])
    ST = keep("ST", [64])
    WR = keep("WR", [KD, 36])
    BR = keep("BR", [36])
    RT = keep("RT", [3, NE])
    RW = keep("RW", [3, NE])
    CNT = keep("CNT", [4], I32)
    PGT = keep("PGT", [NB * NPG], I32)
    U1 = cur[0]
    U2 = U1 + 32768
    ARENA = U2 + 21120

    def place(name, off, shape, dt=F32, base=ARENA):
        n = int(np.prod(shape)) * 4
        assert base + off + n <= nc.sbuf_usable_end, (name, base + off + n - nc.sbuf_usable_end)
        return nc.alloc_sbuf_tensor_at(f"{name}_{next(names)}", [P] + list(shape), dt, offset=base + off)

    XNoff = (nconst * 4 + 31) // 32 * 32 + 12288 + base0
    WM = place("WM", 0, [KD, 512], base=U1)
    MEM = place("MEM", 16384, [2, D], base=U1)
    MT = place("MT", 24576, [KD, SEQ], base=U1)
    WO = place("WO", 0, [KD, D], base=U1)
    KV = place("KV", 0, [3, KVN], base=U2)
    PRT = place("PRT", 0, [NCH, NT], base=U2)
    QT = place("QT", 0, [8, NT], base=XNoff)
    KMT = place("KMT", 8448, [2, SEQ], base=XNoff)
    WIN_A = place("WIN_A", 0, [KD, C_A])
    SQ_A = place("SQ_A", KD * C_A * 4, [8, NT])
    RS_A = place("RS_A", KD * C_A * 4 + 8448, [8, NT])
    KVMS = [place("KVM", 14272, [2, 512], base=U2), place("KVM", 2112, [2, 512], base=XNoff)]
    WIN_B = place("WIN_B", 0, [KD, C_B])

    KT = place("KT", 0, [2, G, SEQ])
    KNEW = place("KNEW", 6144, [2, 2, NB])
    PP = place("PP", 88064, [3, 512])
    PPT = place("PPT", 10496, [2, 512])
    SPT = place("SPT", 6400, [14, RS])
    CS = place("CS", 14592, [2, H * NCP])
    CPT = place("CPT", 16064, [2 * H, P])
    CKT = place("CKT", 28352, [2, 9, 64])
    CV = place("CV", 32960, [9, KVW])
    W1 = place("W1", 39872, [2, 16, P])
    HID = place("HID", 56256, [2, 256])
    XR = [place("XR", o, [4, 384]) for o in (58304, 64448, 16064, 22208)]
    XT = place("XT", 70592, [G, 4, 512])
    PE_T = place("PE_T", 95168, [2, 16])
    W2 = place("W2", 95296, [2, DH])
    CB = place("CB", 95808, [2])
    CBR = place("CBR", 95840, [2, P])
    OLD = [place("OLD", o, [NPG + 4, KVW], base=b) for o, b in (
        (39872, ARENA), (0, U1), (9216, U1), (49088, ARENA), (18432, U1))]
    KTS = place("KTS", 58304, [2, PAST + WIN])
    QBD = place("QBD", 70592, [2, NB, RS])
    VO = place("VO", 70592, [NB, KVW])
    SS = place("SS", 76736, [1604])
    PD = place("PD", 83200, [2, RS])
    SMALL = place("SMALL", 83968, [128])
    RINGW = place("RINGW", 0, [RING, 4096])
    HG_T = place("HG_T", 0, [KD, P], base=U2)
    SELT = place("SELT", 4096, [3, P], base=U2)
    SELW = place("SELW", 5632, [3, P], base=U2)
    SWT = place("SWT", 7168, [NT], base=U2)
    SG = place("SG", 8256, [FE], base=U2)
    AV = place("AV", 10304, [FE], base=U2)
    AVT = place("AVT", 12352, [4, P], base=U2)
    OUT4 = place("OUT4", 14400, [D], base=U2)
    RTMP = place("RTMP", 0, [16, 3, 36], base=U2)

    banks = [nc.alloc_psum_tensor(f"bank{i}", [P, 512], F32) for i in range(8)]
    v, a = Banks(banks[0:4]), Banks(banks[4:8])
    v_full, v_free, a_full, a_free, dve_done, act_done, stored = (
        nc.alloc_semaphore(n) for n in ("v_full", "v_free", "a_full", "a_free", "dve_done", "act_done", "stored"))
    w_used = nc.alloc_semaphore("w_used")
    w_in_ring = [nc.alloc_semaphore(f"w_in_ring{s}") for s in range(RING)]
    sems, counted = {}, {}

    def sem(name):
        if name not in sems:
            sems[name] = nc.alloc_semaphore(name)
        return sems[name]

    def count(who, name):
        return counted.setdefault((who, name), Count())

    def nth(who, name, k=1):
        return count(who, name).add(k)

    NM = {"SP": nc.sync, "PE": nc.tensor, "DVE": nc.vector, "ACT": nc.scalar, "POOL": nc.gpsimd}

    ident = C("ident")
    V, AC, PE = nc.vector, nc.scalar, nc.tensor
    tt, ts, stt = V.tensor_tensor, V.tensor_scalar, V.scalar_tensor_tensor

    def mm(out, l, r, start=True, stop=True):
        return PE.matmul(out, lhsT=l, rhs=r, start=start, stop=stop, skip_group_check=True)

    def tr(out, in_):
        p = in_.shape[0]
        return PE.transpose(out, in_, ident[0:p, 0:p])

    def col(off, src, chunks):
        nc.sync.dma_start(PAR[:, off:off + chunks], src.rearrange("(c p) -> p c", p=P)).then_inc(sem("params"), 16)

    MIXG, FFNG, MEMG, QG, MQG, KG0, MU, W0, A0, KK, KA, RK, LNW, LNB = (
        0, 16, 32, 48, 50, 52, 54, 74, 80, 86, 92, 98, 104, 110)
    CB1 = 116

    def sp_params():
        nc.sync.dma_start(CONST[:, :], A["consts"]).then_inc(sem("consts"), 16)
        nc.sync.dma_start(X[:, 0:2, :], A["x_prompt"].rearrange("o (i p) d -> p (o i) d", p=P)).then_inc(sem("x"), 16)
        nc.sync.dma_start(X[0:NB, 2, :], A["x_sample"].rearrange("b o d -> (b o) d")).then_inc(sem("x"), 16)
        nc.sync.dma_start(PGT[0:1, :],
                          A["page_table"].rearrange("(o a) b -> o (a b)", o=1)).then_inc(sem("pages"), 16)
        for l in range(2):
            col(MIXG + 8 * l, A["norm_mix"][l], 8)
            col(FFNG + 8 * l, A["norm_ffn"][l], 8)
            col(MEMG + 8 * l, A["norm_mem"][l], 8)
            for hf in range(2):
                nc.sync.dma_start(PAR[64 * hf:64 * hf + 64, MQG + l:MQG + l + 1],
                                  A["mem_q_gain"][l].rearrange("(d o) -> d o", o=1)).then_inc(sem("params"), 16)
            nc.sync.dma_start(ROWG[:, l, :],
                              A["mem_k_gain"][l:l + 1, :].broadcast_to([P, DH])).then_inc(sem("params"), 16)
            nc.sync.dma_start(ROWG[:, 2 + l, :],
                              A["nsa_k_gain"][0, 1 + l:2 + l, :].broadcast_to([P, DH])).then_inc(sem("params"), 16)
        for hf in range(2):
            nc.sync.dma_start(PAR[64 * hf:64 * hf + 64, QG:QG + 1],
                              A["nsa_q_gain"][0].rearrange("(d o) -> d o", o=1)).then_inc(sem("params"), 16)
            nc.sync.dma_start(PAR[64 * hf:64 * hf + 64, KG0:KG0 + 1],
                              A["nsa_k_gain"][0, 0].rearrange("(d o) -> d o", o=1)).then_inc(sem("params"), 16)
        nc.sync.dma_start(PAR[:, CB1:CB1 + 2], A["cmp_b1"][0].rearrange("c p -> p c")).then_inc(sem("params"), 16)
        col(MU, A["rwkv_mu"][0], NCH)
        for off, n in ((W0, "rwkv_w0"), (A0, "rwkv_a0"), (KK, "rwkv_k_k"), (KA, "rwkv_k_a"),
                       (LNW, "rwkv_ln_w"), (LNB, "rwkv_ln_b")):
            col(off, A[n][0], 6)
        nc.sync.dma_start(PAR[:, RK:RK + 6],
                          A["rwkv_r_k"][0].rearrange("(c two) n -> (two n) c", two=2)).then_inc(sem("params"), 16)

    NPARAM = 2 * 7 + 4 + 1 + 1 + 6 + 1
    STORES = 4 + 4 + 4 + 4 + 2

    def rsqrt_dve(ap, scale, eps, op=ALU.add):
        ts(ap, ap, scale, eps, ALU.mult, op).then_inc(sem("var"), 1)
        V.wait_ge(sem("var"), nth("DVE", "var"))
        V.wait_ge(sem("std"), nth("DVE", "std"))
        V.reciprocal(ap, ap).then_inc(dve_done, 1)
        V.wait_ge(dve_done, nth("DVE", "dve_done"))

    def rsqrt_act(ap):
        AC.wait_ge(sem("var"), nth("ACT", "var"))
        AC.activation(ap, ap, ACT.Sqrt).then_inc(sem("std"), 1)
        AC.wait_ge(sem("std"), nth("ACT", "std"))

    def dve_norm(gain):
        for i in range(3):
            V.tensor_tensor_reduce(out=XN[:, i, :], in0=X[:, i, :], in1=X[:, i, :], scale=1.0, scalar=0.0,
                                      op0=ALU.mult, op1=ALU.add, accum_out=ST[:, i:i + 1]).then_inc(dve_done, 1)
            V.wait_ge(dve_done, nth("DVE", "dve_done"))
        rsqrt_dve(ST[:, 0:3], 1.0 / D, 1e-6)
        for i in range(3):
            ts(XN[:, i, :], X[:, i, :], ST[:, i:i + 1], None, ALU.mult).then_inc(dve_done, 1)
            V.wait_ge(dve_done, nth("DVE", "dve_done"))
        V.memset(ST[:, 8:9], 0.0).then_inc(sem("xn"), 1)
        V.wait_ge(sem("xn"), nth("DVE", "xn"))
        for c in range(KD):
            V.wait_ge(v_full, v.filled())
            b = v.take()
            ts(HT[:, c, :], b[:, 0:NT], PAR[:, gain + c:gain + c + 1], None, ALU.mult).then_inc(v_free, 1)
            V.wait_ge(v_free, v.emptied())

    def act_norm():
        rsqrt_act(ST[:, 0:3])

    def pe_norm():
        PE.wait_ge(sem("xn"), nth("PE", "xn"))
        for c in range(KD):
            PE.wait_ge(v_free, v.room())
            b = v.claim()
            for i, (t0, n) in enumerate(TILES):
                m = tr(b[:, t0:t0 + n], XN[0:n, i, c * P:(c + 1) * P])
            m.then_inc(v_full, 1)
        PE.wait_ge(v_free, v.all_free())

    def load_mem(eng, l):
        eng.dma_start(WM[:, :, :], A["w_mem_kv"][l].rearrange("(k p) n -> p k n", p=P)).then_inc(sem(f"w_mem{l}"), 16)
        eng.dma_start(MEM[:, :, :], A["mem_prompt"][0].rearrange("(i p) d -> p i d", p=P)).then_inc(sem(f"mem{l}"), 16)

    def dve_mem(l):
        KVM = KVMS[l]
        V.wait_ge(sem(f"mem{l}"), nth("DVE", f"mem{l}", 16))
        for i in range(2):
            V.tensor_tensor_reduce(out=MT[:, 4 * i:4 * i + 4, :].rearrange("p a b -> p (a b)"), in0=MEM[:, i, :],
                                      in1=MEM[:, i, :], scale=1.0, scalar=0.0, op0=ALU.mult, op1=ALU.add,
                                      accum_out=ST[:, i:i + 1]).then_inc(dve_done, 1)
            V.wait_ge(dve_done, nth("DVE", "dve_done"))
        rsqrt_dve(ST[:, 0:2], 1.0 / D, 1e-6)
        for i in range(2):
            ins = ts(MEM[:, i, :], MEM[:, i, :], ST[:, i:i + 1], None, ALU.mult)
            if i == 0:
                ins.then_inc(dve_done, 1)
                V.wait_ge(dve_done, nth("DVE", "dve_done"))
            else:
                ins.then_inc(sem("memn"), 1)
                V.wait_ge(sem("memn"), nth("DVE", "memn"))
        for c in range(KD):
            V.wait_ge(v_full, v.filled())
            b = v.take()
            ts(MT[:, c, :], b[:, 0:SEQ], PAR[:, MEMG + 8 * l + c:MEMG + 8 * l + c + 1], None, ALU.mult).then_inc(v_free, 1)
            V.wait_ge(v_free, v.emptied())
        for i in range(2):
            V.wait_ge(v_full, v.filled())
            b = v.take()
            V.tensor_copy(KVM[:, i, :], b[:, :]).then_inc(v_free, 1)
            V.wait_ge(v_free, v.emptied())
        kk = KVM[:, :, 0:MEMQ]
        sq = MT[:, 0:2, :]
        tt(sq, kk, kk, ALU.mult).then_inc(dve_done, 1)
        V.wait_ge(dve_done, nth("DVE", "dve_done"))
        st = ST[:, 16:24].rearrange("p (a h) -> p a h", a=2)
        V.tensor_reduce(st, sq.rearrange("p a (h d) -> p a h d", h=MH), AX_X, ALU.add).then_inc(dve_done, 1)
        V.wait_ge(dve_done, nth("DVE", "dve_done"))
        rsqrt_dve(ST[:, 16:24], 1.0 / DH, 1e-6)
        for i in range(2):
            k4 = KVM[:, i, 0:MEMQ].rearrange("p (h d) -> p h d", h=MH)
            tt(k4, k4, st[:, i, :].unsqueeze(2).broadcast_to([P, MH, DH]), ALU.mult).then_inc(dve_done, 1)
            V.wait_ge(dve_done, nth("DVE", "dve_done"))
            ins = tt(k4, k4, ROWG[:, l:l + 1, :].broadcast_to([P, MH, DH]), ALU.mult)
            if i == 0:
                ins.then_inc(dve_done, 1)
                V.wait_ge(dve_done, nth("DVE", "dve_done"))
            else:
                ins.then_inc(sem("km"), 1)
                V.wait_ge(sem("km"), nth("DVE", "km"))
        for c in range(2):
            V.wait_ge(v_full, v.filled())
            b = v.take()
            V.tensor_copy(KMT[:, c, :], b[:, 0:SEQ]).then_inc(v_free, 1)
            V.wait_ge(v_free, v.emptied())
        V.memset(ST[:, 8:9], 0.0).then_inc(sem("u1_used"), 1)
        V.wait_ge(sem("u1_used"), nth("DVE", "u1_used"))

    def act_mem(l):
        rsqrt_act(ST[:, 0:2])
        rsqrt_act(ST[:, 16:24])

    def pe_mem(l):
        KVM = KVMS[l]
        PE.wait_ge(sem("memn"), nth("PE", "memn"))
        for c in range(KD):
            PE.wait_ge(v_free, v.room())
            b = v.claim()
            for i in range(2):
                m = tr(b[:, i * P:(i + 1) * P], MEM[:, i, c * P:(c + 1) * P])
            m.then_inc(v_full, 1)
        PE.wait_ge(v_free, v.all_free())
        PE.wait_ge(sem(f"w_mem{l}"), nth("PE", f"w_mem{l}", 16))
        for i in range(2):
            PE.wait_ge(v_free, v.room())
            b = v.claim()
            for k in range(KD):
                m = mm(b[:, :], MT[:, k, i * P:(i + 1) * P], WM[:, k, :], k == 0, k == KD - 1)
            m.then_inc(v_full, 1)
        PE.wait_ge(sem("km"), nth("PE", "km"))
        for c in range(2):
            PE.wait_ge(v_free, v.room())
            b = v.claim()
            for i in range(2):
                m = tr(b[:, i * P:(i + 1) * P], KVM[:, i, c * P:(c + 1) * P])
            m.then_inc(v_full, 1)
        PE.wait_ge(v_free, v.all_free())

    def pool_mem(l):
        KVM = KVMS[l]
        nc.gpsimd.wait_ge(sem("km"), nth("POOL", "km"))
        for o, c0 in (("p_mem_k", 0), ("p_mem_v", MEMQ)):
            nc.gpsimd.dma_start(O[o][l, 0].rearrange("(i p) h d -> p i (h d)", p=P),
                                KVM[:, :, c0:c0 + MEMQ]).then_inc(stored, 16)

    CK2 = place("CK2", 96896, [G, NCP])

    def sp_win(l, name, tile, cols):
        if l:
            nc.sync.wait_ge(sem("moe_done"), nth("SP", "moe_done"))
        w = A[name][0].rearrange("(k p) n -> p k n", p=P)
        for k in range(KD):
            nc.sync.dma_start(tile[:, k, :], w[:, k, :]).then_inc(sem("w_in"), 16)

    def pe_channels(tile, cols, out_chunks):
        for c0 in cols:
            PE.wait_ge(v_free, v.room())
            b = v.claim()
            for k in range(KD):
                m = mm(b[:, 0:NT], tile[:, k, c0:c0 + P], HT[:, k, :], k == 0, k == KD - 1)
            m.then_inc(v_full, 1)

    def pe_headnorm(sq, n):
        PE.wait_ge(sem("sq"), nth("PE", "sq"))
        for c in range(n):
            PE.wait_ge(v_free, v.room())
            b = v.claim()
            mm(b[:, 0:sq.shape[2]], C("headones"), sq[:, c, :]).then_inc(v_full, 1)

    def act_headnorm(rs):
        rsqrt_act(rs[:, :, :])

    def dve_headnorm(x, sq, rs, n, gains):
        w = x.shape[2]
        tt(sq[:, :, :], x[:, :, :], x[:, :, :], ALU.mult).then_inc(sem("sq"), 1)
        V.wait_ge(sem("sq"), nth("DVE", "sq"))
        for c in range(n):
            V.wait_ge(v_full, v.filled())
            b = v.take()
            V.tensor_copy(rs[:, c, :], b[:, 0:w]).then_inc(v_free, 1)
            V.wait_ge(v_free, v.emptied())
        rsqrt_dve(rs[:, :, :], 1.0 / DH, 1e-6)
        for c in range(n):
            g = gains[c]
            stt(x[:, c, :], x[:, c, :], PAR[:, g:g + 1], rs[:, c, :], ALU.mult, ALU.mult).then_inc(dve_done, 1)
            V.wait_ge(dve_done, nth("DVE", "dve_done"))

    KVCUTS = ((0, 512), (512, 512), (1024, KVN - 1024))

    def pe_proj_a():
        PE.wait_ge(sem("w_in"), nth("PE", "w_in", 16 * KD))
        pe_channels(WIN_A, [P * c for c in range(6)] + [KV0 + KVN, KV0 + KVN + P], None)
        for i, (t0, n) in enumerate(TILES):
            for c0, w in KVCUTS:
                PE.wait_ge(v_free, v.room())
                b = v.claim()
                for k in range(KD):
                    m = mm(b[0:n, 0:w], HT[:, k, t0:t0 + n], WIN_A[:, k, KV0 + c0:KV0 + c0 + w], k == 0, k == KD - 1)
                m.then_inc(v_full, 1)
        pe_headnorm(SQ_A, 8)

    def dve_proj_a():
        for c in range(8):
            V.wait_ge(v_full, v.filled())
            b = v.take()
            V.tensor_copy(QT[:, c, :], b[:, 0:NT]).then_inc(v_free, 1)
            V.wait_ge(v_free, v.emptied())
        for i, (t0, n) in enumerate(TILES):
            for c0, w in KVCUTS:
                V.wait_ge(v_full, v.filled())
                b = v.take()
                V.tensor_copy(KV[0:n, i, c0:c0 + w], b[0:n, 0:w]).then_inc(v_free, 1)
                V.wait_ge(v_free, v.emptied())
        V.memset(ST[:, 8:9], 0.0).then_inc(sem("gates_in"), 1)
        V.wait_ge(sem("gates_in"), nth("DVE", "gates_in"))
        ts(PAR[:, QG:QG + 1], PAR[:, QG:QG + 1], DH ** -0.5, None, ALU.mult).then_inc(dve_done, 1)
        V.wait_ge(dve_done, nth("DVE", "dve_done"))
        dve_headnorm(QT, SQ_A, RS_A, 8, [QG] * 6 + [MQG] * 2)
        for i, (t0, n) in enumerate(TILES):
            kk = KV[0:n, i, 2 * KVW:6 * KVW].rearrange("p (a b) -> p a b", a=2)[:, :, 0:KVW]
            sq = SQ_A[0:n, 0:2, 0:KVW]
            st = ST[0:n, 16:22].rearrange("p (a g) -> p a g", a=2)
            tt(sq, kk, kk, ALU.mult).then_inc(dve_done, 1)
            V.wait_ge(dve_done, nth("DVE", "dve_done"))
            V.tensor_reduce(st, sq.rearrange("p a (g d) -> p a g d", g=G), AX_X, ALU.add).then_inc(dve_done, 1)
            V.wait_ge(dve_done, nth("DVE", "dve_done"))
            rsqrt_dve(ST[0:n, 16:22], 1.0 / DH, 1e-6)
            for z in range(2):
                c0 = (2 + 2 * z) * KVW
                k3 = KV[0:n, i, c0:c0 + KVW].rearrange("p (g d) -> p g d", g=G)
                tt(k3, k3, st[:, z, :].unsqueeze(2).broadcast_to([n, G, DH]), ALU.mult).then_inc(dve_done, 1)
                V.wait_ge(dve_done, nth("DVE", "dve_done"))
                tt(k3, k3, ROWG[0:n, 2 + z:3 + z, :].broadcast_to([n, G, DH]), ALU.mult).then_inc(dve_done, 1)
                V.wait_ge(dve_done, nth("DVE", "dve_done"))
        V.memset(ST[:, 8:9], 0.0).then_inc(sem("kv"), 1)
        V.wait_ge(sem("kv"), nth("DVE", "kv"))

    def act_proj_a():
        AC.wait_ge(sem("gates_in"), nth("ACT", "gates_in"))
        for i, (t0, n) in enumerate(TILES):
            g = KV[0:n, i, 6 * KVW:KVN]
            ins = AC.activation(g, g, ACT.Sigmoid)
            if i < 2:
                ins.then_inc(act_done, 1)
                AC.wait_ge(act_done, nth("ACT", "act_done"))
            else:
                ins.then_inc(sem("gates"), 1)
                AC.wait_ge(sem("gates"), nth("ACT", "gates"))
        act_headnorm(RS_A)
        for i, (t0, n) in enumerate(TILES):
            rsqrt_act(ST[0:n, 16:22])

    ROWS = ("cmp_k", "cmp_v", "sel_k", "sel_v", "win_k", "win_v")

    def pool_proj_a():
        nc.gpsimd.wait_ge(sem("kv"), nth("POOL", "kv"))
        for z, n in enumerate(ROWS):
            c = slice(z * KVW, (z + 1) * KVW)
            dst = O["p_" + n][0, 0].rearrange("(i p) g d -> p i (g d)", p=P)
            if z < 2:
                nc.gpsimd.dma_start(dst, KV[:, 0:2, c]).then_inc(sem("cmp_rows"), 16)
            else:
                nc.gpsimd.dma_start(dst, KV[:, 0:2, c]).then_inc(stored, 16)
            if z < 4:
                nc.gpsimd.dma_start(O["s_" + n][0].rearrange("b o g d -> b (o g d)"),
                                    KV[0:NB, 2, c]).then_inc(stored, 16)
            else:
                out = O["s_" + n][0].rearrange("b w g d -> b w (g d)")
                old = A["cache_" + n][0].rearrange("b w g d -> b w (g d)")
                nc.gpsimd.dma_start(out[:, WIN - 1, :], KV[0:NB, 2, c]).then_inc(stored, 16)
                nc.gpsimd.dma_start(out[:, 0:WIN - 1, :], old[:, 1:WIN, :]).then_inc(stored, 16)

    NXR = len(XR)

    def sp_cmp():
        nc.sync.wait_ge(sem("gates_in"), nth("SP", "gates_in"))
        nc.sync.dma_start(W1[:, :, :, :], A["cmp_w1"][0].rearrange("c (m p) f -> p c m f", p=P)).then_inc(sem("cmp_w"), 16)
        nc.sync.dma_start(PE_T[:, :, :], A["cmp_pe"][0].rearrange("c (m j) d -> (j d) c m", j=2)).then_inc(sem("cmp_w"), 16)
        nc.sync.dma_start(W2[:, :, :], A["cmp_w2"][0].rearrange("c f d -> f c d")).then_inc(sem("cmp_w"), 16)
        n = 0
        for z, nm in enumerate(("k", "v")):
            pool = A["cache_cmp_" + nm][0].rearrange("n (q j) g d -> n q (j g d)", j=2)
            for s in range(NB):
                if n >= NXR:
                    nc.sync.wait_ge(sem("xr_used"), nth("SP", "xr_used"))
                for pg in range(NPG):
                    page = nc.sync.value_load(PGT[0:1, s * NPG + pg:s * NPG + pg + 1], min_val=0, max_val=79)
                    nc.sync.dma_start(XR[n % NXR][64 * (pg % 2):64 * (pg % 2) + 64, pg // 2, :],
                                      pool[bass.ds(page, 1)].rearrange("n q c -> (n q) c")).then_inc(sem(f"xr{n % NXR}"), 16)
                n += 1
            nc.sync.wait_ge(sem("xr_used"), nth("SP", "xr_used"))
            if z == 0:
                nc.sync.wait_ge(sem("cmp_rows"), nth("SP", "cmp_rows", 16 * 2))
            nc.sync.dma_start(XR[n % NXR][:, 0, :],
                              O["p_cmp_" + nm][0, 0].rearrange("(q j) g d -> q (j g d)", j=2)).then_inc(sem(f"xr{n % NXR}"), 16)
            n += 1

    def halves(third):
        for hf in range(2):
            j, g = divmod(2 * third + hf, G)
            yield slice(64 * hf, 64 * hf + 64), slice(64 * j, 64 * j + 64), g

    def pe_turn(n, tiles, slot):
        for third in range(3):
            if third == 1:
                PE.wait_ge(v_free, v.room())
                b = v.claim()
            else:
                PE.wait_ge(a_free, a.room())
                b = a.claim()
            for t in range(tiles):
                m = tr(b[:, t * P:(t + 1) * P], XR[n % NXR][:, t, third * P:(third + 1) * P])
            m.then_inc(v_full if third == 1 else a_full, 1)

    def pe_windows(z, g0, ng, slots, w, n):
        PE.wait_ge(a_free, a.room())
        b = a.claim()
        for m in range(16):
            if ng == 1:
                x = XT[:, g0, 0:slots, m:m + 8 * (n - 1) + 1:8]
            else:
                x = XT[:, 0:ng, 0, m:m + 8 * (n - 1) + 1:8]
            i = mm(b[:, 0:w], W1[:, z, m, :], x, m == 0, m == 15)
        i.then_inc(a_full, 1)

    def pe_summaries(z, hid, g, seqs, n):
        PE.wait_ge(v_free, v.room())
        b = v.claim()
        if z == 0:
            o = 64 * (g % 2)
            m = mm(b[o:o + DH, 0:len(seqs) * n], W2[:, 0, :], hid)
        else:
            for q, s in enumerate(seqs):
                m = mm(b[0:n, q * DH:(q + 1) * DH], hid[:, q * n:(q + 1) * n], W2[:, 1, :])
        m.then_inc(v_full, 1)

    def act_turn(tiles, slot):
        for third in (0, 2):
            AC.wait_ge(a_full, a.filled())
            b = a.take()
            (src, dst, g), (src2, dst2, g2) = halves(third)
            AC.copy(XT[dst, g, slot, 0:tiles * P], b[src, 0:tiles * P])
            AC.copy(XT[dst2, g2, slot, 0:tiles * P], b[src2, 0:tiles * P]).then_inc(a_free, 1)
        AC.wait_ge(a_free, a.emptied())

    def dve_turn(tiles, slot):
        V.wait_ge(v_full, v.filled())
        b = v.take()
        (src, dst, g), (src2, dst2, g2) = halves(1)
        V.tensor_copy(XT[dst, g, slot, 0:tiles * P], b[src, 0:tiles * P])
        V.tensor_copy(XT[dst2, g2, slot, 0:tiles * P], b[src2, 0:tiles * P]).then_inc(v_free, 1)
        V.wait_ge(v_free, v.emptied())

    def act_windows(z, w, hb):
        AC.wait_ge(a_full, a.filled())
        b = a.take()
        AC.activation(HID[:, hb, 0:w], b[:, 0:w], ACT.Gelu_apprx_tanh, bias=CB[:, z:z + 1]).then_inc(a_free, 1)
        AC.wait_ge(a_free, a.emptied())

    def dve_summaries(z, g, seqs, n):
        V.wait_ge(v_full, v.filled())
        b = v.take()
        ns = len(seqs)
        if z == 0:
            o = 64 * (g % 2)
            V.tensor_copy(CKT[o:o + DH, g // 2, seqs[0]:seqs[0] + ns, 0:n],
                                    b[o:o + DH, 0:ns * n].rearrange("p (s n) -> p s n", n=n)).then_inc(v_free, 1)
            V.wait_ge(v_free, v.emptied())
        else:
            V.tensor_copy(CV[0:n, seqs[0]:seqs[0] + ns, g * DH:(g + 1) * DH],
                                    b[0:n, 0:ns * DH].rearrange("p (s d) -> p s d", d=DH)).then_inc(v_free, 1)
            V.wait_ge(v_free, v.emptied())

    def pe_cmp():
        PE.wait_ge(sem("cmp_w"), nth("PE", "cmp_w", 16 * 3))
        for z in range(2):
            PE.wait_ge(v_free, v.room())
            b = v.claim()
            for m in range(16):
                i = mm(b[0:1, 0:P], PE_T[:, z, m:m + 1], W1[:, z, m, :], m == 0, m == 15)
            i.then_inc(v_full, 1)
        PE.wait_ge(v_free, v.all_free())
        PE.wait_ge(v_free, v.room())
        b = v.claim()
        for z in range(2):
            i = tr(b[:, z:z + 1], CBR[0:1, z, :])
        i.then_inc(v_full, 1)
        n = 0
        hb = 0
        for z in range(2):
            for half in range(2):
                for s in range(4):
                    PE.wait_ge(sem(f"xr{n % NXR}"), nth("PE", f"xr{n % NXR}", 16 * NPG))
                    pe_turn(n, 4, s)
                    n += 1
                PE.wait_ge(a_free, a.all_free())
                PE.wait_ge(v_free, v.all_free())
                for g in range(G):
                    pe_windows(z, g, 1, 4, 4 * NCS, NCS)
                    PE.wait_ge(a_free, a.all_free())
                    pe_summaries(z, HID[:, hb % 2, 0:4 * NCS], g, range(4 * half, 4 * half + 4), NCS)
                    hb += 1
            PE.wait_ge(sem(f"xr{n % NXR}"), nth("PE", f"xr{n % NXR}", 16))
            pe_turn(n, 1, 0)
            n += 1
            PE.wait_ge(a_free, a.all_free())
            PE.wait_ge(v_free, v.all_free())
            pe_windows(z, 0, G, 1, G * NCP, NCP)
            PE.wait_ge(a_free, a.all_free())
            for g in range(G):
                pe_summaries(z, HID[:, hb % 2, g * NCP:(g + 1) * NCP], g, [8], NCP)
            hb += 1
        PE.wait_ge(sem("cksq"), nth("PE", "cksq"))
        for c in range(2):
            pp = P if c == 0 else DH
            PE.wait_ge(v_free, v.room())
            b = v.claim()
            PE.wait_ge(v_free, v.room())
            b2 = v.claim()
            mm(b[0:pp, 0:NB * NCS], C("headones", pp)[:, 0:pp], XT[0:pp, c, 0, 0:NB * NCS]).then_inc(v_full, 1)
            mm(b2[0:pp, 0:NCP], C("headones", pp)[:, 0:pp], XT[0:pp, c, 1, 0:NCP]).then_inc(v_full, 1)

    def act_cmp():
        hb = 0
        AC.wait_ge(sem("cmp_bias"), nth("ACT", "cmp_bias"))
        for z in range(2):
            for half in range(2):
                for s in range(4):
                    act_turn(4, s)
                    AC.copy(ST[:, 30:31], ST[:, 31:32]).then_inc(sem("xr_used"), 1)
                for g in range(G):
                    act_windows(z, 4 * NCS, hb % 2)
                    hb += 1
            act_turn(1, 0)
            AC.copy(ST[:, 30:31], ST[:, 31:32]).then_inc(sem("xr_used"), 1)
            act_windows(z, G * NCP, hb % 2)
            hb += 1
        for c in range(2):
            pp = P if c == 0 else DH
            rsqrt_act(XT[0:pp, c, 2:4, :].rearrange("p a b -> p (a b)")[:, 0:NB * NCS + NCP])

    def dve_cmp():
        for z in range(2):
            V.wait_ge(v_full, v.filled())
            b = v.take()
            V.tensor_copy(CBR[0:1, z, :], b[0:1, 0:P]).then_inc(v_free, 1)
            V.wait_ge(v_free, v.emptied())
        V.wait_ge(v_full, v.filled())
        b = v.take()
        tt(CB[:, :], b[:, 0:2], PAR[:, CB1:CB1 + 2], ALU.add).then_inc(v_free, 1)
        V.wait_ge(v_free, v.emptied())
        V.memset(ST[:, 8:9], 0.0).then_inc(sem("cmp_bias"), 1)
        V.wait_ge(sem("cmp_bias"), nth("DVE", "cmp_bias"))
        for z in range(2):
            for half in range(2):
                for s in range(4):
                    dve_turn(4, s)
                for g in range(G):
                    dve_summaries(z, g, range(4 * half, 4 * half + 4), NCS)
            dve_turn(1, 0)
            for g in range(G):
                dve_summaries(z, g, [8], NCP)
        for c in range(2):
            pp = P if c == 0 else DH
            s8 = XT[0:pp, c, 0, 0:NB * NCS].rearrange("p (s n) -> p s n", n=NCS)
            tt(s8, CKT[0:pp, c, 0:NB, 0:NCS], CKT[0:pp, c, 0:NB, 0:NCS], ALU.mult).then_inc(dve_done, 1)
            V.wait_ge(dve_done, nth("DVE", "dve_done"))
            tt(XT[0:pp, c, 1, 0:NCP], CKT[0:pp, c, 8, 0:NCP], CKT[0:pp, c, 8, 0:NCP], ALU.mult).then_inc(dve_done, 1)
            V.wait_ge(dve_done, nth("DVE", "dve_done"))
        V.memset(ST[:, 8:9], 0.0).then_inc(sem("cksq"), 1)
        V.wait_ge(sem("cksq"), nth("DVE", "cksq"))
        for c in range(2):
            pp = P if c == 0 else DH
            r = XT[0:pp, c, 2:4, :].rearrange("p a b -> p (a b)")[:, 0:NB * NCS + NCP]
            V.wait_ge(v_full, v.filled())
            b = v.take()
            V.tensor_copy(r[:, 0:NB * NCS], b[0:pp, 0:NB * NCS]).then_inc(v_free, 1)
            V.wait_ge(v_free, v.emptied())
            V.wait_ge(v_full, v.filled())
            b = v.take()
            V.tensor_copy(r[:, NB * NCS:], b[0:pp, 0:NCP]).then_inc(v_free, 1)
            V.wait_ge(v_free, v.emptied())
            rsqrt_dve(r, 1.0 / DH, 1e-6)
            k8, r8 = CKT[0:pp, c, 0:NB, 0:NCS], r[:, 0:NB * NCS].rearrange("p (s n) -> p s n", n=NCS)
            stt(k8, k8, PAR[0:pp, KG0:KG0 + 1], r8, ALU.mult, ALU.mult).then_inc(dve_done, 1)
            V.wait_ge(dve_done, nth("DVE", "dve_done"))
            k1 = CKT[0:pp, c, 8, 0:NCP]
            stt(k1, k1, PAR[0:pp, KG0:KG0 + 1], r[:, NB * NCS:], ALU.mult, ALU.mult).then_inc(dve_done, 1)
            V.wait_ge(dve_done, nth("DVE", "dve_done"))
        V.memset(ST[:, 8:9], 0.0).then_inc(sem("ck"), 1)
        V.wait_ge(sem("ck"), nth("DVE", "ck"))

    def gate(i, h, z):
        n = TILES[i][1]
        return KV[0:n, i, 6 * KVW + 3 * h + z:6 * KVW + 3 * h + z + 1]

    def qh(h, t0, n):
        o = 64 * (h % 2)
        return QT[o:o + DH, h // 2, t0:t0 + n]

    def pe_prompt():
        PE.wait_ge(sem("kv"), nth("PE", "kv"))
        for z in range(2):
            c0 = (2 + 2 * z) * KVW
            for c in range(2):
                w = P if c == 0 else DH
                PE.wait_ge(v_free, v.room())
                b = v.claim()
                for i in range(2):
                    m = tr(b[0:w, i * P:(i + 1) * P], KV[:, i, c0 + c * P:c0 + c * P + w])
                m.then_inc(v_full, 1)
            PE.wait_ge(v_free, v.room())
            b = v.claim()
            tr(b[:, 0:NB], KV[0:NB, 2, c0:c0 + P])
            tr(b[0:DH, NB:2 * NB], KV[0:NB, 2, c0 + P:c0 + KVW]).then_inc(v_full, 1)
        PE.wait_ge(sem("ck2"), nth("PE", "ck2"))
        for i in range(2):
            for odd in range(2):
                PE.wait_ge(v_free, v.room())
                b = v.claim()
                for h in range(odd, H, 2):
                    m = mm(b[:, h // 2 * NCP:(h // 2 + 1) * NCP], qh(h, i * P, P), CK2[64 * odd:64 * odd + DH, h // HG, :])
                m.then_inc(v_full, 1)
        PE.wait_ge(sem("cs"), nth("PE", "cs"))
        for i in range(2):
            for q in range(3):
                PE.wait_ge(v_free, v.room())
                b = v.claim()
                for h in range(4 * q, 4 * q + 4):
                    m = tr(b[0:NCP, (h % 4) * P:(h % 4 + 1) * P], CS[:, i, h * NCP:(h + 1) * NCP])
                m.then_inc(v_full, 1)
        for u in range(UNITS_P + 3):
            if u < UNITS_P:
                h, i, o, g, s = unit(u)
                PE.wait_ge(v_free, v.room())
                b = v.claim()
                for z in range(2):
                    m = mm(b[:, z * SEQ:z * SEQ + s], qh(h, i * P, P), KT[o:o + DH, z, g, 0:s])
                m.then_inc(v_full, 1)
            if u >= 3:
                h, i, o, g, s = unit(u - 3)
                PE.wait_ge(a_free, a.all_free())
                PE.wait_ge(v_free, v.room())
                b = v.claim()
                pt = PPT[:, (u - 3) % 2, :]
                mm(b[o:o + DH, 0:P], CV[0:NCP, 8, g * DH:(g + 1) * DH], CPT[0:NCP, i * H + h, :], True, False)
                for z in range(2):
                    c0 = (3 + 2 * z) * KVW + g * DH
                    for k in range(i + 1):
                        m = mm(b[o:o + DH, 0:P], KV[:, k, c0:c0 + DH], pt[:, z * SEQ + k * P:z * SEQ + (k + 1) * P],
                               False, z == 1 and k == i)
                m.then_inc(v_full, 1)
            if 2 <= u < UNITS_P + 2:
                h, i, o, g, s = unit(u - 2)
                PE.wait_ge(sem("probs"), nth("PE", "probs"))
                PE.wait_ge(a_free, a.room())
                b = a.claim()
                pp = PP[:, (u - 2) % 3, :]
                for z in range(2):
                    for k in range(i + 1):
                        c = slice(z * SEQ + k * P, z * SEQ + (k + 1) * P)
                        m = tr(b[:, c], pp[:, c])
                m.then_inc(a_full, 1)

    UNITS_P = 2 * H

    def unit(u):
        h, i = u // 2, u % 2
        return h, i, 64 * (h % 2), h // HG, (i + 1) * P

    def act_prompt():
        AC.wait_ge(sem("cs_max"), nth("ACT", "cs_max"))
        for i in range(2):
            ins = AC.activation(CS[:, i, :], CS[:, i, :], ACT.Exp)
            if i == 0:
                ins.then_inc(act_done, 1)
                AC.wait_ge(act_done, nth("ACT", "act_done"))
            else:
                ins.then_inc(sem("cs_exp"), 1)
                AC.wait_ge(sem("cs_exp"), nth("ACT", "cs_exp"))
        for u in range(UNITS_P + 2):
            if u < UNITS_P:
                h, i, o, g, s = unit(u)
                AC.wait_ge(sem("pmax"), nth("ACT", "pmax"))
                pp, st = PP[:, u % 3, :], ST[:, 40 + 4 * (u % 2):44 + 4 * (u % 2)]
                for z in range(2):
                    r = pp[:, z * SEQ:z * SEQ + s]
                    ins = AC.activation(r, r, ACT.Exp, bias=st[:, z:z + 1], accum_out=st[:, 2 + z:3 + z])
                ins.then_inc(sem("pexp"), 1)
            if u >= 2:
                h, i, o, g, s = unit(u - 2)
                AC.wait_ge(a_full, a.filled())
                b = a.take()
                AC.copy(PPT[:, u % 2, :].rearrange("p (z s) -> p z s", z=2)[:, :, 0:s],
                        b[:, :].rearrange("p (z s) -> p z s", z=2)[:, :, 0:s]).then_inc(a_free, 1)
        AC.wait_ge(a_free, a.emptied())

    def dve_prompt():
        for z in range(2):
            for c in range(2):
                V.wait_ge(v_full, v.filled())
                b = v.take()
                for g in (0, 1) if c == 0 else (2,):
                    o = 64 * (g % 2)
                    V.tensor_copy(KT[0:DH, z, g, :], b[o:o + DH, 0:SEQ]).then_inc(dve_done, 1)
                    V.wait_ge(dve_done, nth("DVE", "dve_done"))
                    ins = V.tensor_copy(KT[DH:P, z, g, :], b[o:o + DH, 0:SEQ])
                    if g:
                        ins.then_inc(v_free, 1)
                        V.wait_ge(v_free, v.emptied())
                    else:
                        ins.then_inc(dve_done, 1)
                        V.wait_ge(dve_done, nth("DVE", "dve_done"))
            V.wait_ge(v_full, v.filled())
            b = v.take()
            V.tensor_copy(KNEW[:, z, 0, :], b[:, 0:NB]).then_inc(dve_done, 1)
            V.wait_ge(dve_done, nth("DVE", "dve_done"))
            V.tensor_copy(KNEW[0:DH, z, 1, :], b[0:DH, NB:2 * NB]).then_inc(v_free, 1)
            V.wait_ge(v_free, v.emptied())
        for g in range(G):
            o = 64 * (g % 2)
            for hf in range(2):
                V.tensor_copy(CK2[64 * hf:64 * hf + DH, g, :], CKT[o:o + DH, g // 2, 8, 0:NCP]).then_inc(dve_done, 1)
                V.wait_ge(dve_done, nth("DVE", "dve_done"))
        V.memset(ST[:, 8:9], 0.0).then_inc(sem("ck2"), 1)
        V.wait_ge(sem("ck2"), nth("DVE", "ck2"))
        for i in range(2):
            for odd in range(2):
                V.wait_ge(v_full, v.filled())
                b = v.take()
                half = lambda ap: ap.rearrange("p (h two n) -> p h two n", two=2, n=NCP)[:, :, odd, :]
                tt(half(CS[:, i, :]), b[:, 0:H // 2 * NCP].rearrange("p (h n) -> p h n", n=NCP),
                             half(C("cmpbias")[:, i * H * NCP:(i + 1) * H * NCP]), ALU.add).then_inc(v_free, 1)
                V.wait_ge(v_free, v.emptied())
        for i in range(2):
            c3 = CS[:, i, :].rearrange("p (h n) -> p h n", h=H)
            mx = ST[:, 44:56]
            V.tensor_reduce(mx, c3, AX_X, ALU.max).then_inc(dve_done, 1)
            V.wait_ge(dve_done, nth("DVE", "dve_done"))
            tt(c3, c3, mx.unsqueeze(2).broadcast_to([P, H, NCP]), ALU.subtract).then_inc(dve_done, 1)
            V.wait_ge(dve_done, nth("DVE", "dve_done"))
        V.memset(ST[:, 8:9], 0.0).then_inc(sem("cs_max"), 1)
        V.wait_ge(sem("cs_max"), nth("DVE", "cs_max"))
        V.wait_ge(sem("cs_exp"), nth("DVE", "cs_exp"))
        for i in range(2):
            c3 = CS[:, i, :].rearrange("p (h n) -> p h n", h=H)
            ms = C("cmpmask")[:, i * NCP:(i + 1) * NCP].unsqueeze(1).broadcast_to([P, H, NCP])
            sm = ST[:, 44:56]
            tt(c3, c3, ms, ALU.mult).then_inc(dve_done, 1)
            V.wait_ge(dve_done, nth("DVE", "dve_done"))
            V.tensor_reduce(sm, c3, AX_X, ALU.add).then_inc(dve_done, 1)
            V.wait_ge(dve_done, nth("DVE", "dve_done"))
            ts(sm, sm, 1e-30, None, ALU.max).then_inc(dve_done, 1)
            V.wait_ge(dve_done, nth("DVE", "dve_done"))
            V.reciprocal(sm, sm).then_inc(dve_done, 1)
            V.wait_ge(dve_done, nth("DVE", "dve_done"))
            if i == 0:
                V.wait_ge(sem("gates"), nth("DVE", "gates"))
            gt = KV[:, i, 6 * KVW:KVN].rearrange("p (h z) -> p h z", z=3)[:, :, 0]
            tt(sm, sm, gt, ALU.mult).then_inc(dve_done, 1)
            V.wait_ge(dve_done, nth("DVE", "dve_done"))
            tt(c3, c3, sm.unsqueeze(2).broadcast_to([P, H, NCP]), ALU.mult).then_inc(dve_done, 1)
            V.wait_ge(dve_done, nth("DVE", "dve_done"))
        V.memset(ST[:, 8:9], 0.0).then_inc(sem("cs"), 1)
        V.wait_ge(sem("cs"), nth("DVE", "cs"))
        for i in range(2):
            for q in range(3):
                V.wait_ge(v_full, v.filled())
                b = v.take()
                V.tensor_copy(CPT[0:NCP, i * H + 4 * q:i * H + 4 * q + 4, :],
                                        b[0:NCP, :].rearrange("p (h t) -> p h t", h=4)).then_inc(v_free, 1)
                V.wait_ge(v_free, v.emptied())
        for u in range(UNITS_P + 3):
            if u < UNITS_P:
                h, i, o, g, s = unit(u)
                st = ST[:, 40 + 4 * (u % 2):44 + 4 * (u % 2)]
                V.wait_ge(v_full, v.filled())
                b = v.take()
                pv = PP[:, u % 3, :].rearrange("p (z s) -> p z s", z=2)[:, :, 0:s]
                dist = C("distp").rearrange("p (i s) -> p i s", i=2)[:, i:i + 1, 0:s].broadcast_to([P, 2, s])
                stt(pv, dist, float(SLOPES[h]), b[:, :].rearrange("p (z s) -> p z s", z=2)[:, :, 0:s],
                    ALU.mult, ALU.add).then_inc(v_free, 1)
                V.wait_ge(v_free, v.emptied())
                V.tensor_reduce(st[:, 0:2], pv, AX_X, ALU.max, negate=True).then_inc(sem("pmax"), 1)
            if 1 <= u < UNITS_P + 1:
                h, i, o, g, s = unit(u - 1)
                st = ST[:, 40 + 4 * ((u - 1) % 2):44 + 4 * ((u - 1) % 2)]
                V.wait_ge(sem("pexp"), nth("DVE", "pexp"))
                V.reciprocal(st[:, 2:4], st[:, 2:4]).then_inc(dve_done, 1)
                V.wait_ge(dve_done, nth("DVE", "dve_done"))
                tt(st[:, 2:4], st[:, 2:4], KV[:, i, 6 * KVW + 3 * h + 1:6 * KVW + 3 * h + 3], ALU.mult).then_inc(dve_done, 1)
                V.wait_ge(dve_done, nth("DVE", "dve_done"))
                pv = PP[:, (u - 1) % 3, :].rearrange("p (z s) -> p z s", z=2)[:, :, 0:s]
                tt(pv, pv, st[:, 2:4].unsqueeze(2).broadcast_to([P, 2, s]), ALU.mult).then_inc(sem("probs"), 1)
            if u >= 3:
                h, i, o, g, s = unit(u - 3)
                V.wait_ge(v_full, v.filled())
                b = v.take()
                V.tensor_copy(MIXT[o:o + DH, h // 2, i * P:(i + 1) * P], b[o:o + DH, 0:P]).then_inc(v_free, 1)
        V.wait_ge(v_free, v.emptied())

    NS = PAST + 1
    NW = WIN + 1
    S_SEL, S_WIN, S_CMP = slice(0, NS), slice(NS, NS + NW), slice(NS + NW, NS + NW + NCS)

    NOLD = len(OLD)

    def sp_sample():
        nc.sync.wait_ge(sem("ck"), nth("SP", "ck"))
        nc.sync.wait_ge(sem("u1_used"), nth("SP", "u1_used"))
        for n in range(2 * NB):
            s, nm = n % NB, "k" if n < NB else "v"
            if n >= NOLD:
                used = "keys_used" if n - NOLD < NB else "v_used"
                nc.sync.wait_ge(sem(used), nth("SP", used))
            pool = A["cache_sel_" + nm][0].rearrange("n p g d -> n p (g d)")
            for pg in range(NPG):
                page = nc.sync.value_load(PGT[0:1, s * NPG + pg:s * NPG + pg + 1], min_val=0, max_val=79)
                nc.sync.dma_start(OLD[n % NOLD][:, pg, :],
                                  pool[bass.ds(page, 1)].rearrange("n p c -> (n p) c")).then_inc(sem(f"old{n % NOLD}"), 16)
            nc.sync.dma_start(OLD[n % NOLD][:, NPG:NPG + 4, :],
                              A["cache_win_" + nm][0, s].rearrange("(t p) g d -> p t (g d)", p=P)).then_inc(
                                  sem(f"old{n % NOLD}"), 16)

    def pe_sample_scores():
        PE.wait_ge(sem("qbd"), nth("PE", "qbd"))
        PE.wait_ge(v_free, v.room())
        b3 = v.claim()
        for s in range(NB):
            mm(b3[0:RS, 0:NCS], QBD[:, 0, s, :], CKT[:, 0, s, 0:NCS], s == 0, False)
            m = mm(b3[0:RS, 0:NCS], QBD[0:DH, 1, s, :], CKT[0:DH, 1, s, 0:NCS], False, s == NB - 1)
        for z in range(2):
            for s in range(NB):
                mm(b3[0:RS, 64 + z:65 + z], QBD[:, 0, s, :], KNEW[:, z, 0, s:s + 1], s == 0, False)
                m = mm(b3[0:RS, 64 + z:65 + z], QBD[0:DH, 1, s, :], KNEW[0:DH, z, 1, s:s + 1], False, s == NB - 1)
        m.then_inc(v_full, 1)
        bs = []
        for _ in range(3):
            PE.wait_ge(v_free, v.room())
            bs.append(v.claim())
        for s in range(NB):
            old = f"old{s % NOLD}"
            PE.wait_ge(sem(old), nth("PE", old, 16 * (NPG + 1)))
            for c in range(2):
                w = P if c == 0 else DH
                for q in range(3):
                    PE.wait_ge(a_free, a.room())
                    b = a.claim()
                    for t in range(4):
                        m = tr(b[0:w, t * P:(t + 1) * P], OLD[s % NOLD][:, 4 * q + t, c * P:c * P + w])
                    m.then_inc(a_full, 1)
            PE.wait_ge(a_free, a.all_free())
            for c in range(2):
                w = P if c == 0 else DH
                for q in range(3):
                    m = mm(bs[q][0:RS, :], QBD[0:w, c, s, :], KTS[0:w, c, q * 512:(q + 1) * 512],
                           s == 0 and c == 0, s == NB - 1 and c == 1)
                    if s == NB - 1 and c == 1:
                        m.then_inc(v_full, 1)

    def act_sample_scores():
        for s in range(NB):
            for c in range(2):
                w = P if c == 0 else DH
                for q in range(3):
                    AC.wait_ge(a_full, a.filled())
                    b = a.take()
                    AC.copy(KTS[0:w, c, q * 512:(q + 1) * 512], b[0:w, :]).then_inc(a_free, 1)
                    AC.wait_ge(a_free, a.emptied())
            AC.copy(ST[:, 30:31], ST[:, 31:32]).then_inc(sem("keys_used"), 1)

    def dve_sample_scores():
        V.memset(QBD[:, :, :, :], 0.0).then_inc(dve_done, 1)
        V.wait_ge(dve_done, nth("DVE", "dve_done"))
        for h in range(H):
            g = h // HG
            o, src = 64 * (g % 2), 64 * (h % 2)
            rows = QBD[o:o + DH, g // 2, :, :].rearrange("p b r -> p (b r)")
            V.tensor_copy(rows[:, h:h + (RS + H) * (NB - 1) + 1:RS + H], QT[src:src + DH, h // 2, SEQ:NT]).then_inc(dve_done, 1)
            V.wait_ge(dve_done, nth("DVE", "dve_done"))
        V.memset(ST[:, 8:9], 0.0).then_inc(sem("qbd"), 1)
        V.wait_ge(sem("qbd"), nth("DVE", "qbd"))
        sl = C("slope", RS)
        V.wait_ge(v_full, v.filled())
        b3 = v.take()
        stt(SS[0:RS, S_CMP], C("cpos", RS), sl, b3[0:RS, 0:NCS], ALU.mult, ALU.add).then_inc(dve_done, 1)
        V.wait_ge(dve_done, nth("DVE", "dve_done"))
        V.tensor_copy(SS[0:RS, NS - 1:NS], b3[0:RS, 64:65]).then_inc(dve_done, 1)
        V.wait_ge(dve_done, nth("DVE", "dve_done"))
        V.tensor_copy(SS[0:RS, NS + NW - 1:NS + NW], b3[0:RS, 65:66]).then_inc(v_free, 1)
        V.wait_ge(v_free, v.emptied())
        pos = C("pos", RS)
        for q in range(3):
            V.wait_ge(v_full, v.filled())
            b = v.take()
            o, c = (512 * q, 512 * q) if q < 2 else (NS, PAST - WIN)
            stt(SS[0:RS, o:o + 512], pos[:, c:c + 512], sl, b[0:RS, :], ALU.mult, ALU.add).then_inc(v_free, 1)
            V.wait_ge(v_free, v.emptied())
        V.memset(ST[:, 8:9], 0.0).then_inc(sem("mem_go"), 1)
        V.wait_ge(sem("mem_go"), nth("DVE", "mem_go"))

        sm = SMALL
        soft(S_CMP, 0)
        V.reciprocal(sm[0:RS, 8:9], sm[0:RS, 4:5]).then_inc(dve_done, 1)
        V.wait_ge(dve_done, nth("DVE", "dve_done"))
        ts(SS[0:RS, S_CMP], SS[0:RS, S_CMP], sm[0:RS, 8:9], None, ALU.mult).then_inc(sem("pc"), 1)
        V.wait_ge(sem("pc"), nth("DVE", "pc"))
        V.wait_ge(v_full, v.filled())
        b = v.take()
        V.tensor_copy(SPT[0:NCS, 12, :], b[0:NCS, 0:RS]).then_inc(v_free, 1)
        V.wait_ge(v_free, v.emptied())
        V.wait_ge(v_full, v.filled())
        b = v.take()
        V.tensor_copy(sm[0:RS, 16:16 + NSEL], b[0:RS, 0:NSEL]).then_inc(v_free, 1)
        V.wait_ge(v_free, v.emptied())
        V.wait_ge(v_full, v.filled())
        b = v.take()
        V.tensor_copy(sm[0:RS, 40:40 + NSEL], b[0:RS, 0:NSEL]).then_inc(v_free, 1)
        V.wait_ge(v_free, v.emptied())
        nb = NSEL - 3
        imp, eq = sm[0:RS, 41:41 + nb], sm[0:RS, 60:60 + nb]
        V.tensor_reduce(sm[0:RS, 10:11], imp, AX_X, ALU.min).then_inc(dve_done, 1)
        V.wait_ge(dve_done, nth("DVE", "dve_done"))
        ts(eq, imp, sm[0:RS, 10:11], None, ALU.is_le).then_inc(dve_done, 1)
        V.wait_ge(dve_done, nth("DVE", "dve_done"))
        tt(eq, eq, C("blkno", RS), ALU.mult).then_inc(dve_done, 1)
        V.wait_ge(dve_done, nth("DVE", "dve_done"))
        V.tensor_reduce(sm[0:RS, 11:12], eq, AX_X, ALU.max).then_inc(dve_done, 1)
        V.wait_ge(dve_done, nth("DVE", "dve_done"))
        ts(sm[0:RS, 80:80 + nb], C("blkno", RS), sm[0:RS, 11:12], NEG, ALU.is_equal, ALU.mult).then_inc(dve_done, 1)
        V.wait_ge(dve_done, nth("DVE", "dve_done"))
        blocks = SS[0:RS, SEL:SEL * (nb + 1)].rearrange("p (n k) -> p n k", k=SEL)
        tt(blocks, blocks, sm[0:RS, 80:80 + nb].unsqueeze(2).broadcast_to([RS, nb, SEL]), ALU.add).then_inc(dve_done, 1)
        V.wait_ge(dve_done, nth("DVE", "dve_done"))
        soft(S_SEL, 1)
        soft(S_WIN, 2)
        V.reciprocal(sm[0:RS, 8:10], sm[0:RS, 5:7]).then_inc(dve_done, 1)
        V.wait_ge(dve_done, nth("DVE", "dve_done"))
        V.wait_ge(sem("gate_rows"), nth("DVE", "gate_rows", 16 * NB))
        tt(sm[0:RS, 8:10], sm[0:RS, 8:10], sm[0:RS, 13:15], ALU.mult).then_inc(dve_done, 1)
        V.wait_ge(dve_done, nth("DVE", "dve_done"))
        ts(SS[0:RS, S_SEL], SS[0:RS, S_SEL], sm[0:RS, 8:9], None, ALU.mult).then_inc(dve_done, 1)
        V.wait_ge(dve_done, nth("DVE", "dve_done"))
        ts(SS[0:RS, S_WIN], SS[0:RS, S_WIN], sm[0:RS, 9:10], None, ALU.mult).then_inc(dve_done, 1)
        V.wait_ge(dve_done, nth("DVE", "dve_done"))
        ts(SS[0:RS, S_CMP], SS[0:RS, S_CMP], sm[0:RS, 12:13], None, ALU.mult).then_inc(dve_done, 1)
        V.wait_ge(dve_done, nth("DVE", "dve_done"))
        for z, c in enumerate((NS - 1, NS + NW - 1)):
            ts(PDD[0:RS, z, :], ident[0:RS, 0:RS], SS[0:RS, c:c + 1], None, ALU.mult).then_inc(dve_done, 1)
            V.wait_ge(dve_done, nth("DVE", "dve_done"))
        V.memset(ST[:, 8:9], 0.0).then_inc(sem("ps"), 1)
        V.wait_ge(sem("ps"), nth("DVE", "ps"))
        for t in range(4):
            V.wait_ge(v_full, v.filled())
            b = v.take()
            n = min(4, 13 - 4 * t)
            w = P if t < 3 else NCS
            V.tensor_copy(SPT[0:w, 4 * t:4 * t + n, :], b[0:w, 0:n * RS].rearrange("p (a r) -> p a r", r=RS)).then_inc(v_free, 1)
            V.wait_ge(v_free, v.emptied())
        V.wait_ge(v_full, v.filled())
        b = v.take()
        V.tensor_copy(PD[0:NB, :, :], b[0:NB, 0:2 * RS].rearrange("p (a r) -> p a r", r=RS)).then_inc(v_free, 1)
        V.wait_ge(v_free, v.emptied())
        for s in range(NB):
            V.wait_ge(v_full, v.filled())
            b = v.take()
            V.tensor_copy(VO[:, s, :], b[:, 0:KVW]).then_inc(v_free, 1)
        V.wait_ge(v_full, v.filled())
        b = v.take()
        o = b[0:DH, 0:RS].rearrange("p (b c two) -> p c b two", b=NB, two=2)
        V.tensor_copy(MIXT[0:DH, 0:6, SEQ:NT], o[:, :, :, 0]).then_inc(dve_done, 1)
        V.wait_ge(dve_done, nth("DVE", "dve_done"))
        V.tensor_copy(MIXT[DH:P, 0:6, SEQ:NT], o[:, :, :, 1]).then_inc(v_free, 1)
        V.wait_ge(v_free, v.emptied())

    def soft(cols, z):
        sm = SMALL
        V.tensor_reduce(sm[0:RS, z:z + 1], SS[0:RS, cols], AX_X, ALU.max).then_inc(dve_done, 1)
        V.wait_ge(dve_done, nth("DVE", "dve_done"))
        ts(sm[0:RS, z:z + 1], sm[0:RS, z:z + 1], -1.0, None, ALU.mult).then_inc(sem("smax"), 1)
        V.wait_ge(sem("smax"), nth("DVE", "smax"))
        V.wait_ge(sem("sexp"), nth("DVE", "sexp"))

    def act_soft(cols, z):
        AC.wait_ge(sem("smax"), nth("ACT", "smax"))
        AC.activation(SS[0:RS, cols], SS[0:RS, cols], ACT.Exp, bias=SMALL[0:RS, z:z + 1],
                                          accum_out=SMALL[0:RS, 4 + z:5 + z]).then_inc(sem("sexp"), 1)
        AC.wait_ge(sem("sexp"), nth("ACT", "sexp"))

    def act_sample():
        act_sample_scores()
        act_soft(S_CMP, 0)
        act_soft(S_SEL, 1)
        act_soft(S_WIN, 2)

    def pool_sample():
        nc.gpsimd.wait_ge(sem("gates"), nth("POOL", "gates"))
        nc.gpsimd.wait_ge(sem("qbd"), nth("POOL", "qbd"))
        g = KV[0:NB, 2, 6 * KVW:KVN].rearrange("b (h z) -> b h z", z=3)
        for s in range(NB):
            nc.gpsimd.dma_start(SMALL[s * H:(s + 1) * H, 12:15], g[s:s + 1, :, :]).then_inc(sem("gate_rows"), 16)

    PDD = place("PDD", 87000 // 32 * 32, [2, RS])

    def pe_sample_values():
        PE.wait_ge(sem("pc"), nth("PE", "pc"))
        PE.wait_ge(v_free, v.room())
        b = v.claim()
        tr(b[0:NCS, 0:RS], SS[0:RS, S_CMP]).then_inc(v_full, 1)
        PE.wait_ge(v_free, v.all_free())
        PE.wait_ge(v_free, v.room())
        b = v.claim()
        mm(b[0:RS, 0:NSEL], SPT[0:NCS, 12, :], C("cmpsel", NCS)).then_inc(v_full, 1)
        PE.wait_ge(v_free, v.all_free())
        PE.wait_ge(v_free, v.room())
        b = v.claim()
        mm(b[0:RS, 0:NSEL], C("samegroup", RS), SMALL[0:RS, 16:16 + NSEL]).then_inc(v_full, 1)
        PE.wait_ge(sem("ps"), nth("PE", "ps"))
        for t in range(4):
            PE.wait_ge(v_free, v.room())
            b = v.claim()
            for j in range(min(4, 13 - 4 * t)):
                k = 4 * t + j
                c0 = P * k if k < 8 else NS + P * (k - 8) if k < 12 else NS + NW
                w = P if k < 12 else NCS
                m = tr(b[0:w, j * RS:(j + 1) * RS], SS[0:RS, c0:c0 + w])
            m.then_inc(v_full, 1)
        PE.wait_ge(v_free, v.room())
        b = v.claim()
        for z in range(2):
            m = mm(b[0:NB, z * RS:(z + 1) * RS], C("rowseq", RS), PDD[0:RS, z, :])
        m.then_inc(v_full, 1)
        PE.wait_ge(v_free, v.all_free())
        PE.wait_ge(v_free, v.room())
        b = v.claim()
        for s in range(NB):
            if s:
                PE.wait_ge(v_free, v.room())
                b = v.claim()
            r = slice(ROW0[s], ROW0[s] + SLOT)
            items = [(SPT[0:NCS, 12, r], CV[0:NCS, s, :])]
            for z in range(2):
                c0 = (3 + 2 * z) * KVW
                items.append((PD[0:NB, z, r], KV[0:NB, 2, c0:c0 + KVW]))
            items += [(SPT[:, t, r], OLD[(NB + s) % NOLD][:, t, :]) for t in range(NPG + 4)]
            old = f"old{(NB + s) % NOLD}"
            for n, (probs, values) in enumerate(items):
                if n == 3:
                    PE.wait_ge(sem(old), nth("PE", old, 16 * (NPG + 1)))
                q = n % 4
                m = PE.matmul(b[q * SLOT:(q + 1) * SLOT, 0:KVW], lhsT=probs, rhs=values, start=n < 4,
                              stop=n >= len(items) - 4, skip_group_check=True)
                if n == 0 and s:
                    m.then_inc(sem("v_used"), 1)
            m.then_inc(v_full, 1)
        PE.wait_ge(v_free, v.all_free())
        PE.wait_ge(v_free, v.room())
        b = v.claim()
        for s in range(NB):
            for g in range(G):
                c = s * H - ROW0[s] + g * HG
                m = mm(b[0:DH, s * H + g * HG:s * H + (g + 1) * HG], VO[:, s, g * DH:(g + 1) * DH], C("fold")[:, c:c + HG])
        m.then_inc(v_full, 1)

    ROW0 = [min(s * H, RS - SLOT) for s in range(NB)]

    def mem_tiles(base):
        return dict(
            MK=place("MK", base, [2, 2, SEQ]), MV=place("MV", base + 4096, [2, 2, SEQ]),
            MQ=place("MQ", base + 8192, [2, NB, NB * MH]), MS=place("MS", base + 10240, [SEQ]),
            MPT=place("MPT", base + 11264, [2, SEQ]), MST=place("MST", base + 13312, [2, NB * MH]),
            MP=place("MP", base + 13568, [2, 2, SEQ]), MKT=place("MKT", base + 17664, [NB, 2, SEQ]))

    MTL = [mem_tiles(58304), mem_tiles(0)]
    RM = NB * MH

    def sp_memattn(l):
        m = MTL[l]
        nc.sync.wait_ge(sem("mem_go"), nth("SP", "mem_go"))
        for z, nm in enumerate(("k", "v")):
            for s in range(NB):
                if s >= 2:
                    nc.sync.wait_ge(sem(f"m{nm}_used"), nth("SP", f"m{nm}_used"))
                nc.sync.dma_start(m["MK" if z == 0 else "MV"][:, s % 2, :, :],
                    A["cache_mem_" + nm][l, s].rearrange("(t p) h d -> p t (h d)", p=P)).then_inc(sem(f"m{nm}{s % 2}"), 16)
            nth("SP", f"m{nm}_used", 2 - z)

    def pe_memattn(l):
        T, KVM, q0 = MTL[l], KVMS[l], 6 if l == 0 else 0
        PE.wait_ge(sem("mq"), nth("PE", "mq"))
        for u in range(NB):
            if 2 <= u < MH + 2:
                h = u - 2
                o = 64 * (h % 2)
                PE.wait_ge(v_free, v.all_free())
                PE.wait_ge(v_free, v.room())
                b = v.claim()
                for t in range(2):
                    m = mm(b[o:o + DH, 0:SEQ], KVM[:, t, MEMQ + h * DH:MEMQ + (h + 1) * DH], T["MPT"][:, t, :], t == 0, t == 1)
                m.then_inc(v_full, 1)
            if u < MH:
                o = 64 * (u % 2)
                PE.wait_ge(v_free, v.room())
                b = v.claim()
                for i in range(2):
                    m = mm(b[:, i * SEQ:(i + 1) * SEQ], QT[o:o + DH, q0 + u // 2, i * P:(i + 1) * P], KMT[o:o + DH, u // 2, :])
                m.then_inc(v_full, 1)
            PE.wait_ge(sem(f"mk{u % 2}"), nth("PE", f"mk{u % 2}", 16))
            PE.wait_ge(a_free, a.room())
            b = a.claim()
            for c in range(2):
                for t in range(2):
                    m = tr(b[:, c * SEQ + t * P:c * SEQ + (t + 1) * P], T["MK"][:, u % 2, t, c * P:(c + 1) * P])
            m.then_inc(a_full, 1)
            if 1 <= u < MH + 1:
                PE.wait_ge(sem("mprobs"), nth("PE", "mprobs"))
                PE.wait_ge(v_free, v.room())
                b = v.claim()
                for t in range(2):
                    for i in range(2):
                        m = tr(b[:, (2 * t + i) * P:(2 * t + i + 1) * P], T["MP"][:, (u - 1) % 2, i, t * P:(t + 1) * P])
                m.then_inc(v_full, 1)
        PE.wait_ge(a_free, a.all_free())
        PE.wait_ge(v_free, v.room())
        b = v.claim()
        for s in range(NB):
            for c in range(2):
                m = mm(b[0:RM, 0:SEQ], T["MQ"][:, c, s, :], T["MKT"][:, s, c, :], s == 0 and c == 0, s == NB - 1 and c == 1)
        m.then_inc(v_full, 1)
        PE.wait_ge(sem("msprobs"), nth("PE", "msprobs"))
        PE.wait_ge(v_free, v.room())
        b = v.claim()
        for t in range(2):
            m = tr(b[:, t * RM:(t + 1) * RM], T["MS"][0:RM, t * P:(t + 1) * P])
        m.then_inc(v_full, 1)
        PE.wait_ge(v_free, v.all_free())
        PE.wait_ge(v_free, v.room())
        b = v.claim()
        for s in range(NB):
            PE.wait_ge(sem(f"mv{s % 2}"), nth("PE", f"mv{s % 2}", 16))
            for h in range(MH):
                r = s * MH + h
                for t in range(2):
                    m = mm(b[0:DH, r:r + 1], T["MV"][:, s % 2, t, h * DH:(h + 1) * DH], T["MST"][:, t, r:r + 1], t == 0, t == 1)
            if s < NB - 1:
                m.then_inc(sem("mv_used"), 1)
            else:
                m.then_inc(v_full, 1)

    def act_memattn(l):
        T = MTL[l]
        for u in range(NB):
            if u < MH:
                AC.wait_ge(sem("mmax"), nth("ACT", "mmax"))
                st = ST[:, 40 + 4 * (u % 2):44 + 4 * (u % 2)]
                for i in range(2):
                    r = T["MP"][:, u % 2, i, :]
                    ins = AC.activation(r, r, ACT.Exp, bias=st[:, i:i + 1], scale=DH ** -0.5, accum_out=st[:, 2 + i:3 + i])
                ins.then_inc(sem("mexp"), 1)
            AC.wait_ge(a_full, a.filled())
            b = a.take()
            AC.copy(T["MKT"][:, u, :, :].rearrange("p c m -> p (c m)"), b[:, :]).then_inc(a_free, 1)
            AC.wait_ge(a_free, a.emptied())
            AC.copy(ST[:, 30:31], ST[:, 31:32]).then_inc(sem("mk_used"), 1)
        AC.wait_ge(sem("msmax"), nth("ACT", "msmax"))
        AC.activation(T["MS"][0:RM, :], T["MS"][0:RM, :], ACT.Exp, bias=ST[0:RM, 40:41],
                                           accum_out=ST[0:RM, 42:43]).then_inc(sem("msexp"), 1)
        AC.wait_ge(sem("msexp"), nth("ACT", "msexp"))

    def dve_memattn(l):
        T, q0 = MTL[l], 6 if l == 0 else 0
        if l:
            V.memset(ST[:, 8:9], 0.0).then_inc(sem("mem_go"), 1)
            V.wait_ge(sem("mem_go"), nth("DVE", "mem_go"))
        V.memset(T["MQ"][:, :, :, :], 0.0).then_inc(dve_done, 1)
        V.wait_ge(dve_done, nth("DVE", "dve_done"))
        for h in range(MH):
            o = 64 * (h % 2)
            rows = T["MQ"][o:o + DH, h // 2, :, :].rearrange("p b r -> p (b r)")
            V.tensor_copy(rows[:, h:h + (RM + MH) * (NB - 1) + 1:RM + MH], QT[o:o + DH, q0 + h // 2, SEQ:NT]).then_inc(dve_done, 1)
            V.wait_ge(dve_done, nth("DVE", "dve_done"))
        V.memset(ST[:, 8:9], 0.0).then_inc(sem("mq"), 1)
        V.wait_ge(sem("mq"), nth("DVE", "mq"))
        for u in range(MH + 2):
            if u >= 2:
                h = u - 2
                o = 64 * (h % 2)
                V.wait_ge(v_full, v.filled())
                b = v.take()
                V.tensor_copy(MIXT[o:o + DH, 6 + h // 2, 0:SEQ], b[o:o + DH, 0:SEQ]).then_inc(v_free, 1)
            if u < MH:
                st = ST[:, 40 + 4 * (u % 2):44 + 4 * (u % 2)]
                V.wait_ge(v_full, v.filled())
                b = v.take()
                V.tensor_copy(T["MP"][:, u % 2, :, :].rearrange("p i m -> p (i m)"), b[:, :]).then_inc(v_free, 1)
                V.wait_ge(v_free, v.emptied())
                V.tensor_reduce(st[:, 0:2], T["MP"][:, u % 2, :, :], AX_X, ALU.max).then_inc(dve_done, 1)
                V.wait_ge(dve_done, nth("DVE", "dve_done"))
                ts(st[:, 0:2], st[:, 0:2], -(DH ** -0.5), None, ALU.mult).then_inc(sem("mmax"), 1)
            if 1 <= u < MH + 1:
                st = ST[:, 40 + 4 * ((u - 1) % 2):44 + 4 * ((u - 1) % 2)]
                mp = T["MP"][:, (u - 1) % 2, :, :]
                V.wait_ge(sem("mexp"), nth("DVE", "mexp"))
                V.reciprocal(st[:, 2:4], st[:, 2:4]).then_inc(dve_done, 1)
                V.wait_ge(dve_done, nth("DVE", "dve_done"))
                tt(mp, mp, st[:, 2:4].unsqueeze(2).broadcast_to([P, 2, SEQ]), ALU.mult).then_inc(sem("mprobs"), 1)
                V.wait_ge(v_full, v.filled())
                b = v.take()
                V.tensor_copy(T["MPT"][:, :, :].rearrange("p i m -> p (i m)"), b[:, :]).then_inc(v_free, 1)
        V.wait_ge(v_free, v.emptied())
        V.wait_ge(v_full, v.filled())
        b = v.take()
        MS = T["MS"]
        ts(MS[0:RM, :], b[0:RM, 0:SEQ], DH ** -0.5, None, ALU.mult).then_inc(v_free, 1)
        V.wait_ge(v_free, v.emptied())
        V.tensor_reduce(ST[0:RM, 40:41], MS[0:RM, :], AX_X, ALU.max).then_inc(dve_done, 1)
        V.wait_ge(dve_done, nth("DVE", "dve_done"))
        ts(ST[0:RM, 40:41], ST[0:RM, 40:41], -1.0, None, ALU.mult).then_inc(sem("msmax"), 1)
        V.wait_ge(sem("msmax"), nth("DVE", "msmax"))
        V.wait_ge(sem("msexp"), nth("DVE", "msexp"))
        V.reciprocal(ST[0:RM, 42:43], ST[0:RM, 42:43]).then_inc(dve_done, 1)
        V.wait_ge(dve_done, nth("DVE", "dve_done"))
        ts(MS[0:RM, :], MS[0:RM, :], ST[0:RM, 42:43], None, ALU.mult).then_inc(sem("msprobs"), 1)
        V.wait_ge(sem("msprobs"), nth("DVE", "msprobs"))
        V.wait_ge(v_full, v.filled())
        b = v.take()
        V.tensor_copy(T["MST"][:, :, :].rearrange("p i m -> p (i m)"), b[:, 0:2 * RM]).then_inc(v_free, 1)
        V.wait_ge(v_free, v.emptied())
        V.wait_ge(v_full, v.filled())
        b = v.take()
        o = b[0:DH, 0:RM].rearrange("p (b c two) -> p c b two", b=NB, two=2)
        V.tensor_copy(MIXT[0:DH, 6:8, SEQ:NT], o[:, :, :, 0]).then_inc(dve_done, 1)
        V.wait_ge(dve_done, nth("DVE", "dve_done"))
        V.tensor_copy(MIXT[DH:P, 6:8, SEQ:NT], o[:, :, :, 1]).then_inc(v_free, 1)
        V.wait_ge(v_free, v.emptied())

    def sp_wo(l):
        nc.sync.wait_ge(sem("v_used"), NB - 1)
        nc.sync.dma_start(WO[:, :, :], A["w_out"][l].rearrange("(k p) n -> p k n", p=P)).then_inc(sem("w_out"), 16)

    def pe_out(l):
        PE.wait_ge(sem("w_out"), nth("PE", "w_out", 16))
        PE.wait_ge(v_free, v.all_free())
        PE.wait_ge(sem("mix"), nth("PE", "mix"))
        for i, (t0, n) in enumerate(TILES):
            for hf in range(2):
                PE.wait_ge(v_free, v.room())
                b = v.claim()
                for c in range(KD):
                    m = mm(b[0:n, :], MIXT[:, c, t0:t0 + n], WO[:, c, hf * 512:(hf + 1) * 512], c == 0, c == KD - 1)
                m.then_inc(v_full, 1)

    def dve_out(l):
        V.memset(ST[:, 8:9], 0.0).then_inc(sem("mix"), 1)
        V.wait_ge(sem("mix"), nth("DVE", "mix"))
        V.memset(ST[:, 8:9], 0.0).then_inc(sem("arena_free"), 1)
        V.wait_ge(sem("arena_free"), nth("DVE", "arena_free"))
        for i, (t0, n) in enumerate(TILES):
            for hf in range(2):
                V.wait_ge(v_full, v.filled())
                b = v.take()
                x = X[0:n, i, hf * 512:(hf + 1) * 512]
                tt(x, x, b[0:n, :], ALU.add).then_inc(v_free, 1)
                V.wait_ge(v_free, v.emptied())
        V.memset(ST[:, 8:9], 0.0).then_inc(sem("mixed"), 1)
        V.wait_ge(sem("mixed"), nth("DVE", "mixed"))

    def sp_router(l):
        if l:
            nc.sync.wait_ge(sem("router_used"), nth("SP", "router_used"))
        nc.sync.dma_start(WR[:, :, 0:4],
                          A["moe_w_coarse"][l].rearrange("(k p) n -> p k n", p=P)).then_inc(sem("router"), 16)
        nc.sync.dma_start(WR[:, :, 4:36],
                          A["moe_w_fine"][l].rearrange("(k p) n -> p k n", p=P)).then_inc(sem("router"), 16)
        nc.sync.dma_start(BR[:, 0:4], A["moe_b_coarse"][l:l + 1, :].broadcast_to([P, 4])).then_inc(sem("router"), 16)
        nc.sync.dma_start(BR[:, 4:36], A["moe_b_fine"][l:l + 1, :].broadcast_to([P, NE])).then_inc(sem("router"), 16)

    def pe_router():
        PE.wait_ge(sem("router"), nth("PE", "router", 16 * 4))
        PE.wait_ge(v_free, v.room())
        b = v.claim()
        for i, (t0, n) in enumerate(TILES):
            for k in range(KD):
                m = mm(b[0:n, i * 36:(i + 1) * 36], HT[:, k, t0:t0 + n], WR[:, k, :], k == 0, k == KD - 1)
        m.then_inc(v_full, 1)
        PE.wait_ge(sem("assigned"), nth("PE", "assigned"))
        PE.wait_ge(v_free, v.room())
        b = v.claim()
        for i in range(3):
            for j in range(i + 1):
                m = mm(b[:, i * NE:(i + 1) * NE], C("before") if j == i else C("ones"), RTMP[:, 15, j, 0:NE], j == 0, j == i)
        m.then_inc(v_full, 1)
        PE.wait_ge(v_free, v.room())
        b = v.claim()
        for j in range(3):
            m = mm(b[0:1, 0:NE], C("ones")[:, 0:1], RTMP[:, 15, j, 0:NE], j == 0, j == 2)
        m.then_inc(v_full, 1)

    def act_router():
        AC.wait_ge(sem("r_exp_in"), nth("ACT", "r_exp_in"))
        AC.activation(RTMP[:, 2, :, 0:4], RTMP[:, 1, :, 0:4], ACT.Exp).then_inc(sem("r_exp"), 1)
        AC.wait_ge(sem("r_exp"), nth("ACT", "r_exp"))
        AC.wait_ge(sem("r_exp_in"), nth("ACT", "r_exp_in"))
        AC.activation(RTMP[:, 13, :, 0:1], RTMP[:, 12, :, 0:1], ACT.Exp).then_inc(sem("r_exp"), 1)
        AC.wait_ge(sem("r_exp"), nth("ACT", "r_exp"))

    def dve_router():
        T = RTMP
        V.wait_ge(sem("router"), nth("DVE", "router", 16 * 4))
        bc = lambda ap, n: ap.broadcast_to([P, 3, n])
        col = lambda k: T[:, k, :, 0:1]
        V.memset(T[:, :, :, :], 0.0).then_inc(dve_done, 1)
        V.wait_ge(dve_done, nth("DVE", "dve_done"))
        V.wait_ge(v_full, v.filled())
        b = v.take()
        tt(T[:, 0, 0:2, :], b[:, 0:72].rearrange("p (i n) -> p i n", i=2), BR[:, :].unsqueeze(1).broadcast_to([P, 2, 36]), ALU.add).then_inc(dve_done, 1)
        V.wait_ge(dve_done, nth("DVE", "dve_done"))
        tt(T[0:NB, 0, 2, :], b[0:NB, 72:108], BR[0:NB, :], ALU.add).then_inc(v_free, 1)
        V.wait_ge(v_free, v.emptied())
        lg, lf = T[:, 0, :, 0:4], T[:, 0, :, 4:36]
        V.tensor_reduce(T[:, 3, :, 0], lg, AX_X, ALU.max).then_inc(dve_done, 1)
        V.wait_ge(dve_done, nth("DVE", "dve_done"))
        tt(T[:, 1, :, 0:4], lg, bc(col(3), 4), ALU.subtract).then_inc(dve_done, 1)
        V.wait_ge(dve_done, nth("DVE", "dve_done"))
        tt(T[:, 4, :, 0:4], lg, bc(col(3), 4), ALU.is_ge).then_inc(sem("r_exp_in"), 1)
        V.wait_ge(sem("r_exp_in"), nth("DVE", "r_exp_in"))
        go = C("gorder").unsqueeze(1).broadcast_to([P, 3, 4])
        tt(T[:, 4, :, 0:4], T[:, 4, :, 0:4], go, ALU.mult).then_inc(dve_done, 1)
        V.wait_ge(dve_done, nth("DVE", "dve_done"))
        V.tensor_reduce(T[:, 5, :, 0], T[:, 4, :, 0:4], AX_X, ALU.max).then_inc(dve_done, 1)
        V.wait_ge(dve_done, nth("DVE", "dve_done"))
        tt(T[:, 4, :, 0:4], go, bc(col(5), 4), ALU.is_equal).then_inc(dve_done, 1)
        V.wait_ge(dve_done, nth("DVE", "dve_done"))
        V.wait_ge(sem("r_exp"), nth("DVE", "r_exp"))
        V.tensor_reduce(T[:, 6, :, 0], T[:, 2, :, 0:4], AX_X, ALU.add).then_inc(dve_done, 1)
        V.wait_ge(dve_done, nth("DVE", "dve_done"))
        V.reciprocal(col(6), col(6)).then_inc(dve_done, 1)
        V.wait_ge(dve_done, nth("DVE", "dve_done"))
        for i in range(3):
            g4 = T[:, 4, i, 0:4].unsqueeze(2).broadcast_to([P, 4, 8])
            f4 = T[:, 0, i, 4:36].rearrange("p (g e) -> p g e", g=4)
            o4 = T[:, 7, i, 0:32].rearrange("p (g e) -> p g e", g=4)
            q4 = T[:, 8, i, 0:32].rearrange("p (g e) -> p g e", g=4)
            tt(o4, f4, g4, ALU.mult).then_inc(dve_done, 1)
            V.wait_ge(dve_done, nth("DVE", "dve_done"))
            ts(q4, g4, -1.0, -NEG, ALU.add, ALU.mult).then_inc(dve_done, 1)
            V.wait_ge(dve_done, nth("DVE", "dve_done"))
            tt(o4, o4, q4, ALU.add).then_inc(dve_done, 1)
            V.wait_ge(dve_done, nth("DVE", "dve_done"))
        lf = T[:, 7, :, 0:32]
        order = C("order").unsqueeze(1).broadcast_to([P, 3, NE])
        for k, (hot, val) in enumerate(((9, 3), (10, 5))):
            V.tensor_reduce(T[:, val, :, 0], lf, AX_X, ALU.max).then_inc(dve_done, 1)
            V.wait_ge(dve_done, nth("DVE", "dve_done"))
            tt(T[:, 8, :, 0:32], lf, bc(col(val), NE), ALU.is_ge).then_inc(dve_done, 1)
            V.wait_ge(dve_done, nth("DVE", "dve_done"))
            tt(T[:, 8, :, 0:32], T[:, 8, :, 0:32], order, ALU.mult).then_inc(dve_done, 1)
            V.wait_ge(dve_done, nth("DVE", "dve_done"))
            V.tensor_reduce(T[:, 11, :, 0], T[:, 8, :, 0:32], AX_X, ALU.max).then_inc(dve_done, 1)
            V.wait_ge(dve_done, nth("DVE", "dve_done"))
            tt(T[:, hot, :, 0:32], order, bc(col(11), NE), ALU.is_equal).then_inc(dve_done, 1)
            V.wait_ge(dve_done, nth("DVE", "dve_done"))
            if k == 0:
                ts(T[:, 8, :, 0:32], T[:, hot, :, 0:32], 2 * NEG, None, ALU.mult).then_inc(dve_done, 1)
                V.wait_ge(dve_done, nth("DVE", "dve_done"))
                tt(lf, lf, T[:, 8, :, 0:32], ALU.add).then_inc(dve_done, 1)
                V.wait_ge(dve_done, nth("DVE", "dve_done"))
        tt(col(12), col(5), col(3), ALU.subtract).then_inc(sem("r_exp_in"), 1)
        V.wait_ge(sem("r_exp_in"), nth("DVE", "r_exp_in"))
        V.wait_ge(sem("r_exp"), nth("DVE", "r_exp"))
        ts(T[:, 14, :, 0:1], col(13), 1.0, None, ALU.add).then_inc(dve_done, 1)
        V.wait_ge(dve_done, nth("DVE", "dve_done"))
        V.reciprocal(col(14), col(14)).then_inc(dve_done, 1)
        V.wait_ge(dve_done, nth("DVE", "dve_done"))
        tt(col(14), col(14), col(6), ALU.mult).then_inc(dve_done, 1)
        V.wait_ge(dve_done, nth("DVE", "dve_done"))
        tt(col(13), col(13), col(14), ALU.mult).then_inc(dve_done, 1)
        V.wait_ge(dve_done, nth("DVE", "dve_done"))
        real = C("real").unsqueeze(2).broadcast_to([P, 3, NE])
        tt(T[:, 9, :, 0:32], T[:, 9, :, 0:32], real, ALU.mult).then_inc(dve_done, 1)
        V.wait_ge(dve_done, nth("DVE", "dve_done"))
        tt(T[:, 10, :, 0:32], T[:, 10, :, 0:32], real, ALU.mult).then_inc(dve_done, 1)
        V.wait_ge(dve_done, nth("DVE", "dve_done"))
        tt(T[:, 15, :, 0:32], T[:, 9, :, 0:32], T[:, 10, :, 0:32], ALU.add).then_inc(dve_done, 1)
        V.wait_ge(dve_done, nth("DVE", "dve_done"))
        V.memset(ST[:, 8:9], 0.0).then_inc(sem("assigned"), 1)
        V.wait_ge(sem("assigned"), nth("DVE", "assigned"))
        tt(T[:, 9, :, 0:32], T[:, 9, :, 0:32], bc(col(14), NE), ALU.mult).then_inc(dve_done, 1)
        V.wait_ge(dve_done, nth("DVE", "dve_done"))
        tt(T[:, 10, :, 0:32], T[:, 10, :, 0:32], bc(col(13), NE), ALU.mult).then_inc(dve_done, 1)
        V.wait_ge(dve_done, nth("DVE", "dve_done"))
        tt(RW[:, :, :], T[:, 9, :, 0:32], T[:, 10, :, 0:32], ALU.add).then_inc(dve_done, 1)
        V.wait_ge(dve_done, nth("DVE", "dve_done"))
        V.wait_ge(v_full, v.filled())
        b = v.take()
        stt(RT[:, :, :], b[:, 0:96].rearrange("p (i n) -> p i n", i=3), 1.0, T[:, 15, :, 0:32], ALU.add, ALU.mult).then_inc(v_free, 1)
        V.wait_ge(v_free, v.emptied())
        ts(RT[:, :, :], RT[:, :, :], -1.0, None, ALU.add).then_inc(dve_done, 1)
        V.wait_ge(dve_done, nth("DVE", "dve_done"))
        V.wait_ge(v_full, v.filled())
        b = v.take()
        V.tensor_reduce(T[0:1, 8, 0, 0:1], b[0:1, 0:NE], AX_X, ALU.max).then_inc(dve_done, 1)
        V.wait_ge(dve_done, nth("DVE", "dve_done"))
        V.tensor_copy(T[0:1, 8, 1, 0:1], b[0:1, 0:1]).then_inc(v_free, 1)
        V.wait_ge(v_free, v.emptied())
        V.tensor_copy(CNT[0:1, 0:1], T[0:1, 8, 0, 0:1]).then_inc(dve_done, 1)
        V.wait_ge(dve_done, nth("DVE", "dve_done"))
        V.memset(ST[:, 8:9], 0.0).then_inc(sem("counted"), 1)
        V.wait_ge(sem("counted"), nth("DVE", "counted"))
        V.memset(ST[:, 8:9], 0.0).then_inc(sem("router_used"), 1)
        V.wait_ge(sem("router_used"), nth("DVE", "router_used"))

    def sp_step(l, it, g):
        wg = A["moe_w_gate"][l].rearrange("(q e) (k p) f -> q k p e f", e=GE, p=P)
        wu = A["moe_w_up"][l].rearrange("(q e) (k p) f -> q k p e f", e=GE, p=P)
        wd = A["moe_w_down"][l].rearrange("(q e) (k p) d -> q k p e d", e=GE, p=P)
        for u in range(UNITS):
            s = u % RING
            n, i = it
            if n or u >= RING:
                nc.sync.wait_ge(w_used, i * UNITS + (n * UNITS + u - RING + 1))
            dst = RINGW[:, s, :]
            if u < 8:
                d4 = dst.rearrange("p (z e f) -> p z e f", z=2, e=GE)
                for z, w in enumerate((wg, wu)):
                    nc.sync.dma_start(d4[:, z, :, :], w[bass.ds(g, 1), u].rearrange("q p e f -> (q p) e f")).then_inc(
                        w_in_ring[s], 16)
            else:
                d3 = dst.rearrange("p (e d) -> p e d", e=GE)
                for z in range(2):
                    nc.sync.dma_start(d3[:, 2 * z:2 * z + 2, :],
                                      wd[bass.ds(g, 1), u - 8, :, 2 * z:2 * z + 2].rearrange("q p e d -> (q p) e d")).then_inc(
                        w_in_ring[s], 16)

    def pe_step(it):
        PE.wait_ge(sem("sel"), it + 1)
        for q in range(4):
            PE.wait_ge(v_free, v.room())
            b = v.claim()
            for c in range(2):
                for i, (t0, n) in enumerate(TILES):
                    m = mm(b[:, c * P:(c + 1) * P], XN[0:n, i, (2 * q + c) * P:(2 * q + c + 1) * P], SELT[0:n, i, :], i == 0, i == 2)
            m.then_inc(v_full, 1)
        PE.wait_ge(v_free, v.all_free())
        PE.wait_ge(a_free, a.room())
        gate = a.claim()
        PE.wait_ge(v_free, v.room())
        up = v.claim()
        for u in range(8):
            PE.wait_ge(w_in_ring[u % RING], 32 * (2 * it + u // RING + 1))
            w = RINGW[:, u % RING, :].rearrange("p (z e f) -> p z e f", z=2, e=GE)
            for z, out in enumerate((gate, up)):
                for e in range(GE):
                    m = mm(out[e * SLOT:(e + 1) * SLOT, :], HG_T[:, u, e * SLOT:(e + 1) * SLOT], w[:, z, e, :], u == 0, u == 7)
                if u == 7 and z == 0:
                    m.then_inc(a_full, 1)
            if u < 7:
                m.then_inc(w_used, 1)
        m.then_inc(v_full, 1)
        PE.wait_ge(v_free, v.all_free())
        PE.wait_ge(v_free, v.room())
        b = v.claim()
        for f in range(4):
            m = tr(b[:, f * P:(f + 1) * P], AV[:, f * P:(f + 1) * P])
            if f == 0:
                m.then_inc(w_used, 1)
        m.then_inc(v_full, 1)
        PE.wait_ge(v_free, v.all_free())
        outs = []
        for _ in range(2):
            PE.wait_ge(a_free, a.room())
            outs.append(a.claim())
        for f in range(4):
            u = 8 + f
            PE.wait_ge(w_in_ring[u % RING], 32 * (2 * it + u // RING + 1))
            w = RINGW[:, u % RING, :].rearrange("p (e d) -> p e d", e=GE)
            for hf in range(2):
                for e in range(GE):
                    m = mm(outs[hf][e * SLOT:(e + 1) * SLOT, :], AVT[:, f, e * SLOT:(e + 1) * SLOT],
                           w[:, e, hf * 512:(hf + 1) * 512], f == 0, f == 3)
                if f == 3:
                    m.then_inc(a_full, 1)
            if f < 3:
                m.then_inc(w_used, 1)
        PE.wait_ge(a_free, a.room())
        b = a.claim()
        for i, (t0, n) in enumerate(TILES):
            m = tr(b[:, t0:t0 + n], SELW[0:n, i, :])
            if i == 0:
                m.then_inc(w_used, 1)
        m.then_inc(a_full, 1)
        PE.wait_ge(a_free, a.all_free())
        for i, (t0, n) in enumerate(TILES):
            for hf in range(2):
                PE.wait_ge(v_free, v.room())
                b = v.claim()
                m = mm(b[0:n, :], SWT[:, t0:t0 + n], OUT4[:, hf * 512:(hf + 1) * 512])
                m.then_inc(v_full, 1)

    def act_step(it):
        AC.wait_ge(a_full, a.filled())
        b = a.take()
        AC.activation(SG[:, :], b[:, :], ACT.Silu).then_inc(sem("silu"), 1)
        AC.wait_ge(sem("silu"), nth("ACT", "silu"))
        AC.copy(ST[:, 30:31], ST[:, 31:32]).then_inc(a_free, 1)
        AC.wait_ge(a_free, a.emptied())
        for hf in range(2):
            AC.wait_ge(a_full, a.filled())
            b = a.take()
            AC.copy(OUT4[:, hf * 512:(hf + 1) * 512], b[:, :]).then_inc(a_free, 1)
            AC.wait_ge(a_free, a.emptied())
        AC.wait_ge(a_full, a.filled())
        b = a.take()
        AC.copy(SWT[:, :], b[:, 0:NT]).then_inc(a_free, 1)
        AC.wait_ge(a_free, a.emptied())

    def dve_step(it, g, r, gain):
        rt = RT[:, :, bass.ds(g * GE, GE)].unsqueeze(3).broadcast_to([P, 3, GE, SLOT])
        rw = RW[:, :, bass.ds(g * GE, GE)].unsqueeze(3).broadcast_to([P, 3, GE, SLOT])
        o = at["slotno"][0]
        slot = CONST[:, bass.ds(r * SLOT + o, SLOT)].unsqueeze(1).unsqueeze(1).broadcast_to([P, 3, GE, SLOT]) \
            if not isinstance(r, int) else CONST[:, o + r * SLOT:o + (r + 1) * SLOT].unsqueeze(1).unsqueeze(1).broadcast_to([P, 3, GE, SLOT])
        st = SELT[:, :, :].rearrange("p i (e s) -> p i e s", e=GE)
        sw = SELW[:, :, :].rearrange("p i (e s) -> p i e s", e=GE)
        for i in range(3):
            tt(st[:, i], rt[:, i], slot[:, i], ALU.is_equal).then_inc(dve_done, 1)
            V.wait_ge(dve_done, nth("DVE", "dve_done"))
            ins = tt(sw[:, i], st[:, i], rw[:, i], ALU.mult)
            if i < 2:
                ins.then_inc(dve_done, 1)
                V.wait_ge(dve_done, nth("DVE", "dve_done"))
            else:
                ins.then_inc(sem("sel"), 1)
                V.wait_ge(sem("sel"), nth("DVE", "sel"))
        for q in range(4):
            V.wait_ge(v_full, v.filled())
            b = v.take()
            gc = PAR[:, gain + 2 * q:gain + 2 * q + 2].unsqueeze(2).broadcast_to([P, 2, P])
            tt(HG_T[:, 2 * q:2 * q + 2, :], b[:, 0:256].rearrange("p (c s) -> p c s", c=2), gc, ALU.mult).then_inc(v_free, 1)
            V.wait_ge(v_free, v.emptied())
        V.wait_ge(v_full, v.filled())
        b = v.take()
        V.wait_ge(sem("silu"), nth("DVE", "silu"))
        tt(AV[:, :], SG[:, :], b[:, :], ALU.mult).then_inc(v_free, 1)
        V.wait_ge(v_free, v.emptied())
        V.wait_ge(v_full, v.filled())
        b = v.take()
        V.tensor_copy(AVT[:, :, :].rearrange("p f s -> p (f s)"), b[:, :]).then_inc(v_free, 1)
        V.wait_ge(v_free, v.emptied())
        for i, (t0, n) in enumerate(TILES):
            for hf in range(2):
                V.wait_ge(v_full, v.filled())
                b = v.take()
                x = X[0:n, i, hf * 512:(hf + 1) * 512]
                tt(x, x, b[0:n, :], ALU.add).then_inc(v_free, 1)
                V.wait_ge(v_free, v.emptied())


    def counts(who):
        if who == "PE":
            return [(v.claimed, 12), (a.claimed, 4)]
        if who == "ACT":
            return [(a.taken, 4), (count("ACT", "silu"), 1)]
        if who == "DVE":
            return [(v.taken, 12), (count("DVE", "dve_done"), 5), (count("DVE", "sel"), 1),
                    (count("DVE", "silu"), 1)]
        return []

    def increments(who):
        if who == "PE":
            return [(v_full, 12), (a_full, 4), (w_used, UNITS)]
        if who == "ACT":
            return [(a_free, 4), (sem("silu"), 1)]
        if who == "DVE":
            return [(v_free, 12), (dve_done, 5), (sem("sel"), 1)]
        return [(w_in_ring[s], 32 * UNITS // RING) for s in range(RING)]

    def moe(who, l):
        n0 = l * NGRP * (1 + OVER)
        eng = NM[who]
        gain = FFNG + 8 * l

        def step(n, i, g, r):
            if who == "SP":
                sp_step(l, (n, i), g)
            elif who == "PE":
                pe_step(i + n)
            elif who == "ACT":
                act_step(None)
            else:
                dve_step(None, g, r, gain)

        if who == "SP":
            nc.sync.wait_ge(sem("arena_free"), nth("SP", "arena_free"))
            if l == 0:
                sp_step(l, (0, 0), 0)
                with eng.Fori(0, NGRP - 1) as i:
                    step(1, i, i + 1, 0)
        if who != "SP" or l:
            with eng.Fori(0, NGRP) as i:
                for c, per in counts(who):
                    c.loop(i, per)
                step(n0, i, i, 0)
            for c, per in counts(who):
                c.end(NGRP)
        eng.wait_ge(sem("counted"), l + 1)
        most = eng.value_load(CNT[0:1, 0:1], min_val=0, max_val=NT)
        with eng.Fori(0, OVER) as r:
            with eng.If(most > r * SLOT + SLOT):
                with eng.Fori(0, NGRP) as g:
                    i = r * NGRP + g
                    for c, per in counts(who):
                        c.loop(i, per)
                    step(n0 + NGRP, i, g, r + 1)
            with eng.Else():
                if who == "SP":
                    eng.wait_ge(w_used, r * (UNITS * NGRP) + (n0 + NGRP) * UNITS)
                if who == "PE":
                    eng.wait_ge(v_free, r * (12 * NGRP) + v.claimed.n + 4)
                    eng.wait_ge(a_free, r * (4 * NGRP) + a.claimed.n + 4)
                for s, n in increments(who):
                    eng.sem_inc(s, n * NGRP)
        for c, per in counts(who):
            c.end(OVER * NGRP)

    NC = 6
    E_HALF = float(np.exp(-0.5))
    NCK = SEQ // CH
    PR, PK, PV_, PWA, PG = slice(0, 6), slice(6, 12), slice(12, 18), 18, 19
    SQ_B = place("SQ_B", 90112, [2, NT])
    RS_B = place("RS_B", 92224, [2, NT])
    SHF = place("SHF", 0, [SHIFT_W])
    SSH = place("SSH", 12672, [SHIFT_W])
    PREVS = place("PREVS", 25344, [NCH, NB])
    DIF = place("DIF", 25984, [NCH, NT])
    AQ, QL, BT, KL = (place(n, 6336 * i, [NC, NT]) for i, n in enumerate(("AQ", "QL", "BT", "KL")))
    BTOK, KTOK, VTOK = (place(n, 25344 + 6144 * i, [2, QA]) for i, n in enumerate(("BTOK", "KTOK", "VTOK")))
    GG = place("GG", 43776, [NC, NT])
    AA = place("AA", 50112, [NC, NT])
    KN = place("KN", 56448, [NC, NT])
    LWP = place("LWP", 62784, [NC, SEQ])
    CC = place("CC", 68928, [NC, SEQ])
    EX = place("EX", 75072, [NC, SEQ])
    SCM = place("SCM", 81216, [NC, SEQ])
    T1 = place("T1", 81216, [NC, NT])
    LWS = place("LWS", 87584, [NC, NB])
    LAMC = place("LAMC", 87776, [NC, NCK])
    WUP = place("WUP", 93120, [QA])
    GUP = place("GUP", 96192, [QA])
    MATS = [place(f"MAT{i}", 50112 + 3072 * i, [H, CH]) for i in range(14)]
    VRAW = [place("VRAW", 16384 + 3072 * q, [QA], base=U1) for q in range(5)] + [place("VRAW", 90048, [QA])]
    YT = place("YT", 0, [NC, NT], base=XNoff + 12288)
    STT = place("STT", 6336, [NC, CH], base=XNoff + 12288)
    LAMK = place("LAMK", 6336 + 1536, [NC, NCK], base=XNoff + 12288)
    SST = place("SST", 0, [DH, DH], base=U1)
    STMP = place("STMP", 16384, [DH, DH], base=U1)
    VEC = place("VEC", 10496, [6, DH], base=XNoff)
    SAV = place("SAV", 10496 + 1536, [DH], base=XNoff)
    YS = place("YS", 0, [QA], base=U1)
    SOUT = place("SOUT", 4096, [H, DH], base=U1)

    def sp_layer_b():
        nc.sync.wait_ge(sem("moe_done"), nth("SP", "moe_done"))
        w = A["w_in_b"][0].rearrange("(k p) n -> p k n", p=P)
        for k in range(KD):
            nc.sync.dma_start(WIN_B[:, k, :], w[:, k, :]).then_inc(sem("w_in"), 16)
        sp_router(1)
        sp_memattn(1)
        nc.sync.wait_ge(sem("mem_done"), nth("SP", "mem_done"))
        nc.sync.dma_start(SSH[0:NB, :], A["state_shift"][0]).then_inc(sem("b_w"), 16)
        nc.sync.dma_start(WUP[0:64, :], A["rwkv_w_up"][0]).then_inc(sem("b_w"), 16)
        nc.sync.dma_start(WUP[64:P, :], A["rwkv_a_up"][0]).then_inc(sem("b_w"), 16)
        nc.sync.dma_start(GUP[:, :], A["rwkv_g_up"][0]).then_inc(sem("b_w"), 16)
        nc.sync.wait_ge(sem("u1_used"), nth("SP", "u1_used"))
        nc.sync.dma_start(SST[0:RS, :, :],
                          A["state_rwkv"][0].rearrange("b h v k -> (b h) v k")).then_inc(sem("s_state"), 16)

        nc.sync.wait_ge(sem("u1_ys"), nth("SP", "u1_ys"))
        nc.sync.dma_start(WO[:, :, :], A["w_out"][1].rearrange("(k p) n -> p k n", p=P)).then_inc(sem("w_out"), 16)

    def pool_layer_b():
        nc.gpsimd.wait_ge(sem("mixed"), nth("POOL", "mixed"))
        load_mem(nc.gpsimd, 1)
        pool_mem(1)
        nc.gpsimd.wait_ge(sem("shf"), nth("POOL", "shf"))
        nc.gpsimd.dma_start(O["p_shift"][0], SHF[0:1, :]).then_inc(sem("shf_stored"), 16)
        nc.gpsimd.dma_start(O["s_shift"][0], SHF[1:9, :]).then_inc(sem("shf_stored"), 16)
        nc.gpsimd.wait_ge(sem("vraw"), nth("POOL", "vraw"))
        for q in range(6):
            for s in range(NB):
                nc.gpsimd.dma_start(VEC[s * H:(s + 1) * H, q, :],
                                    VRAW[q][s:s + 1, :].rearrange("b (h d) -> b h d", h=H)).then_inc(sem("vecs"), 16)
        pool_sample_step()
        nc.gpsimd.wait_ge(sem("s_stored"), nth("POOL", "s_stored", 16))
        for s in range(NB):
            nc.gpsimd.dma_start(YS[s:s + 1, :].rearrange("b (h d) -> b h d", h=H),
                                SAV[s * H:(s + 1) * H, :]).then_inc(sem("y_rows8"), 16)
        nc.gpsimd.wait_ge(sem("sout"), nth("POOL", "sout"))
        nc.gpsimd.dma_start(O["p_rwkv"][0, 0].rearrange("h v k -> v h k"),
                            SOUT[0:DH, :, :]).then_inc(sem("sout_stored"), 16)

    def pe_layer_b():
        pe_norm()
        pe_mem(1)
        PE.wait_ge(sem("w_in"), nth("PE", "w_in", 16 * KD))
        pe_channels(WIN_B, [P * c for c in range(22)], None)
        pe_headnorm(SQ_B, 2)
        pe_memattn(1)
        pe_rwkv()

    def act_layer_b():
        act_norm()
        act_mem(1)
        act_headnorm(RS_B)
        act_memattn(1)
        act_rwkv()

    def dve_layer_b():
        dve_norm(MIXG + 8)
        dve_mem(1)
        for c in range(22):
            V.wait_ge(v_full, v.filled())
            b = v.take()
            V.tensor_copy(PRT[:, c, :] if c < NCH else QT[:, c - NCH, :], b[:, 0:NT]).then_inc(v_free, 1)
            V.wait_ge(v_free, v.emptied())
        dve_headnorm(QT[:, 0:2, :], SQ_B, RS_B, 2, [MQG + 1] * 2)
        dve_memattn(1)
        V.memset(ST[:, 8:9], 0.0).then_inc(sem("mem_done"), 1)
        V.wait_ge(sem("mem_done"), nth("DVE", "mem_done"))
        dve_rwkv()

    COLS = ((0, 4), (4, 6))

    def pe_rwkv():
        PE.wait_ge(sem("mem_done"), nth("PE", "mem_done"))
        for q in range(5):
            PE.wait_ge(v_free, v.room())
            b = v.claim()
            for c in range(4):
                m = tr(b[0:9, c * P:(c + 1) * P], PRT[:, 4 * q + c, SEQ - 1:NT])
            m.then_inc(v_full, 1)
        PE.wait_ge(sem("b_w"), nth("PE", "b_w", 16 * 4))
        PE.wait_ge(v_free, v.room())
        b = v.claim()
        for c in range(NCH):
            m = tr(b[:, c * NB:(c + 1) * NB], SSH[0:NB, c * P:(c + 1) * P])
        m.then_inc(v_full, 1)
        PE.wait_ge(sem("gates_b"), nth("PE", "gates_b"))
        for c in range(NC):
            PE.wait_ge(a_free, a.room())
            b = a.claim()
            mm(b[:, 0:NT], WUP[0:64, c * P:(c + 1) * P], PRT[0:64, PWA, :]).then_inc(a_full, 1)
        for c in range(NC):
            PE.wait_ge(a_free, a.room())
            b = a.claim()
            mm(b[:, 0:NT], WUP[64:P, c * P:(c + 1) * P], PRT[64:P, PWA, :]).then_inc(a_full, 1)
        for c in range(NC):
            PE.wait_ge(v_free, v.room())
            b = v.claim()
            mm(b[:, 0:NT], GUP[:, c * P:(c + 1) * P], PRT[:, PG, :]).then_inc(v_full, 1)
        pe_headnorm(T1, NC)
        PE.wait_ge(sem("scaled"), nth("PE", "scaled"))
        for src in (lambda c: BT[:, c, :], lambda c: KL[:, c, :], lambda c: PRT[:, 12 + c, :]):
            for j in range(2):
                for c0, c1 in COLS:
                    PE.wait_ge(v_free, v.room())
                    b = v.claim()
                    for c in range(c0, c1):
                        m = tr(b[:, (c - c0) * P:(c - c0 + 1) * P], src(c)[:, j * P:(j + 1) * P])
                    m.then_inc(v_full, 1)
        for src in sample_vectors():
            for c0, c1 in COLS:
                PE.wait_ge(v_free, v.room())
                b = v.claim()
                for c in range(c0, c1):
                    m = tr(b[0:NB, (c - c0) * P:(c - c0 + 1) * P], src(c))
                m.then_inc(v_full, 1)
        PE.wait_ge(v_free, v.all_free())
        PE.wait_ge(sem("state0"), nth("PE", "state0"))
        for j in range(2):
            pe_inverse(j)
            for c in range(2 * j, 2 * j + 2):
                pe_chunk(j, c)
        PE.wait_ge(sem("state"), nth("PE", "state"))
        for c0, c1 in COLS:
            PE.wait_ge(v_free, v.room())
            b = v.claim()
            for c in range(c0, c1):
                m = tr(b[0:DH, (c - c0) * P:(c - c0 + 1) * P], STT[:, c, :])
            m.then_inc(v_full, 1)
        PE.wait_ge(sem("y_rows8"), 16 * NB)
        PE.wait_ge(v_free, v.room())
        b = v.claim()
        for c in range(NC):
            m = tr(b[:, c * NB:(c + 1) * NB], YS[0:NB, c * P:(c + 1) * P])
        m.then_inc(v_full, 1)
        for _ in range(3):
            PE.wait_ge(sem("sq"), nth("PE", "sq"))
            for c in range(NC):
                PE.wait_ge(v_free, v.room())
                b = v.claim()
                mm(b[:, 0:NT], C("headones"), (T1)[:, c, :]).then_inc(v_full, 1)

    def sample_vectors():
        return (lambda c: LWS[:, c, :], lambda c: PRT[:, 6 + c, SEQ:NT], lambda c: PRT[:, 12 + c, SEQ:NT],
                lambda c: KN[:, c, SEQ:NT], lambda c: AA[:, c, SEQ:NT], lambda c: PRT[:, c, SEQ:NT])

    def pe_pairs(f):
        for odd in range(2):
            PE.wait_ge(v_free, v.room())
            b = v.claim()
            for q in range(NC):
                for cp in range(2):
                    l, r = f(2 * q + odd, cp)
                    m = mm(b[64 * cp:64 * cp + 64, q * CH:(q + 1) * CH], l, r)
            m.then_inc(v_full, 1)

    def pe_square(l, r):
        for q in range(2):
            PE.wait_ge(v_free, v.room())
            b = v.claim()
            for h in range(6 * q, 6 * q + 6):
                for cp in range(2):
                    o = slice(64 * cp, 64 * cp + 64)
                    m = mm(b[o, (h % 6) * CH:(h % 6 + 1) * CH], l[o, h, :], r[o, h, :])
            m.then_inc(v_full, 1)

    P0, Q0, P1, Q1, TI, TT_, LO32, LO64, ZZ, LKT, QBT, QKT, SAM, X1M = MATS

    def pe_inverse(j):
        def at_(x, h, cp):
            o = 64 * (h % 2)
            return x[o:o + DH, h // 2, j * P + cp * CH:j * P + (cp + 1) * CH]
        for l, r in ((AQ, BT), (BT, AQ), (KL, AQ), (BT, QL), (KL, QL)):
            pe_pairs(lambda h, cp: (at_(l, h, cp), at_(r, h, cp)))
        PE.wait_ge(v_free, v.all_free())
        p, q, p2, q2 = P0, Q0, P1, Q1
        for k in range(3):
            if k < 2:
                pe_square(q, p)
            pe_square(p, q)
            PE.wait_ge(v_free, v.all_free())
            p, q, p2, q2 = p2, q2, p, q
            pe_square(q, TI)
            PE.wait_ge(v_free, v.all_free())
        for qq in range(2):
            PE.wait_ge(v_free, v.room())
            b = v.claim()
            for h in range(6 * qq, 6 * qq + 6):
                for cp in range(2):
                    o = slice(64 * cp, 64 * cp + 64)
                    m = mm(b[o, (h % 6) * CH:(h % 6 + 1) * CH], TI[o, h, :], C("ident64")[o, :])
            m.then_inc(v_full, 1)
        PE.wait_ge(v_free, v.all_free())
        for lo in (LO32, LO64):
            pe_square(lo, TT_)
            PE.wait_ge(v_free, v.all_free())
            if lo is LO32:
                pe_square(ZZ, TI)
            pe_square(TI, ZZ)
            PE.wait_ge(v_free, v.all_free())

    def pe_chunk(j, c):
        cp = c % 2
        o = slice(64 * cp, 64 * cp + 64)
        t = slice(c * CH, (c + 1) * CH)
        PE.wait_ge(sem("state"), nth("PE", "state"))
        for odd in range(2):
            PE.wait_ge(v_free, v.room())
            b = v.claim()
            hp = slice(64 * odd, 64 * odd + 64)
            for q in range(NC):
                m = mm(b[o, q * CH:(q + 1) * CH], AQ[hp, q, t], STT[hp, q, :])
            m.then_inc(v_full, 1)
        for q in range(2):
            PE.wait_ge(v_free, v.room())
            b = v.claim()
            for h in range(6 * q, 6 * q + 6):
                m = mm(b[o, (h % 6) * CH:(h % 6 + 1) * CH], LKT[o, HX(h), :], VTOK[o, j, h * DH:(h + 1) * DH])
            m.then_inc(v_full, 1)
        PE.wait_ge(v_free, v.all_free())
        for q in range(2):
            PE.wait_ge(v_free, v.room())
            b = v.claim()
            for h in range(6 * q, 6 * q + 6):
                m = mm(b[o, (h % 6) * CH:(h % 6 + 1) * CH], TT_[o, HX(h), :], X1M[o, h, :])
            m.then_inc(v_full, 1)
        PE.wait_ge(v_free, v.room())
        b = v.claim()
        for h in range(H):
            hp = slice(64 * (h % 2), 64 * (h % 2) + 64)
            m = mm(b[hp, h // 2 * CH:(h // 2 + 1) * CH], STT[hp, h // 2, :], QL[hp, h // 2, t])
        m.then_inc(v_full, 1)
        PE.wait_ge(v_free, v.all_free())
        PE.wait_ge(v_free, v.room())
        b = v.claim()
        for h in range(H):
            hp = slice(64 * (h % 2), 64 * (h % 2) + 64)
            out = b[hp, h // 2 * CH:(h // 2 + 1) * CH]
            mm(out, SAM[o, h, :], QBT[o, HX(h), :], True, False)
            m = mm(out, VTOK[o, j, h * DH:(h + 1) * DH], QKT[o, HX(h), :], False, True)
        m.then_inc(v_full, 1)
        PE.wait_ge(v_free, v.room())
        b = v.claim()
        for h in range(H):
            hp = slice(64 * (h % 2), 64 * (h % 2) + 64)
            out = b[hp, h // 2 * CH:(h // 2 + 1) * CH]
            hd = slice(h * DH, (h + 1) * DH)
            mm(out, BTOK[o, j, hd], SAM[o, h, :], True, False)
            m = mm(out, KTOK[o, j, hd], VTOK[o, j, hd], False, True)
        m.then_inc(v_full, 1)

    def HX(h):
        return (h % 2) * 6 + h // 2

    def act_rwkv():
        AC.wait_ge(sem("mixed_x"), nth("ACT", "mixed_x"))
        AC.activation(PRT[0:64, PWA, :], PRT[0:64, PWA, :], ACT.Tanh).then_inc(act_done, 1)
        AC.wait_ge(act_done, nth("ACT", "act_done"))
        AC.activation(PRT[:, PG, :], PRT[:, PG, :], ACT.Sigmoid).then_inc(sem("gates_b"), 1)
        AC.wait_ge(sem("gates_b"), nth("ACT", "gates_b"))
        for c in range(NC):
            AC.wait_ge(a_full, a.filled())
            b = a.take()
            AC.activation(LWP[:, c, :], b[:, 0:SEQ], ACT.Sigmoid, bias=PAR[:, W0 + c:W0 + c + 1]).then_inc(act_done, 1)
            AC.wait_ge(act_done, nth("ACT", "act_done"))
            AC.activation(LWS[:, c, :], b[:, SEQ:NT], ACT.Sigmoid, bias=PAR[:, W0 + c:W0 + c + 1]).then_inc(a_free, 1)
            AC.wait_ge(a_free, a.emptied())
        for c in range(NC):
            AC.wait_ge(a_full, a.filled())
            b = a.take()
            AC.activation(AA[:, c, :], b[:, 0:NT], ACT.Sigmoid, bias=PAR[:, A0 + c:A0 + c + 1]).then_inc(a_free, 1)
            AC.wait_ge(a_free, a.emptied())
        AC.copy(ST[:, 30:31], ST[:, 31:32]).then_inc(sem("sigmoids"), 1)
        AC.wait_ge(sem("sigmoids"), nth("ACT", "sigmoids"))
        rsqrt_act(T1[:, :, :])
        AC.wait_ge(sem("cum"), nth("ACT", "cum"))
        AC.activation(EX[:, :, :], CC[:, :, :], ACT.Exp).then_inc(sem("lam"), 1)
        AC.wait_ge(sem("lam"), nth("ACT", "lam"))
        AC.wait_ge(sem("cum"), nth("ACT", "cum"))
        AC.activation(EX[:, :, :], CC[:, :, :], ACT.Exp, scale=-1.0).then_inc(sem("lam"), 1)
        AC.wait_ge(sem("lam"), nth("ACT", "lam"))
        AC.wait_ge(sem("cum"), nth("ACT", "cum"))
        AC.activation(LWS[:, :, :], LWS[:, :, :], ACT.Exp).then_inc(act_done, 1)
        AC.wait_ge(act_done, nth("ACT", "act_done"))
        AC.activation(CC[:, :, :], CC[:, :, :], ACT.Exp).then_inc(sem("lam"), 1)
        AC.wait_ge(sem("lam"), nth("ACT", "lam"))
        rsqrt_act(T1[:, :, :])

    def dve_rwkv():
        for q in range(5):
            V.wait_ge(v_full, v.filled())
            b = v.take()
            V.tensor_copy(SHF[0:9, q * 512:(q + 1) * 512], b[0:9, :]).then_inc(v_free, 1)
            V.wait_ge(v_free, v.emptied())
        V.memset(ST[:, 8:9], 0.0).then_inc(sem("shf"), 1)
        V.wait_ge(sem("shf"), nth("DVE", "shf"))
        V.wait_ge(v_full, v.filled())
        b = v.take()
        V.tensor_copy(PREVS[:, :, :].rearrange("p c b -> p (c b)"), b[:, 0:NCH * NB]).then_inc(v_free, 1)
        V.wait_ge(v_free, v.emptied())
        tt(DIF[:, :, 1:SEQ], PRT[:, :, 0:SEQ - 1], PRT[:, :, 1:SEQ], ALU.subtract).then_inc(dve_done, 1)
        V.wait_ge(dve_done, nth("DVE", "dve_done"))
        ts(DIF[:, :, 0:1], PRT[:, :, 0:1], -1.0, None, ALU.mult).then_inc(dve_done, 1)
        V.wait_ge(dve_done, nth("DVE", "dve_done"))
        tt(DIF[:, :, SEQ:NT], PREVS[:, :, :], PRT[:, :, SEQ:NT], ALU.subtract).then_inc(dve_done, 1)
        V.wait_ge(dve_done, nth("DVE", "dve_done"))
        for c in range(NCH):
            stt(PRT[:, c, :], DIF[:, c, :], PAR[:, MU + c:MU + c + 1], PRT[:, c, :], ALU.mult, ALU.add).then_inc(dve_done, 1)
            V.wait_ge(dve_done, nth("DVE", "dve_done"))
        V.memset(ST[:, 8:9], 0.0).then_inc(sem("mixed_x"), 1)
        V.wait_ge(sem("mixed_x"), nth("DVE", "mixed_x"))
        for c in range(NC):
            V.wait_ge(v_full, v.filled())
            b = v.take()
            V.tensor_copy(GG[:, c, :], b[:, 0:NT]).then_inc(v_free, 1)
            V.wait_ge(v_free, v.emptied())
        for c in range(NC):
            ts(KN[:, c, :], PRT[:, 6 + c, :], PAR[:, KK + c:KK + c + 1], None, ALU.mult).then_inc(dve_done, 1)
            V.wait_ge(dve_done, nth("DVE", "dve_done"))
        tt(T1[:, :, :], KN[:, :, :], KN[:, :, :], ALU.mult).then_inc(sem("sq"), 1)
        V.wait_ge(sem("sq"), nth("DVE", "sq"))
        for c in range(NC):
            V.wait_ge(v_full, v.filled())
            b = v.take()
            V.tensor_copy(T1[:, c, :], b[:, 0:NT]).then_inc(v_free, 1)
            V.wait_ge(v_free, v.emptied())
        rsqrt_dve(T1[:, :, :], 1.0, 1e-24, ALU.max)
        tt(KN[:, :, :], KN[:, :, :], T1[:, :, :], ALU.mult).then_inc(dve_done, 1)
        V.wait_ge(dve_done, nth("DVE", "dve_done"))
        V.wait_ge(sem("sigmoids"), nth("DVE", "sigmoids"))
        ts(ST[:, 56:62], PAR[:, KA:KA + 6], -1.0, 1.0, ALU.mult, ALU.add).then_inc(dve_done, 1)
        V.wait_ge(dve_done, nth("DVE", "dve_done"))
        for c in range(NC):
            ts(T1[:, c, :], AA[:, c, :], PAR[:, KA + c:KA + c + 1], ST[:, 56 + c:57 + c], ALU.mult, ALU.add).then_inc(dve_done, 1)
            V.wait_ge(dve_done, nth("DVE", "dve_done"))
        tt(PRT[:, PK, :], PRT[:, PK, :], T1[:, :, :], ALU.mult).then_inc(dve_done, 1)
        V.wait_ge(dve_done, nth("DVE", "dve_done"))
        tt(AA[:, :, :], AA[:, :, :], KN[:, :, :], ALU.mult).then_inc(dve_done, 1)
        V.wait_ge(dve_done, nth("DVE", "dve_done"))
        ts(LWP[:, :, :], LWP[:, :, :], -E_HALF, None, ALU.mult).then_inc(dve_done, 1)
        V.wait_ge(dve_done, nth("DVE", "dve_done"))
        ts(LWS[:, :, :], LWS[:, :, :], -E_HALF, None, ALU.mult).then_inc(dve_done, 1)
        V.wait_ge(dve_done, nth("DVE", "dve_done"))
        V.memset(SCM[:, :, :], 1.0).then_inc(dve_done, 1)
        V.wait_ge(dve_done, nth("DVE", "dve_done"))
        V.memset(SCM[:, :, 0:SEQ:CH], 0.0).then_inc(dve_done, 1)
        V.wait_ge(dve_done, nth("DVE", "dve_done"))
        flat = lambda x: x[:, :, :].rearrange("p c t -> p (c t)")
        V.tensor_tensor_scan(flat(CC), flat(SCM), flat(LWP), 0.0, ALU.mult, ALU.add).then_inc(sem("cum"), 1)
        V.wait_ge(sem("cum"), nth("DVE", "cum"))
        pr = slice(0, SEQ)
        V.wait_ge(sem("lam"), nth("DVE", "lam"))
        V.wait_ge(sem("shf_stored"), nth("DVE", "shf_stored", 16 * 2))
        V.tensor_copy(LAMK[:, :, :], EX[:, :, CH - 1:SEQ:CH]).then_inc(dve_done, 1)
        V.wait_ge(dve_done, nth("DVE", "dve_done"))
        tt(QL[:, :, pr], PRT[:, PR, pr], EX[:, :, :], ALU.mult).then_inc(sem("cum"), 1)
        V.wait_ge(sem("cum"), nth("DVE", "cum"))
        V.wait_ge(sem("lam"), nth("DVE", "lam"))
        tt(BT[:, :, pr], AA[:, :, pr], EX[:, :, :], ALU.mult).then_inc(dve_done, 1)
        V.wait_ge(dve_done, nth("DVE", "dve_done"))
        tt(KL[:, :, pr], PRT[:, PK, pr], EX[:, :, :], ALU.mult).then_inc(dve_done, 1)
        V.wait_ge(dve_done, nth("DVE", "dve_done"))
        tt(CC[:, :, :], CC[:, :, :], LWP[:, :, :], ALU.subtract).then_inc(sem("cum"), 1)
        V.wait_ge(sem("cum"), nth("DVE", "cum"))
        V.wait_ge(sem("lam"), nth("DVE", "lam"))
        tt(AQ[:, :, pr], KN[:, :, pr], CC[:, :, :], ALU.mult).then_inc(dve_done, 1)
        V.wait_ge(dve_done, nth("DVE", "dve_done"))
        V.memset(ST[:, 8:9], 0.0).then_inc(sem("scaled"), 1)
        V.wait_ge(sem("scaled"), nth("DVE", "scaled"))
        for tok in (BTOK, KTOK, VTOK):
            for j in range(2):
                for c0, c1 in COLS:
                    V.wait_ge(v_full, v.filled())
                    b = v.take()
                    V.tensor_copy(tok[:, j, c0 * P:c1 * P], b[:, 0:(c1 - c0) * P]).then_inc(v_free, 1)
                    V.wait_ge(v_free, v.emptied())
        for q in range(6):
            for c0, c1 in COLS:
                V.wait_ge(v_full, v.filled())
                b = v.take()
                V.tensor_copy(VRAW[q][0:NB, c0 * P:c1 * P], b[0:NB, 0:(c1 - c0) * P]).then_inc(v_free, 1)
                V.wait_ge(v_free, v.emptied())
        V.memset(ST[:, 8:9], 0.0).then_inc(sem("vraw"), 1)
        V.wait_ge(sem("vraw"), nth("DVE", "vraw"))
        V.memset(STT[:, :, :], 0.0).then_inc(dve_done, 1)
        V.wait_ge(dve_done, nth("DVE", "dve_done"))
        V.memset(ST[:, 8:9], 0.0).then_inc(sem("state0"), 1)
        V.wait_ge(sem("state0"), nth("DVE", "state0"))
        for j in range(2):
            dve_inverse(j)
            if j == 0:
                V.wait_ge(sem("vecs"), 16 * 6 * NB)
            for c in range(2 * j, 2 * j + 2):
                dve_chunk(j, c)
        for c0, c1 in COLS:
            V.wait_ge(v_full, v.filled())
            b = v.take()
            if c0 == 0:
                V.wait_ge(sem("y_rows8"), 16 * NB)
            V.tensor_copy(SOUT[0:DH, 2 * c0:2 * c1, :].rearrange("p h k -> p (h k)"), b[0:DH, 0:(c1 - c0) * P]).then_inc(v_free, 1)
            V.wait_ge(v_free, v.emptied())
        V.wait_ge(v_full, v.filled())
        b = v.take()
        V.tensor_copy(YT[:, :, SEQ:NT], b[:, 0:NC * NB].rearrange("p (c b) -> p c b", b=NB)).then_inc(v_free, 1)
        V.wait_ge(v_free, v.emptied())
        V.memset(ST[:, 8:9], 0.0).then_inc(sem("sout"), 1)
        V.wait_ge(sem("sout"), nth("DVE", "sout"))
        V.tensor_copy(T1[:, :, :], YT[:, :, :]).then_inc(sem("sq"), 1)
        V.wait_ge(sem("sq"), nth("DVE", "sq"))
        for c in range(NC):
            V.wait_ge(v_full, v.filled())
            b = v.take()
            stt(YT[:, c, :], b[:, 0:NT], -1.0 / DH, YT[:, c, :], ALU.mult, ALU.add).then_inc(v_free, 1)
            V.wait_ge(v_free, v.emptied())
        tt(T1[:, :, :], YT[:, :, :], YT[:, :, :], ALU.mult).then_inc(sem("sq"), 1)
        V.wait_ge(sem("sq"), nth("DVE", "sq"))
        for c in range(NC):
            V.wait_ge(v_full, v.filled())
            b = v.take()
            V.tensor_copy(T1[:, c, :], b[:, 0:NT]).then_inc(v_free, 1)
            V.wait_ge(v_free, v.emptied())
        rsqrt_dve(T1[:, :, :], 1.0 / DH, 64e-5)
        tt(YT[:, :, :], YT[:, :, :], T1[:, :, :], ALU.mult).then_inc(dve_done, 1)
        V.wait_ge(dve_done, nth("DVE", "dve_done"))
        for c in range(NC):
            ts(YT[:, c, :], YT[:, c, :], PAR[:, LNW + c:LNW + c + 1], PAR[:, LNB + c:LNB + c + 1], ALU.mult, ALU.add).then_inc(dve_done, 1)
            V.wait_ge(dve_done, nth("DVE", "dve_done"))
        for c in range(NC):
            stt(T1[:, c, :], PRT[:, c, :], PAR[:, RK + c:RK + c + 1], PRT[:, 6 + c, :], ALU.mult, ALU.mult).then_inc(dve_done, 1)
            V.wait_ge(dve_done, nth("DVE", "dve_done"))
        V.memset(ST[:, 8:9], 0.0).then_inc(sem("sq"), 1)
        V.wait_ge(sem("sq"), nth("DVE", "sq"))
        for c in range(NC):
            V.wait_ge(v_full, v.filled())
            b = v.take()
            tt(T1[:, c, :], b[:, 0:NT], PRT[:, 12 + c, :], ALU.mult).then_inc(v_free, 1)
            V.wait_ge(v_free, v.emptied())
        tt(YT[:, :, :], YT[:, :, :], T1[:, :, :], ALU.add).then_inc(dve_done, 1)
        V.wait_ge(dve_done, nth("DVE", "dve_done"))
        tt(MIXT[:, 0:NC, :], YT[:, :, :], GG[:, :, :], ALU.mult).then_inc(dve_done, 1)
        V.wait_ge(dve_done, nth("DVE", "dve_done"))
        V.wait_ge(sem("sout_stored"), 16)
        V.memset(ST[:, 8:9], 0.0).then_inc(sem("u1_ys"), 1)
        V.wait_ge(sem("u1_ys"), nth("DVE", "u1_ys"))

    def pool_sample_step():
        nc.gpsimd.wait_ge(sem("s_state"), 16)
        nc.gpsimd.wait_ge(sem("vecs"), 16 * 6 * NB)
        s, t = SST[0:RS, :, :], STMP[0:RS, :, :]
        row = lambda q: VEC[0:RS, q:q + 1, :].broadcast_to([RS, DH, DH])
        colv = lambda ap: ap.unsqueeze(2).broadcast_to([RS, DH, DH])
        sa = SAV[0:RS, :]
        G_ = nc.gpsimd
        G_.tensor_tensor(t, s, row(3), ALU.mult).then_inc(sem("s_step"), 1)
        G_.wait_ge(sem("s_step"), 1)
        pool_sum(t, 1)
        G_.tensor_scalar(sa, t[:, :, 0], -1.0, None, ALU.mult).then_inc(sem("s_step"), 1)
        G_.tensor_tensor(s, s, row(0), ALU.mult).then_inc(sem("s_step"), 1)
        G_.wait_ge(sem("s_step"), 9)
        G_.tensor_tensor(t, colv(sa), row(4), ALU.mult).then_inc(sem("s_step"), 1)
        G_.wait_ge(sem("s_step"), 10)
        G_.tensor_tensor(s, s, t, ALU.add).then_inc(sem("s_step"), 1)
        G_.wait_ge(sem("s_step"), 11)
        G_.tensor_tensor(t, colv(VEC[0:RS, 2, :]), row(1), ALU.mult).then_inc(sem("s_step"), 1)
        G_.wait_ge(sem("s_step"), 12)
        G_.tensor_tensor(s, s, t, ALU.add).then_inc(sem("s_step"), 1)
        G_.wait_ge(sem("s_step"), 13)
        G_.dma_start(O["s_rwkv"][0].rearrange("b h v k -> (b h) v k"), s).then_inc(sem("s_stored"), 16)
        G_.tensor_tensor(t, s, row(5), ALU.mult).then_inc(sem("s_step"), 1)
        G_.wait_ge(sem("s_step"), 14)
        pool_sum(t, 14)
        G_.tensor_copy(sa, t[:, :, 0]).then_inc(sem("s_step"), 1)
        G_.wait_ge(sem("s_step"), 21)

    def pool_sum(t, n):
        w = DH // 2
        while w:
            nc.gpsimd.tensor_tensor(t[:, :, 0:w], t[:, :, 0:w], t[:, :, w:2 * w], ALU.add).then_inc(sem("s_step"), 1)
            n, w = n + 1, w // 2
            nc.gpsimd.wait_ge(sem("s_step"), n)

    def dve_inverse(j):
        msk = lambda k: C(k).unsqueeze(1).broadcast_to([P, 6, CH])
        bank = lambda b: b[:, 0:6 * CH].rearrange("p (h t) -> p h t", h=6)
        half = lambda m, q: m[:, 6 * q:6 * q + 6, :]
        for q in range(2):
            V.wait_ge(v_full, v.filled())
            b = bank(v.take())
            stt(half(P0, q), b, -1.0, msk("m16l"), ALU.mult, ALU.mult)
            tt(half(LO32, q), b, msk("off32"), ALU.mult)
            tt(half(LO64, q), b, msk("off64"), ALU.mult).then_inc(v_free, 1)
            V.wait_ge(v_free, v.emptied())
            tt(half(TI, q), half(P0, q), msk("ident64"), ALU.add)
        for q in range(2):
            V.wait_ge(v_full, v.filled())
            b = bank(v.take())
            stt(half(Q0, q), b, -1.0, msk("m16u"), ALU.mult, ALU.mult).then_inc(v_free, 1)
        for m, k in ((LKT, "m_iu"), (QBT, "m_ieu"), (QKT, "m_ieu")):
            for q in range(2):
                V.wait_ge(v_full, v.filled())
                b = bank(v.take())
                tt(half(m, q), b, msk(k), ALU.mult).then_inc(v_free, 1)
        p, q_, p2, q2 = P0, Q0, P1, Q1
        for k in range(3):
            for m in (p2, q2) if k < 2 else (q2,):
                for q in range(2):
                    V.wait_ge(v_full, v.filled())
                    b = bank(v.take())
                    V.tensor_copy(half(m, q), b).then_inc(v_free, 1)
            p, q_, p2, q2 = p2, q2, p, q_
            V.wait_ge(v_free, v.emptied())
            for q in range(2):
                V.wait_ge(v_full, v.filled())
                b = bank(v.take())
                tt(half(TI, q), half(TI, q), b, ALU.add).then_inc(v_free, 1)
        for q in range(2):
            V.wait_ge(v_full, v.filled())
            b = bank(v.take())
            V.tensor_copy(half(TT_, q), b).then_inc(v_free, 1)
        V.wait_ge(v_free, v.emptied())
        for lo in (LO32, LO64):
            for q in range(2):
                V.wait_ge(v_full, v.filled())
                b = bank(v.take())
                V.tensor_copy(half(ZZ, q), b).then_inc(v_free, 1)
            held = []
            for m in (TI, TT_) if lo is LO32 else (TT_,):
                for q in range(2):
                    V.wait_ge(v_full, v.filled())
                    held.append((m, q, v.take()))
            for m, q, bk in held:
                tt(half(m, q), half(m, q), bank(bk), ALU.subtract).then_inc(v_free, 1)
            V.wait_ge(v_free, v.emptied())
        V.memset(ST[:, 8:9], 0.0).then_inc(sem("state"), 1)
        V.wait_ge(sem("state"), nth("DVE", "state"))

    def dve_chunk(j, c):
        cp = c % 2
        o = slice(64 * cp, 64 * cp + 64)
        t = slice(c * CH, (c + 1) * CH)
        x = X1M[o, :, :]
        for odd in range(2):
            V.wait_ge(v_full, v.filled())
            b = v.take()
            V.tensor_copy(x[:, odd:H:2, :], b[o, 0:6 * CH].rearrange("p (h v) -> p h v", h=6)).then_inc(v_free, 1)
            V.wait_ge(v_free, v.emptied())
        for q in range(2):
            V.wait_ge(v_full, v.filled())
            b = v.take()
            xq = x[:, 6 * q:6 * q + 6, :]
            stt(xq, b[o, 0:6 * CH].rearrange("p (h v) -> p h v", h=6), -1.0, xq, ALU.mult, ALU.subtract).then_inc(v_free, 1)
            V.wait_ge(v_free, v.emptied())
        for q in range(2):
            V.wait_ge(v_full, v.filled())
            b = v.take()
            V.tensor_copy(SAM[o, 6 * q:6 * q + 6, :], b[o, 0:6 * CH].rearrange("p (h v) -> p h v", h=6)).then_inc(v_free, 1)
            V.wait_ge(v_free, v.emptied())
        V.wait_ge(v_full, v.filled())
        b = v.take()
        yt = YT[:, :, t]
        V.tensor_copy(yt, b[:, 0:6 * CH].rearrange("p (h v) -> p h v", h=6)).then_inc(v_free, 1)
        V.wait_ge(v_free, v.emptied())
        V.wait_ge(v_full, v.filled())
        b = v.take()
        tt(yt, yt, b[:, 0:6 * CH].rearrange("p (h v) -> p h v", h=6), ALU.add).then_inc(v_free, 1)
        V.wait_ge(v_free, v.emptied())
        V.wait_ge(v_full, v.filled())
        b = v.take()
        tt(STT[:, :, :], STT[:, :, :], b[:, 0:6 * CH].rearrange("p (h v) -> p h v", h=6), ALU.add).then_inc(v_free, 1)
        V.wait_ge(v_free, v.emptied())
        tt(STT[:, :, :], STT[:, :, :], LAMK[:, :, c:c + 1].broadcast_to([P, NC, CH]), ALU.mult).then_inc(dve_done, 1)
        V.wait_ge(dve_done, nth("DVE", "dve_done"))
        if c % 2 == 0 or c == NCK - 1:
            V.memset(ST[:, 8:9], 0.0).then_inc(sem("state"), 1)
            V.wait_ge(sem("state"), nth("DVE", "state"))

    with nc.Block() as block:

        @block.sync
        def _(sp):
            nc.sync.wait_ge(sem("x_zero"), nth("SP", "x_zero"))
            sp_params()
            sp.wait_ge(sem("pages"), 16)
            load_mem(sp, 0)
            sp_win(0, "w_in_a", WIN_A, C_A)
            sp_router(0)
            sp_cmp()
            sp_sample()
            sp_wo(0)
            sp_memattn(0)
            moe("SP", 0)
            sp_layer_b()
            moe("SP", 1)

        @block.gpsimd
        def _(pool):
            pool.memset(X[:, 2, :], 0.0).then_inc(sem("x_zero"), 1)
            nc.gpsimd.wait_ge(sem("x_zero"), nth("POOL", "x_zero"))
            pool_mem(0)
            pool_proj_a()
            pool_sample()
            pool_layer_b()
            nc.gpsimd.wait_ge(sem("y"), nth("POOL", "y"))
            nc.gpsimd.dma_start(O["y_prompt"].rearrange("o (i p) d -> p (o i) d", p=P),
                                X[:, 0:2, :]).then_inc(stored, 16)
            nc.gpsimd.dma_start(O["y_sample"].rearrange("b o d -> (b o) d"), X[0:NB, 2, :]).then_inc(stored, 16)
            pool.wait_ge(stored, 16 * STORES)

        @block.scalar
        def _(act):
            AC.wait_ge(sem("st_zero"), nth("ACT", "st_zero"))
            AC.copy(ST[:, 29:30], ST[:, 31:32]).then_inc(a_free, 4)
            act_norm()
            act_mem(0)
            act_proj_a()
            act_cmp()
            act_prompt()
            act_sample()
            act_memattn(0)
            act_norm()
            act_router()
            moe("ACT", 0)
            act_layer_b()
            act_norm()
            act_router()
            moe("ACT", 1)

        @block.vector
        def _(dve):
            V.memset(ST[:, :], 0.0).then_inc(sem("st_zero"), 1)
            V.wait_ge(sem("st_zero"), nth("DVE", "st_zero"))
            V.memset(ST[:, 9:10], 0.0).then_inc(v_free, 4)
            V.wait_ge(sem("x"), nth("DVE", "x", 16 * 2))
            V.wait_ge(sem("consts"), nth("DVE", "consts", 16))
            dve.wait_ge(sem("params"), 16 * NPARAM)
            dve_norm(MIXG)
            dve_mem(0)
            dve_proj_a()
            dve_cmp()
            dve_prompt()
            dve_sample_scores()
            dve_memattn(0)
            dve_out(0)
            dve_norm(FFNG)
            dve_router()
            moe("DVE", 0)
            V.memset(ST[:, 8:9], 0.0).then_inc(sem("moe_done"), 1)
            V.wait_ge(sem("moe_done"), nth("DVE", "moe_done"))
            dve_layer_b()
            dve_out(1)
            dve_norm(FFNG + 8)
            dve_router()
            moe("DVE", 1)
            V.memset(ST[:, 8:9], 0.0).then_inc(sem("y"), 1)
            V.wait_ge(sem("y"), nth("DVE", "y"))

        @block.tensor
        def _(pe):
            PE.wait_ge(sem("consts"), nth("PE", "consts", 16))
            pe_norm()
            pe_mem(0)
            pe_proj_a()
            pe_cmp()
            pe_prompt()
            pe_sample_scores()
            pe_sample_values()
            pe_memattn(0)
            pe_out(0)
            pe_norm()
            pe_router()
            moe("PE", 0)
            pe_layer_b()
            pe_out(1)
            pe_norm()
            pe_router()
            moe("PE", 1)
    ctx.close()


INS = ("x_prompt", "x_sample", "cache_cmp_k", "cache_cmp_v", "cache_sel_k", "cache_sel_v", "cache_win_k",
       "cache_win_v", "cache_mem_k", "cache_mem_v", "state_rwkv", "state_shift", "page_table", "mem_prompt",
       "norm_mix", "norm_ffn", "norm_mem", "w_mem_kv", "mem_q_gain", "mem_k_gain", "w_in_a", "nsa_q_gain",
       "nsa_k_gain", "cmp_pe", "cmp_w1", "cmp_b1", "cmp_w2", "w_in_b", "rwkv_mu", "rwkv_w0", "rwkv_w_up",
       "rwkv_a0", "rwkv_a_up", "rwkv_g_up", "rwkv_k_k", "rwkv_k_a", "rwkv_r_k", "rwkv_ln_w", "rwkv_ln_b",
       "w_out", "moe_w_coarse", "moe_b_coarse", "moe_w_fine", "moe_b_fine", "moe_w_gate", "moe_w_up", "moe_w_down")
ROW = (1, 1, SEQ, G, DH)
SROW = (1, NB, 1, G, DH)
OUTS = (("y_prompt", (1, SEQ, D)), ("y_sample", (NB, 1, D)),
        ("p_cmp_k", ROW), ("p_cmp_v", ROW), ("p_sel_k", ROW), ("p_sel_v", ROW), ("p_win_k", ROW), ("p_win_v", ROW),
        ("p_mem_k", (2, 1, SEQ, MH, DH)), ("p_mem_v", (2, 1, SEQ, MH, DH)),
        ("p_rwkv", (1, 1, H, DH, DH)), ("p_shift", (1, 1, SHIFT_W)),
        ("s_cmp_k", SROW), ("s_cmp_v", SROW), ("s_sel_k", SROW), ("s_sel_v", SROW),
        ("s_win_k", (1, NB, WIN, G, DH)), ("s_win_v", (1, NB, WIN, G, DH)),
        ("s_rwkv", (1, NB, H, DH, DH)), ("s_shift", (1, NB, SHIFT_W)))

def kernel(**inputs):
    import concourse.bacc as bacc
    from concourse.bass_utils import run_bass_kernel_spmd

    nc = bacc.Bacc("TRN2", target_bir_lowering=False, num_devices=1)
    at, consts = constants()
    arrays = {name: np.ascontiguousarray(inputs[name]) for name in INS}
    arrays["consts"] = consts
    A = {n: nc.dram_tensor(f"in_{n}", x.shape, mybir.dt.from_np(x.dtype), kind="ExternalInput").ap()
         for n, x in arrays.items()}
    O = {n: nc.dram_tensor(f"out_{n}", shape, F32, kind="ExternalOutput").ap() for n, shape in OUTS}
    build(nc, A, O, at)
    r = run_bass_kernel_spmd(nc, [{f"in_{n}": x for n, x in arrays.items()}], core_ids=[0])
    return tuple(r.results[0][f"out_{n}"] for n, _ in OUTS)
```

```python
from contextlib import ExitStack

import numpy as np
import concourse.bass as bass
from concourse import mybir

F32 = mybir.dt.float32
I32 = mybir.dt.int32
ALU = mybir.AluOpType
ACT = mybir.ActivationFunctionType
AX_X = mybir.AxisListType.X

P = 128
D = 1024
KD = D // P
SEQ, NB = 256, 8
NT = SEQ + NB
TILES = ((0, 128), (128, 128), (256, 8))
DH = 64
H, G, HG = 12, 3, 4
MH = 4
QA, KVW, MEMQ = H * DH, G * DH, MH * DH
GATES = 3 * H
C_A = QA + 6 * KVW + GATES + MEMQ
KV0 = QA
KVN = 6 * KVW + GATES
SHIFT_W = 3 * QA + 256
NCH = SHIFT_W // P
C_B = SHIFT_W + MEMQ
PAST, PAGE = 1024, 128
NPG = PAST // PAGE
SEL = 64
NSEL = PAST // SEL + 1
WIN = 512
NCS, NCP = 63, 15
RS = NB * H
CH = 64
NE, GE, NGRP = 32, 4, 8
FE = 512
SLOT = 32
OVER = (NT + SLOT - 1) // SLOT - 1
UNITS = 12
RING = 6
NEG = -1e30

SLOPES = np.exp2(-8.0 * np.arange(1, H + 1, dtype=np.float32) / H).astype(np.float32)


def constants():
    p = np.arange(P)
    t = np.arange(SEQ)
    f4 = lambda a: np.ascontiguousarray(a, dtype=np.float32)

    def rows(a):
        out = np.zeros((P, a.shape[1]), np.float32)
        out[: a.shape[0]] = a
        return out

    parts = {}
    parts["ident"] = np.eye(P)
    parts["headones"] = (p[:, None] // DH == p[None] // DH)
    parts["ones"] = np.ones((P, P))
    parts["before"] = p[:, None] < p[None]
    dist = np.stack([t[None] - (128 * i + p[:, None]) for i in range(2)], 1).astype(np.float64)
    parts["distp"] = np.where(dist <= 0, dist, NEG).reshape(P, -1)
    cend = np.arange(NCP) * 16 + 31
    dc = np.stack([cend[None] - (128 * i + p[:, None]) for i in range(2)], 1)
    cb = np.where(dc[:, :, None, :] <= 0, dc[:, :, None, :] * SLOPES[None, None, :, None], NEG)
    parts["cmpbias"] = cb.reshape(P, -1)
    parts["cmpmask"] = (dc <= 0).reshape(P, -1)
    parts["slope"] = rows(np.tile(SLOPES, NB)[:, None])
    parts["pos"] = np.tile(np.arange(PAST + 1) - float(PAST), (P, 1))
    parts["cpos"] = np.tile(np.arange(NCS) * 16 + 31 - float(PAST), (P, 1))
    c0, s0 = np.arange(NCS) * 16, np.arange(NSEL) * SEL
    parts["cmpsel"] = rows(((c0[:, None] < s0[None] + SEL) & (c0[:, None] + 32 > s0[None])))
    r = np.arange(RS)
    grp = (r // H) * G + (r % H) // HG
    parts["samegroup"] = rows(grp[:, None] == grp[None])
    parts["rowseq"] = rows(r[:, None] // H == np.arange(NB)[None])
    parts["blkno"] = np.tile(np.arange(1, NSEL - 2), (P, 1))
    i, q = (p % CH)[:, None], np.arange(CH)[None]
    same = lambda n: i // n == q // n
    parts["m_iu"] = (i < q)
    parts["m_ieu"] = (i <= q)
    parts["m16u"] = (i < q) & same(16)
    parts["m16l"] = (i > q) & same(16)
    parts["off32"] = (i > q) & same(32) & ~same(16)
    parts["off64"] = (i > q) & ~same(32)
    parts["ident64"] = (i == q)
    parts["slotno"] = np.tile(np.arange(SLOT * (OVER + 1)), (P, 1))
    hc = np.zeros((P, 2 * H - 2), np.float32)
    hc[:DH, H - 2], hc[DH:, H - 1] = 1, 1
    parts["headcol"] = hc
    parts["fold"] = (p % SLOT)[:, None] == np.arange(SLOT)[None]
    parts["order"] = np.tile(NE - np.arange(NE), (P, 1))
    parts["gorder"] = np.tile(4 - np.arange(4), (P, 1))
    parts["real"] = np.stack([np.ones(P), np.ones(P), p < NB], 1)
    at, cols, off = {}, [], 0
    for k, v in parts.items():
        v = f4(v)
        at[k] = (off, v.shape[1])
        cols.append(v)
        off += v.shape[1]
    return at, f4(np.concatenate(cols, 1))


class Count:

    def __init__(self):
        self.n, self.i, self.per = 0, None, 0

    def value(self, more=0):
        v = self.n + more
        return v if self.i is None else self.i * self.per + v

    def add(self, k):
        self.n += k
        return self.value()

    def loop(self, i, per):
        self.i, self.per, self.start = i, per, self.n

    def end(self, turns):
        assert self.n - self.start == self.per, (self.n - self.start, self.per)
        self.i, self.n = None, self.start + self.per * turns


class Banks:

    def __init__(self, banks):
        self.banks = banks
        self.claimed, self.taken = Count(), Count()

    def room(self):
        return self.claimed.value(1)

    def claim(self):
        self.claimed.add(1)
        return self.banks[(self.claimed.n - 1) % 4]

    def all_free(self, but=0):
        return self.claimed.value(4 - but)

    def filled(self):
        return self.taken.value(1)

    def take(self):
        self.taken.add(1)
        return self.banks[(self.taken.n - 1) % 4]

    def emptied(self):
        return self.taken.value(4)


def build(nc, A, O, at):
    ctx = ExitStack()
    ctx.enter_context(nc.allow_non_contiguous_dma(reason="parameter columns and cut cache rows"))
    base0 = 16512
    names = iter(range(10 ** 6))

    cur = [base0]

    def keep(name, shape, dt=F32):
        t = nc.alloc_sbuf_tensor_at(name, [P] + list(shape), dt, offset=cur[0])
        cur[0] += (int(np.prod(shape)) * 4 + 31) // 32 * 32
        return t

    nconst = sum(w for _, w in at.values())
    CONST = keep("CONST", [nconst])
    C = lambda k, p=P: CONST[0:p, at[k][0]:at[k][0] + at[k][1]]
    X = keep("X", [3, D])
    XN = keep("XN", [3, D])
    HT = keep("HT", [KD, NT])
    MIXT = keep("MIXT", [KD, NT])
    PAR = keep("PAR", [120])
    ROWG = keep("ROWG", [4, DH])
    ST = keep("ST", [64])
    WR = keep("WR", [KD, 36])
    BR = keep("BR", [36])
    RT = keep("RT", [3, NE])
    RW = keep("RW", [3, NE])
    CNT = keep("CNT", [4], I32)
    PGT = keep("PGT", [NB * NPG], I32)
    U1 = cur[0]
    U2 = U1 + 32768
    ARENA = U2 + 21120

    def place(name, off, shape, dt=F32, base=ARENA):
        n = int(np.prod(shape)) * 4
        assert base + off + n <= nc.sbuf_usable_end, (name, base + off + n - nc.sbuf_usable_end)
        return nc.alloc_sbuf_tensor_at(f"{name}_{next(names)}", [P] + list(shape), dt, offset=base + off)

    XNoff = (nconst * 4 + 31) // 32 * 32 + 12288 + base0
    WM = place("WM", 0, [KD, 512], base=U1)
    MEM = place("MEM", 16384, [2, D], base=U1)
    MT = place("MT", 24576, [KD, SEQ], base=U1)
    WO = place("WO", 0, [KD, D], base=U1)
    KV = place("KV", 0, [3, KVN], base=U2)
    PRT = place("PRT", 0, [NCH, NT], base=U2)
    QT = place("QT", 0, [8, NT], base=XNoff)
    KMT = place("KMT", 8448, [2, SEQ], base=XNoff)
    WIN_A = place("WIN_A", 0, [KD, C_A])
    SQ_A = place("SQ_A", KD * C_A * 4, [8, NT])
    RS_A = place("RS_A", 0, [8, NT])
    SQ_K = place("SQ_K", 10496, [3, 2 * KVW])
    KVMS = [place("KVM", 14272, [2, 512], base=U2), place("KVM", 2112, [2, 512], base=XNoff)]
    WIN_B = place("WIN_B", 0, [KD, C_B])

    KT = place("KT", 0, [2, G, SEQ])
    KNEW = place("KNEW", 6144, [2, 2, NB])
    PP = place("PP", 88064, [3, 512])
    PPT = place("PPT", 10496, [2, 512])
    SPT = place("SPT", 6400, [14, RS])
    CS = place("CS", 14592, [2, H * NCP])
    CPT = place("CPT", 16064, [2 * H, P])
    CKT = place("CKT", 28352, [2, 9, 64])
    CV = place("CV", 32960, [9, KVW])
    W1 = place("W1", 39872, [2, 16, P])
    HID = place("HID", 56256, [2, 256])
    XR = [place("XR", 6144 * n, [4, 384], base=U1) for n in range(5)] + [
        place("XR", o, [4, 384]) for o in (58304, 64448, 16064, 22208)]
    XT = place("XT", 70592, [G, 4, 512])
    PE_T = place("PE_T", 95168, [2, 16])
    W2 = place("W2", 95296, [2, DH])
    CB = place("CB", 95808, [2])
    CBR = place("CBR", 95840, [2, P])
    OLD = [place("OLD", o, [NPG + 4, KVW], base=b) for o, b in (
        (39872, ARENA), (0, U1), (9216, U1), (49088, ARENA), (18432, U1))]
    KTS = [place("KTS", o, [2, PAST + WIN]) for o in (58304, 14592)]
    QBD = place("QBD", 70592, [2, NB, RS])
    VO = place("VO", 70592, [NB, KVW])
    SS = place("SS", 76736, [1604])
    PD = place("PD", 83200, [2, RS])
    SMALL = place("SMALL", 83968, [128])
    RINGW = place("RINGW", 0, [RING, 4096])
    HG_T = place("HG_T", 0, [KD, P], base=U2)
    SELT = place("SELT", 4096, [3, P], base=U2)
    SELW = place("SELW", 5632, [3, P], base=U2)
    SWT = place("SWT", 7168, [NT], base=U2)
    SG = place("SG", 8256, [FE], base=U2)
    AV = place("AV", 10304, [FE], base=U2)
    AVT = place("AVT", 12352, [4, P], base=U2)
    OUT4 = place("OUT4", 14400, [D], base=U2)
    RTMP = place("RTMP", 0, [16, 3, 36], base=U2)

    banks = [nc.alloc_psum_tensor(f"bank{i}", [P, 512], F32) for i in range(8)]
    v, a = Banks(banks[0:4]), Banks(banks[4:8])
    v_full, v_free, a_full, a_free, dve_done, act_done, stored = (
        nc.alloc_semaphore(n) for n in ("v_full", "v_free", "a_full", "a_free", "dve_done", "act_done", "stored"))
    w_used = nc.alloc_semaphore("w_used")
    w_in_ring = [nc.alloc_semaphore(f"w_in_ring{s}") for s in range(RING)]
    sems, counted = {}, {}

    def sem(name):
        if name not in sems:
            sems[name] = nc.alloc_semaphore(name)
        return sems[name]

    def count(who, name):
        return counted.setdefault((who, name), Count())

    def nth(who, name, k=1):
        return count(who, name).add(k)

    NM = {"SP": nc.sync, "PE": nc.tensor, "DVE": nc.vector, "ACT": nc.scalar, "POOL": nc.gpsimd}

    ident = C("ident")
    V, AC, PE = nc.vector, nc.scalar, nc.tensor
    tt, ts, stt = V.tensor_tensor, V.tensor_scalar, V.scalar_tensor_tensor

    def mm(out, l, r, start=True, stop=True):
        return PE.matmul(out, lhsT=l, rhs=r, start=start, stop=stop, skip_group_check=True)

    def tr(out, in_):
        p = in_.shape[0]
        return PE.transpose(out, in_, ident[0:p, 0:p])

    def col(off, src, chunks):
        nc.sync.dma_start(PAR[:, off:off + chunks], src.rearrange("(c p) -> p c", p=P)).then_inc(sem("params"), 16)

    MIXG, FFNG, MEMG, QG, MQG, KG0, MU, W0, A0, KK, KA, RK, LNW, LNB = (
        0, 16, 32, 48, 50, 52, 54, 74, 80, 86, 92, 98, 104, 110)
    CB1 = 116

    def sp_params():
        nc.sync.dma_start(X[:, 0:2, :], A["x_prompt"].rearrange("o (i p) d -> p (o i) d", p=P)).then_inc(sem("x"), 16)
        nc.sync.dma_start(X[0:NB, 2, :], A["x_sample"].rearrange("b o d -> (b o) d")).then_inc(sem("x"), 16)
        nc.sync.dma_start(CONST[:, :], A["consts"]).then_inc(sem("consts"), 16)
        nc.sync.dma_start(PGT[0:1, :],
                          A["page_table"].rearrange("(o a) b -> o (a b)", o=1)).then_inc(sem("pages"), 16)
        for off, n in ((MIXG, "norm_mix"), (MEMG, "norm_mem")):
            nc.sync.dma_start(PAR[:, off:off + 8], A[n][0].rearrange("(c p) -> p c", p=P)).then_inc(sem("first_gains"), 16)

    def sp_more_params():
        for l in range(2):
            if l:
                col(MIXG + 8 * l, A["norm_mix"][l], 8)
                col(MEMG + 8 * l, A["norm_mem"][l], 8)
            col(FFNG + 8 * l, A["norm_ffn"][l], 8)
            for hf in range(2):
                nc.sync.dma_start(PAR[64 * hf:64 * hf + 64, MQG + l:MQG + l + 1],
                                  A["mem_q_gain"][l].rearrange("(d o) -> d o", o=1)).then_inc(sem("params"), 16)
            nc.sync.dma_start(ROWG[:, l, :],
                              A["mem_k_gain"][l:l + 1, :].broadcast_to([P, DH])).then_inc(sem("params"), 16)
            nc.sync.dma_start(ROWG[:, 2 + l, :],
                              A["nsa_k_gain"][0, 1 + l:2 + l, :].broadcast_to([P, DH])).then_inc(sem("params"), 16)
        for hf in range(2):
            nc.sync.dma_start(PAR[64 * hf:64 * hf + 64, QG:QG + 1],
                              A["nsa_q_gain"][0].rearrange("(d o) -> d o", o=1)).then_inc(sem("params"), 16)
            nc.sync.dma_start(PAR[64 * hf:64 * hf + 64, KG0:KG0 + 1],
                              A["nsa_k_gain"][0, 0].rearrange("(d o) -> d o", o=1)).then_inc(sem("params"), 16)
        nc.sync.dma_start(PAR[:, CB1:CB1 + 2], A["cmp_b1"][0].rearrange("c p -> p c")).then_inc(sem("params"), 16)
        col(MU, A["rwkv_mu"][0], NCH)
        for off, n in ((W0, "rwkv_w0"), (A0, "rwkv_a0"), (KK, "rwkv_k_k"), (KA, "rwkv_k_a"),
                       (LNW, "rwkv_ln_w"), (LNB, "rwkv_ln_b")):
            col(off, A[n][0], 6)
        nc.sync.dma_start(PAR[:, RK:RK + 6],
                          A["rwkv_r_k"][0].rearrange("(c two) n -> (two n) c", two=2)).then_inc(sem("params"), 16)

    NPARAM = 7 + 5 + 4 + 1 + 1 + 6 + 1
    STORES = 4 + 4 + 4 + 4 + 2

    def rsqrt_dve(ap, scale, eps, op=ALU.add):
        ts(ap, ap, scale, eps, ALU.mult, op).then_inc(sem("var"), 1)
        V.wait_ge(sem("var"), nth("DVE", "var"))
        V.wait_ge(sem("std"), nth("DVE", "std"))
        V.reciprocal(ap, ap).then_inc(dve_done, 1)
        V.wait_ge(dve_done, nth("DVE", "dve_done"))

    def rsqrt_act(ap):
        AC.wait_ge(sem("var"), nth("ACT", "var"))
        AC.activation(ap, ap, ACT.Sqrt).then_inc(sem("std"), 1)
        AC.wait_ge(sem("std"), nth("ACT", "std"))

    def dve_squares(i):
        V.tensor_tensor_reduce(out=XN[:, i, :], in0=X[:, i, :], in1=X[:, i, :], scale=1.0, scalar=0.0,
                                  op0=ALU.mult, op1=ALU.add, accum_out=ST[:, i:i + 1]).then_inc(dve_done, 1)
        V.wait_ge(dve_done, nth("DVE", "dve_done"))

    def dve_norm(gain, first=False, squares=True):
        for i in range(3 if squares else 0):
            dve_squares(i)
        rsqrt_dve(ST[:, 0:3], 1.0 / D, 1e-6)
        for i in range(3):
            ts(XN[:, i, :], X[:, i, :], ST[:, i:i + 1], None, ALU.mult)
        V.memset(ST[:, 8:9], 0.0).then_inc(sem("xn"), 1)
        V.wait_ge(sem("xn"), nth("DVE", "xn"))
        if first:
            V.wait_ge(sem("first_gains"), 16 * 2)
        for c in range(KD):
            V.wait_ge(v_full, v.filled())
            b = v.take()
            ts(HT[:, c, :], b[:, 0:NT], PAR[:, gain + c:gain + c + 1], None, ALU.mult).then_inc(v_free, 1)

    def act_norm():
        rsqrt_act(ST[:, 0:3])

    def pe_norm():
        PE.wait_ge(sem("xn"), nth("PE", "xn"))
        for c in range(KD):
            PE.wait_ge(v_free, v.room())
            b = v.claim()
            for i, (t0, n) in enumerate(TILES):
                m = tr(b[:, t0:t0 + n], XN[0:n, i, c * P:(c + 1) * P])
            m.then_inc(v_full, 1)
        PE.wait_ge(v_free, v.all_free())

    def load_mem(eng, l):
        eng.dma_start(WM[:, :, :], A["w_mem_kv"][l].rearrange("(k p) n -> p k n", p=P)).then_inc(sem(f"w_mem{l}"), 16)
        eng.dma_start(MEM[:, :, :], A["mem_prompt"][0].rearrange("(i p) d -> p i d", p=P)).then_inc(sem(f"mem{l}"), 16)

    def dve_mem(l):
        KVM = KVMS[l]
        V.wait_ge(sem(f"mem{l}"), nth("DVE", f"mem{l}", 16))
        for i in range(2):
            V.tensor_tensor_reduce(out=MT[:, 4 * i:4 * i + 4, :].rearrange("p a b -> p (a b)"), in0=MEM[:, i, :],
                                      in1=MEM[:, i, :], scale=1.0, scalar=0.0, op0=ALU.mult, op1=ALU.add,
                                      accum_out=ST[:, i:i + 1]).then_inc(dve_done, 1)
            V.wait_ge(dve_done, nth("DVE", "dve_done"))
        rsqrt_dve(ST[:, 0:2], 1.0 / D, 1e-6)
        for i in range(2):
            ins = ts(MEM[:, i, :], MEM[:, i, :], ST[:, i:i + 1], None, ALU.mult)
            if i == 0:
                ins
            else:
                ins.then_inc(sem("memn"), 1)
                V.wait_ge(sem("memn"), nth("DVE", "memn"))
        for c in range(KD):
            V.wait_ge(v_full, v.filled())
            b = v.take()
            ts(MT[:, c, :], b[:, 0:SEQ], PAR[:, MEMG + 8 * l + c:MEMG + 8 * l + c + 1], None, ALU.mult).then_inc(v_free, 1)
        for i in range(2):
            V.wait_ge(v_full, v.filled())
            b = v.take()
            V.tensor_copy(KVM[:, i, :], b[:, :]).then_inc(v_free, 1)
            V.wait_ge(v_free, v.emptied())
        if l == 0:
            V.wait_ge(sem("params"), 16 * NPARAM)
        kk = KVM[:, :, 0:MEMQ]
        sq = MT[:, 0:2, :]
        tt(sq, kk, kk, ALU.mult).then_inc(dve_done, 1)
        V.wait_ge(dve_done, nth("DVE", "dve_done"))
        st = ST[:, 16:24].rearrange("p (a h) -> p a h", a=2)
        V.tensor_reduce(st, sq.rearrange("p a (h d) -> p a h d", h=MH), AX_X, ALU.add).then_inc(dve_done, 1)
        V.wait_ge(dve_done, nth("DVE", "dve_done"))
        rsqrt_dve(ST[:, 16:24], 1.0 / DH, 1e-6)
        for i in range(2):
            k4 = KVM[:, i, 0:MEMQ].rearrange("p (h d) -> p h d", h=MH)
            tt(k4, k4, st[:, i, :].unsqueeze(2).broadcast_to([P, MH, DH]), ALU.mult).then_inc(dve_done, 1)
            V.wait_ge(dve_done, nth("DVE", "dve_done"))
            ins = tt(k4, k4, ROWG[:, l:l + 1, :].broadcast_to([P, MH, DH]), ALU.mult)
            if i == 0:
                ins
            else:
                ins.then_inc(sem("km"), 1)
                V.wait_ge(sem("km"), nth("DVE", "km"))
        for c in range(2):
            V.wait_ge(v_full, v.filled())
            b = v.take()
            V.tensor_copy(KMT[:, c, :], b[:, 0:SEQ]).then_inc(v_free, 1)
        V.memset(ST[:, 8:9], 0.0).then_inc(sem("u1_used"), 1)
        V.wait_ge(sem("u1_used"), nth("DVE", "u1_used"))

    def act_mem(l):
        rsqrt_act(ST[:, 0:2])
        rsqrt_act(ST[:, 16:24])

    def pe_mem(l):
        KVM = KVMS[l]
        PE.wait_ge(sem("memn"), nth("PE", "memn"))
        for c in range(KD):
            PE.wait_ge(v_free, v.room())
            b = v.claim()
            for i in range(2):
                m = tr(b[:, i * P:(i + 1) * P], MEM[:, i, c * P:(c + 1) * P])
            m.then_inc(v_full, 1)
        PE.wait_ge(v_free, v.all_free())
        PE.wait_ge(sem(f"w_mem{l}"), nth("PE", f"w_mem{l}", 16))
        for i in range(2):
            PE.wait_ge(v_free, v.room())
            b = v.claim()
            for k in range(KD):
                m = mm(b[:, :], MT[:, k, i * P:(i + 1) * P], WM[:, k, :], k == 0, k == KD - 1)
            m.then_inc(v_full, 1)
        PE.wait_ge(sem("km"), nth("PE", "km"))
        for c in range(2):
            PE.wait_ge(v_free, v.room())
            b = v.claim()
            for i in range(2):
                m = tr(b[:, i * P:(i + 1) * P], KVM[:, i, c * P:(c + 1) * P])
            m.then_inc(v_full, 1)
        PE.wait_ge(v_free, v.all_free())

    def pool_mem(l):
        KVM = KVMS[l]
        nc.gpsimd.wait_ge(sem("km"), nth("POOL", "km"))
        for o, c0 in (("p_mem_k", 0), ("p_mem_v", MEMQ)):
            nc.gpsimd.dma_start(O[o][l, 0].rearrange("(i p) h d -> p i (h d)", p=P),
                                KVM[:, :, c0:c0 + MEMQ]).then_inc(stored, 16)

    CK2 = place("CK2", 96896, [G, NCP])

    def sp_win(l, name, tile, cols):
        if l:
            nc.sync.wait_ge(sem("moe_done"), nth("SP", "moe_done"))
        w = A[name][0].rearrange("(k p) n -> p k n", p=P)
        for k in range(KD):
            nc.sync.dma_start(tile[:, k, :], w[:, k, :]).then_inc(sem("w_in"), 16)

    def pe_channels(tile, cols):
        for c0 in cols:
            PE.wait_ge(v_free, v.room())
            b = v.claim()
            for k in range(KD):
                m = mm(b[:, 0:NT], tile[:, k, c0:c0 + P], HT[:, k, :], k == 0, k == KD - 1)
            m.then_inc(v_full, 1)

    def pe_headnorm(sq, n):
        PE.wait_ge(sem("sq"), nth("PE", "sq"))
        for c in range(n):
            PE.wait_ge(v_free, v.room())
            b = v.claim()
            mm(b[:, 0:sq.shape[2]], C("headones"), sq[:, c, :]).then_inc(v_full, 1)

    def act_headnorm(rs):
        rsqrt_act(rs[:, :, :])

    def dve_headnorm(x, sq, rs, n, gains):
        w = x.shape[2]
        tt(sq[:, :, :], x[:, :, :], x[:, :, :], ALU.mult).then_inc(sem("sq"), 1)
        V.wait_ge(sem("sq"), nth("DVE", "sq"))
        for c in range(n):
            V.wait_ge(v_full, v.filled())
            b = v.take()
            V.tensor_copy(rs[:, c, :], b[:, 0:w]).then_inc(v_free, 1)
            V.wait_ge(v_free, v.emptied())
        rsqrt_dve(rs[:, :, :], 1.0 / DH, 1e-6)
        for c in range(n):
            g = gains[c]
            stt(x[:, c, :], x[:, c, :], PAR[:, g:g + 1], rs[:, c, :], ALU.mult, ALU.mult)

    KVCUTS = ((0, 512), (512, 512), (1024, KVN - 1024))

    def pe_few(b, x, w, cols):
        for k in range(KD):
            q = 32 * (k % 4)
            m = mm(b[q:q + NB, 0:cols.stop - cols.start], x[:, k, SEQ:NT], w[:, k, cols], k < 4, k >= KD - 4)
        return m

    def pe_proj_a():
        PE.wait_ge(sem("w_in"), nth("PE", "w_in", 16 * KD))
        pe_channels(WIN_A, [P * c for c in range(6)] + [KV0 + KVN, KV0 + KVN + P])
        for i, (t0, n) in reversed(list(enumerate(TILES))):
            for c0, w in KVCUTS:
                PE.wait_ge(v_free, v.room())
                b = v.claim()
                if n == NB:
                    m = pe_few(b, HT, WIN_A, slice(KV0 + c0, KV0 + c0 + w))
                else:
                    for k in range(KD):
                        m = mm(b[0:n, 0:w], HT[:, k, t0:t0 + n], WIN_A[:, k, KV0 + c0:KV0 + c0 + w], k == 0, k == KD - 1)
                m.then_inc(v_full, 1)
        pe_headnorm(SQ_A, 8)

    def dve_few(x, b, first):
        w = x.shape[1]
        for q in range(first, 4):
            ins = tt(x, x, b[32 * q:32 * q + NB, 0:w], ALU.add)
            if q < 3:
                ins.then_inc(dve_done, 1)
                V.wait_ge(dve_done, nth("DVE", "dve_done"))
        ins.then_inc(v_free, 1)

    def dve_proj_a():
        for c in range(8):
            V.wait_ge(v_full, v.filled())
            b = v.take()
            V.tensor_copy(QT[:, c, :], b[:, 0:NT]).then_inc(v_free, 1)
        for i, (t0, n) in reversed(list(enumerate(TILES))):
            for c0, w in KVCUTS:
                V.wait_ge(v_full, v.filled())
                b = v.take()
                rows = KV[0:n, i, c0:c0 + w]
                if n == NB:
                    V.tensor_copy(rows, b[0:n, 0:w]).then_inc(dve_done, 1)
                    V.wait_ge(dve_done, nth("DVE", "dve_done"))
                    dve_few(rows, b, 1)
                else:
                    V.tensor_copy(rows, b[0:n, 0:w]).then_inc(v_free, 1)
        V.memset(ST[:, 8:9], 0.0).then_inc(sem("gates_in"), 1)
        V.wait_ge(sem("gates_in"), nth("DVE", "gates_in"))
        ts(PAR[:, QG:QG + 1], PAR[:, QG:QG + 1], DH ** -0.5, None, ALU.mult)
        tt(SQ_A[:, :, :], QT[:, :, :], QT[:, :, :], ALU.mult).then_inc(sem("sq"), 1)
        V.wait_ge(sem("sq"), nth("DVE", "sq"))
        for c in range(8):
            V.wait_ge(v_full, v.filled())
            b = v.take()
            V.tensor_copy(RS_A[:, c, :], b[:, 0:NT]).then_inc(v_free, 1)
        V.wait_ge(v_free, v.emptied())
        ts(RS_A[:, :, :], RS_A[:, :, :], 1.0 / DH, 1e-6, ALU.mult, ALU.add).then_inc(sem("var"), 1)

    def dve_norms(k):
        if k < 8:
            if k == 0:
                V.wait_ge(sem("std"), nth("DVE", "std"))
            g = QG if k < 6 else MQG
            V.reciprocal(RS_A[:, k, :], RS_A[:, k, :]).then_inc(dve_done, 1)
            V.wait_ge(dve_done, nth("DVE", "dve_done"))
            stt(QT[:, k, :], QT[:, k, :], PAR[:, g:g + 1], RS_A[:, k, :], ALU.mult, ALU.mult)
        elif k == 8:
            for i, (t0, n) in enumerate(TILES):
                kk = KV[0:n, i, 2 * KVW:6 * KVW].rearrange("p (a b) -> p a b", a=2)[:, :, 0:KVW]
                tt(SQ_K[0:n, i, :].rearrange("p (a b) -> p a b", a=2), kk, kk, ALU.mult).then_inc(dve_done, 1)
                V.wait_ge(dve_done, nth("DVE", "dve_done"))
                V.tensor_reduce(ST[0:n, 10 + 6 * i:16 + 6 * i], SQ_K[0:n, i, :].rearrange("p (a d) -> p a d", d=DH),
                                AX_X, ALU.add).then_inc(dve_done, 1)
                V.wait_ge(dve_done, nth("DVE", "dve_done"))
            ts(ST[:, 10:28], ST[:, 10:28], 1.0 / DH, 1e-6, ALU.mult, ALU.add).then_inc(sem("var"), 1)
        elif k < 12:
            if k == 9:
                V.wait_ge(sem("std"), nth("DVE", "std"))
                V.reciprocal(ST[:, 10:28], ST[:, 10:28]).then_inc(dve_done, 1)
                V.wait_ge(dve_done, nth("DVE", "dve_done"))
            i = k - 9
            n = TILES[i][1]
            for z in range(2):
                c0 = (2 + 2 * z) * KVW
                k3 = KV[0:n, i, c0:c0 + KVW].rearrange("p (g d) -> p g d", g=G)
                r3 = ST[0:n, 10 + 6 * i + 3 * z:13 + 6 * i + 3 * z]
                tt(k3, k3, r3.unsqueeze(2).broadcast_to([n, G, DH]), ALU.mult).then_inc(dve_done, 1)
                V.wait_ge(dve_done, nth("DVE", "dve_done"))
                tt(k3, k3, ROWG[0:n, 2 + z:3 + z, :].broadcast_to([n, G, DH]), ALU.mult)
            if k == 11:
                V.memset(ST[:, 8:9], 0.0).then_inc(sem("kv"), 1)
                V.wait_ge(sem("kv"), nth("DVE", "kv"))

    def act_proj_a():
        AC.wait_ge(sem("gates_in"), nth("ACT", "gates_in"))
        for i, (t0, n) in enumerate(TILES):
            g = KV[0:n, i, 6 * KVW:KVN]
            ins = AC.activation(g, g, ACT.Sigmoid)
            if i < 2:
                ins
            else:
                ins.then_inc(sem("gates"), 1)
                AC.wait_ge(sem("gates"), nth("ACT", "gates"))
        act_headnorm(RS_A)

    ROWS = ("cmp_k", "cmp_v", "sel_k", "sel_v", "win_k", "win_v")

    def pool_proj_a():
        nc.gpsimd.wait_ge(sem("gates_in"), nth("POOL", "gates_in"))
        for z, n in enumerate(ROWS):
            if z == 2:
                nc.gpsimd.wait_ge(sem("kv"), nth("POOL", "kv"))
            c = slice(z * KVW, (z + 1) * KVW)
            dst = O["p_" + n][0, 0].rearrange("(i p) g d -> p i (g d)", p=P)
            if z < 2:
                nc.gpsimd.dma_start(dst, KV[:, 0:2, c]).then_inc(sem("cmp_rows"), 16)
            else:
                nc.gpsimd.dma_start(dst, KV[:, 0:2, c]).then_inc(stored, 16)
            if z < 4:
                nc.gpsimd.dma_start(O["s_" + n][0].rearrange("b o g d -> b (o g d)"),
                                    KV[0:NB, 2, c]).then_inc(stored, 16)
            else:
                out = O["s_" + n][0].rearrange("b w g d -> b w (g d)")
                old = A["cache_" + n][0].rearrange("b w g d -> b w (g d)")
                nc.gpsimd.dma_start(out[:, WIN - 1, :], KV[0:NB, 2, c]).then_inc(stored, 16)
                nc.gpsimd.dma_start(out[:, 0:WIN - 1, :], old[:, 1:WIN, :]).then_inc(stored, 16)

    NXR = len(XR)

    def sp_cmp_weights():
        nc.sync.wait_ge(sem("gates_in"), nth("SP", "gates_in"))
        nc.sync.dma_start(W1[:, :, :, :], A["cmp_w1"][0].rearrange("c (m p) f -> p c m f", p=P)).then_inc(sem("cmp_w"), 16)
        nc.sync.dma_start(PE_T[:, :, :], A["cmp_pe"][0].rearrange("c (m j) d -> (j d) c m", j=2)).then_inc(sem("cmp_w"), 16)
        nc.sync.dma_start(W2[:, :, :], A["cmp_w2"][0].rearrange("c f d -> f c d")).then_inc(sem("cmp_w"), 16)

    def sp_cmp():
        nc.sync.wait_ge(sem("u1_used"), nth("SP", "u1_used"))
        n = 0
        for z, nm in enumerate(("k", "v")):
            pool = A["cache_cmp_" + nm][0].rearrange("n (q j) g d -> n q (j g d)", j=2)
            for s in range(NB):
                if n == 5:
                    sp_cmp_weights()
                if n >= NXR:
                    nc.sync.wait_ge(sem("xr_used"), nth("SP", "xr_used"))
                for pg in range(NPG):
                    page = nc.sync.value_load(PGT[0:1, s * NPG + pg:s * NPG + pg + 1], min_val=0, max_val=79)
                    nc.sync.dma_start(XR[n % NXR][64 * (pg % 2):64 * (pg % 2) + 64, pg // 2, :],
                                      pool[bass.ds(page, 1)].rearrange("n q c -> (n q) c")).then_inc(sem(f"xr{n % NXR}"), 16)
                n += 1
            nc.sync.wait_ge(sem("xr_used"), nth("SP", "xr_used"))
            if z == 0:
                nc.sync.wait_ge(sem("cmp_rows"), nth("SP", "cmp_rows", 16 * 2))
            nc.sync.dma_start(XR[n % NXR][:, 0, :],
                              O["p_cmp_" + nm][0, 0].rearrange("(q j) g d -> q (j g d)", j=2)).then_inc(sem(f"xr{n % NXR}"), 16)
            n += 1

    def halves(third):
        for hf in range(2):
            j, g = divmod(2 * third + hf, G)
            yield slice(64 * hf, 64 * hf + 64), slice(64 * j, 64 * j + 64), g

    def pe_turn(n, tiles, slot):
        for third in range(3):
            if third == 1:
                PE.wait_ge(v_free, v.room())
                b = v.claim()
            else:
                PE.wait_ge(a_free, a.room())
                b = a.claim()
            for t in range(tiles):
                m = tr(b[:, t * P:(t + 1) * P], XR[n % NXR][:, t, third * P:(third + 1) * P])
            m.then_inc(v_full if third == 1 else a_full, 1)

    def pe_windows(z, g0, ng, slots, w, n):
        PE.wait_ge(a_free, a.room())
        b = a.claim()
        for m in range(16):
            if ng == 1:
                x = XT[:, g0, 0:slots, m:m + 8 * (n - 1) + 1:8]
            else:
                x = XT[:, 0:ng, 0, m:m + 8 * (n - 1) + 1:8]
            i = mm(b[:, 0:w], W1[:, z, m, :], x, m == 0, m == 15)
        i.then_inc(a_full, 1)

    def pe_summaries(z, hid, g, seqs, n):
        PE.wait_ge(v_free, v.room())
        b = v.claim()
        if z == 0:
            o = 64 * (g % 2)
            m = mm(b[o:o + DH, 0:len(seqs) * n], W2[:, 0, :], hid)
        else:
            for q, s in enumerate(seqs):
                m = mm(b[0:n, q * DH:(q + 1) * DH], hid[:, q * n:(q + 1) * n], W2[:, 1, :])
        m.then_inc(v_full, 1)

    def act_turn(tiles, slot):
        for third in (0, 2):
            AC.wait_ge(a_full, a.filled())
            b = a.take()
            (src, dst, g), (src2, dst2, g2) = halves(third)
            AC.copy(XT[dst, g, slot, 0:tiles * P], b[src, 0:tiles * P])
            AC.copy(XT[dst2, g2, slot, 0:tiles * P], b[src2, 0:tiles * P]).then_inc(a_free, 1)
        AC.wait_ge(a_free, a.emptied())

    def dve_turn(tiles, slot):
        V.wait_ge(v_full, v.filled())
        b = v.take()
        (src, dst, g), (src2, dst2, g2) = halves(1)
        V.tensor_copy(XT[dst, g, slot, 0:tiles * P], b[src, 0:tiles * P])
        V.tensor_copy(XT[dst2, g2, slot, 0:tiles * P], b[src2, 0:tiles * P]).then_inc(v_free, 1)

    def act_windows(z, w, hb):
        AC.wait_ge(a_full, a.filled())
        b = a.take()
        AC.activation(HID[:, hb, 0:w], b[:, 0:w], ACT.Gelu_apprx_tanh, bias=CB[:, z:z + 1]).then_inc(a_free, 1)

    def dve_summaries(z, g, seqs, n):
        V.wait_ge(v_full, v.filled())
        b = v.take()
        ns = len(seqs)
        if z == 0:
            o = 64 * (g % 2)
            V.tensor_copy(CKT[o:o + DH, g // 2, seqs[0]:seqs[0] + ns, 0:n],
                                    b[o:o + DH, 0:ns * n].rearrange("p (s n) -> p s n", n=n)).then_inc(v_free, 1)
        else:
            V.tensor_copy(CV[0:n, seqs[0]:seqs[0] + ns, g * DH:(g + 1) * DH],
                                    b[0:n, 0:ns * DH].rearrange("p (s d) -> p s d", d=DH)).then_inc(v_free, 1)

    def pe_cmp():
        PE.wait_ge(sem("cmp_w"), nth("PE", "cmp_w", 16 * 3))
        for z in range(2):
            PE.wait_ge(v_free, v.room())
            b = v.claim()
            for m in range(16):
                i = mm(b[0:1, 0:P], PE_T[:, z, m:m + 1], W1[:, z, m, :], m == 0, m == 15)
            i.then_inc(v_full, 1)
        PE.wait_ge(v_free, v.all_free())
        PE.wait_ge(v_free, v.room())
        b = v.claim()
        for z in range(2):
            i = tr(b[:, z:z + 1], CBR[0:1, z, :])
        i.then_inc(v_full, 1)
        n = 0
        hb = 0
        for z in range(2):
            for half in range(2):
                for s in range(4):
                    PE.wait_ge(sem(f"xr{n % NXR}"), nth("PE", f"xr{n % NXR}", 16 * NPG))
                    pe_turn(n, 4, s)
                    n += 1
                if z and half:
                    pe_keys()
                PE.wait_ge(a_free, a.all_free())
                PE.wait_ge(v_free, v.all_free())
                for g in range(G):
                    pe_windows(z, g, 1, 4, 4 * NCS, NCS)
                    PE.wait_ge(a_free, a.all_free())
                    pe_summaries(z, HID[:, hb % 2, 0:4 * NCS], g, range(4 * half, 4 * half + 4), NCS)
                    hb += 1
            PE.wait_ge(sem(f"xr{n % NXR}"), nth("PE", f"xr{n % NXR}", 16))
            pe_turn(n, 1, 0)
            n += 1
            PE.wait_ge(a_free, a.all_free())
            PE.wait_ge(v_free, v.all_free())
            pe_windows(z, 0, G, 1, G * NCP, NCP)
            PE.wait_ge(a_free, a.all_free())
            for g in range(G):
                pe_summaries(z, HID[:, hb % 2, g * NCP:(g + 1) * NCP], g, [8], NCP)
            hb += 1
        PE.wait_ge(sem("cksq"), nth("PE", "cksq"))
        for c in range(2):
            pp = P if c == 0 else DH
            PE.wait_ge(v_free, v.room())
            b = v.claim()
            PE.wait_ge(v_free, v.room())
            b2 = v.claim()
            mm(b[0:pp, 0:NB * NCS], C("headones", pp)[:, 0:pp], XT[0:pp, c, 0, 0:NB * NCS]).then_inc(v_full, 1)
            mm(b2[0:pp, 0:NCP], C("headones", pp)[:, 0:pp], XT[0:pp, c, 1, 0:NCP]).then_inc(v_full, 1)

    def act_cmp():
        hb = 0
        AC.wait_ge(sem("cmp_bias"), nth("ACT", "cmp_bias"))
        for z in range(2):
            for half in range(2):
                for s in range(4):
                    act_turn(4, s)
                    if (z, half, s) == (1, 0, 0):
                        rsqrt_act(ST[:, 10:28])
                    AC.copy(ST[:, 30:31], ST[:, 31:32]).then_inc(sem("xr_used"), 1)
                for g in range(G):
                    act_windows(z, 4 * NCS, hb % 2)
                    hb += 1
            act_turn(1, 0)
            AC.copy(ST[:, 30:31], ST[:, 31:32]).then_inc(sem("xr_used"), 1)
            act_windows(z, G * NCP, hb % 2)
            hb += 1
        for c in range(2):
            pp = P if c == 0 else DH
            rsqrt_act(XT[0:pp, c, 2:4, :].rearrange("p a b -> p (a b)")[:, 0:NB * NCS + NCP])

    def dve_cmp():
        for z in range(2):
            V.wait_ge(v_full, v.filled())
            b = v.take()
            V.tensor_copy(CBR[0:1, z, :], b[0:1, 0:P]).then_inc(v_free, 1)
        V.wait_ge(v_full, v.filled())
        b = v.take()
        tt(CB[:, :], b[:, 0:2], PAR[:, CB1:CB1 + 2], ALU.add).then_inc(v_free, 1)
        V.memset(ST[:, 8:9], 0.0).then_inc(sem("cmp_bias"), 1)
        V.wait_ge(sem("cmp_bias"), nth("DVE", "cmp_bias"))
        for z in range(2):
            for half in range(2):
                for s in range(4):
                    dve_turn(4, s)
                    dve_norms(8 * z + 4 * half + s)
                if z and half:
                    dve_keys()
                for g in range(G):
                    dve_summaries(z, g, range(4 * half, 4 * half + 4), NCS)
            dve_turn(1, 0)
            for g in range(G):
                dve_summaries(z, g, [8], NCP)
        for c in range(2):
            pp = P if c == 0 else DH
            s8 = XT[0:pp, c, 0, 0:NB * NCS].rearrange("p (s n) -> p s n", n=NCS)
            tt(s8, CKT[0:pp, c, 0:NB, 0:NCS], CKT[0:pp, c, 0:NB, 0:NCS], ALU.mult)
            tt(XT[0:pp, c, 1, 0:NCP], CKT[0:pp, c, 8, 0:NCP], CKT[0:pp, c, 8, 0:NCP], ALU.mult)
        V.memset(ST[:, 8:9], 0.0).then_inc(sem("cksq"), 1)
        V.wait_ge(sem("cksq"), nth("DVE", "cksq"))
        for c in range(2):
            pp = P if c == 0 else DH
            r = XT[0:pp, c, 2:4, :].rearrange("p a b -> p (a b)")[:, 0:NB * NCS + NCP]
            V.wait_ge(v_full, v.filled())
            b = v.take()
            V.tensor_copy(r[:, 0:NB * NCS], b[0:pp, 0:NB * NCS]).then_inc(v_free, 1)
            V.wait_ge(v_free, v.emptied())
            V.wait_ge(v_full, v.filled())
            b = v.take()
            V.tensor_copy(r[:, NB * NCS:], b[0:pp, 0:NCP]).then_inc(v_free, 1)
            V.wait_ge(v_free, v.emptied())
            rsqrt_dve(r, 1.0 / DH, 1e-6)
            k8, r8 = CKT[0:pp, c, 0:NB, 0:NCS], r[:, 0:NB * NCS].rearrange("p (s n) -> p s n", n=NCS)
            stt(k8, k8, PAR[0:pp, KG0:KG0 + 1], r8, ALU.mult, ALU.mult)
            k1 = CKT[0:pp, c, 8, 0:NCP]
            stt(k1, k1, PAR[0:pp, KG0:KG0 + 1], r[:, NB * NCS:], ALU.mult, ALU.mult)
        V.memset(ST[:, 8:9], 0.0).then_inc(sem("ck"), 1)
        V.wait_ge(sem("ck"), nth("DVE", "ck"))

    def gate(i, h, z):
        n = TILES[i][1]
        return KV[0:n, i, 6 * KVW + 3 * h + z:6 * KVW + 3 * h + z + 1]

    def qh(h, t0, n):
        o = 64 * (h % 2)
        return QT[o:o + DH, h // 2, t0:t0 + n]

    def pe_keys():
        PE.wait_ge(sem("kv"), nth("PE", "kv"))
        for z in range(2):
            c0 = (2 + 2 * z) * KVW
            for c in range(2):
                w = P if c == 0 else DH
                PE.wait_ge(v_free, v.room())
                b = v.claim()
                for i in range(2):
                    m = tr(b[0:w, i * P:(i + 1) * P], KV[:, i, c0 + c * P:c0 + c * P + w])
                m.then_inc(v_full, 1)
            PE.wait_ge(v_free, v.room())
            b = v.claim()
            tr(b[:, 0:NB], KV[0:NB, 2, c0:c0 + P])
            tr(b[0:DH, NB:2 * NB], KV[0:NB, 2, c0 + P:c0 + KVW]).then_inc(v_full, 1)

    def pe_prompt():
        PE.wait_ge(sem("ck2"), nth("PE", "ck2"))
        for i in range(2):
            for odd in range(2):
                PE.wait_ge(v_free, v.room())
                b = v.claim()
                for h in range(odd, H, 2):
                    m = mm(b[:, h // 2 * NCP:(h // 2 + 1) * NCP], qh(h, i * P, P), CK2[64 * odd:64 * odd + DH, h // HG, :])
                m.then_inc(v_full, 1)
        PE.wait_ge(sem("cs"), nth("PE", "cs"))
        for i in range(2):
            for q in range(3):
                PE.wait_ge(v_free, v.room())
                b = v.claim()
                for h in range(4 * q, 4 * q + 4):
                    m = tr(b[0:NCP, (h % 4) * P:(h % 4 + 1) * P], CS[:, i, h * NCP:(h + 1) * NCP])
                m.then_inc(v_full, 1)
        for u in range(UNITS_P + 3):
            if u < UNITS_P:
                h, i, o, g, s = unit(u)
                PE.wait_ge(v_free, v.room())
                b = v.claim()
                for z in range(2):
                    m = mm(b[:, z * SEQ:z * SEQ + s], qh(h, i * P, P), KT[o:o + DH, z, g, 0:s])
                m.then_inc(v_full, 1)
            if u >= 3:
                h, i, o, g, s = unit(u - 3)
                PE.wait_ge(a_free, a.all_free())
                PE.wait_ge(v_free, v.room())
                b = v.claim()
                pt = PPT[:, (u - 3) % 2, :]
                mm(b[o:o + DH, 0:P], CV[0:NCP, 8, g * DH:(g + 1) * DH], CPT[0:NCP, i * H + h, :], True, False)
                for z in range(2):
                    c0 = (3 + 2 * z) * KVW + g * DH
                    for k in range(i + 1):
                        m = mm(b[o:o + DH, 0:P], KV[:, k, c0:c0 + DH], pt[:, z * SEQ + k * P:z * SEQ + (k + 1) * P],
                               False, z == 1 and k == i)
                m.then_inc(v_full, 1)
            if 2 <= u < UNITS_P + 2:
                h, i, o, g, s = unit(u - 2)
                PE.wait_ge(sem("probs"), nth("PE", "probs"))
                PE.wait_ge(a_free, a.room())
                b = a.claim()
                pp = PP[:, (u - 2) % 3, :]
                for z in range(2):
                    for k in range(i + 1):
                        c = slice(z * SEQ + k * P, z * SEQ + (k + 1) * P)
                        m = tr(b[:, c], pp[:, c])
                m.then_inc(a_full, 1)

    UNITS_P = 2 * H

    def unit(u):
        h, i = u // 2, u % 2
        return h, i, 64 * (h % 2), h // HG, (i + 1) * P

    def act_prompt():
        AC.wait_ge(sem("cs_max"), nth("ACT", "cs_max"))
        for i in range(2):
            ins = AC.activation(CS[:, i, :], CS[:, i, :], ACT.Exp)
            if i == 0:
                ins
            else:
                ins.then_inc(sem("cs_exp"), 1)
                AC.wait_ge(sem("cs_exp"), nth("ACT", "cs_exp"))
        for u in range(UNITS_P + 2):
            if u < UNITS_P:
                h, i, o, g, s = unit(u)
                AC.wait_ge(sem("pmax"), nth("ACT", "pmax"))
                pp, st = PP[:, u % 3, :], ST[:, 40 + 4 * (u % 2):44 + 4 * (u % 2)]
                for z in range(2):
                    r = pp[:, z * SEQ:z * SEQ + s]
                    ins = AC.activation(r, r, ACT.Exp, bias=st[:, z:z + 1], accum_out=st[:, 2 + z:3 + z])
                ins.then_inc(sem("pexp"), 1)
            if u >= 2:
                h, i, o, g, s = unit(u - 2)
                AC.wait_ge(a_full, a.filled())
                b = a.take()
                AC.copy(PPT[:, u % 2, :].rearrange("p (z s) -> p z s", z=2)[:, :, 0:s],
                        b[:, :].rearrange("p (z s) -> p z s", z=2)[:, :, 0:s]).then_inc(a_free, 1)

    def dve_keys():
        for z in range(2):
            for c in range(2):
                V.wait_ge(v_full, v.filled())
                b = v.take()
                for g in (0, 1) if c == 0 else (2,):
                    o = 64 * (g % 2)
                    V.tensor_copy(KT[0:DH, z, g, :], b[o:o + DH, 0:SEQ])
                    ins = V.tensor_copy(KT[DH:P, z, g, :], b[o:o + DH, 0:SEQ])
                    if g:
                        ins.then_inc(v_free, 1)
                    else:
                        ins
            V.wait_ge(v_full, v.filled())
            b = v.take()
            V.tensor_copy(KNEW[:, z, 0, :], b[:, 0:NB])
            V.tensor_copy(KNEW[0:DH, z, 1, :], b[0:DH, NB:2 * NB]).then_inc(v_free, 1)

    def dve_prompt():
        for g in range(G):
            o = 64 * (g % 2)
            for hf in range(2):
                V.tensor_copy(CK2[64 * hf:64 * hf + DH, g, :], CKT[o:o + DH, g // 2, 8, 0:NCP])
        V.memset(ST[:, 8:9], 0.0).then_inc(sem("ck2"), 1)
        V.wait_ge(sem("ck2"), nth("DVE", "ck2"))
        for i in range(2):
            for odd in range(2):
                V.wait_ge(v_full, v.filled())
                b = v.take()
                half = lambda ap: ap.rearrange("p (h two n) -> p h two n", two=2, n=NCP)[:, :, odd, :]
                tt(half(CS[:, i, :]), b[:, 0:H // 2 * NCP].rearrange("p (h n) -> p h n", n=NCP),
                             half(C("cmpbias")[:, i * H * NCP:(i + 1) * H * NCP]), ALU.add).then_inc(v_free, 1)
                V.wait_ge(v_free, v.emptied())
        for i in range(2):
            c3 = CS[:, i, :].rearrange("p (h n) -> p h n", h=H)
            mx = ST[:, 44:56]
            V.tensor_reduce(mx, c3, AX_X, ALU.max).then_inc(dve_done, 1)
            V.wait_ge(dve_done, nth("DVE", "dve_done"))
            tt(c3, c3, mx.unsqueeze(2).broadcast_to([P, H, NCP]), ALU.subtract).then_inc(dve_done, 1)
            V.wait_ge(dve_done, nth("DVE", "dve_done"))
        V.memset(ST[:, 8:9], 0.0).then_inc(sem("cs_max"), 1)
        V.wait_ge(sem("cs_max"), nth("DVE", "cs_max"))
        V.wait_ge(sem("cs_exp"), nth("DVE", "cs_exp"))
        for i in range(2):
            c3 = CS[:, i, :].rearrange("p (h n) -> p h n", h=H)
            ms = C("cmpmask")[:, i * NCP:(i + 1) * NCP].unsqueeze(1).broadcast_to([P, H, NCP])
            sm = ST[:, 44:56]
            tt(c3, c3, ms, ALU.mult).then_inc(dve_done, 1)
            V.wait_ge(dve_done, nth("DVE", "dve_done"))
            V.tensor_reduce(sm, c3, AX_X, ALU.add).then_inc(dve_done, 1)
            V.wait_ge(dve_done, nth("DVE", "dve_done"))
            ts(sm, sm, 1e-30, None, ALU.max).then_inc(dve_done, 1)
            V.wait_ge(dve_done, nth("DVE", "dve_done"))
            V.reciprocal(sm, sm).then_inc(dve_done, 1)
            V.wait_ge(dve_done, nth("DVE", "dve_done"))
            if i == 0:
                V.wait_ge(sem("gates"), nth("DVE", "gates"))
            gt = KV[:, i, 6 * KVW:KVN].rearrange("p (h z) -> p h z", z=3)[:, :, 0]
            tt(sm, sm, gt, ALU.mult).then_inc(dve_done, 1)
            V.wait_ge(dve_done, nth("DVE", "dve_done"))
            tt(c3, c3, sm.unsqueeze(2).broadcast_to([P, H, NCP]), ALU.mult)
        V.memset(ST[:, 8:9], 0.0).then_inc(sem("cs"), 1)
        V.wait_ge(sem("cs"), nth("DVE", "cs"))
        for i in range(2):
            for q in range(3):
                V.wait_ge(v_full, v.filled())
                b = v.take()
                V.tensor_copy(CPT[0:NCP, i * H + 4 * q:i * H + 4 * q + 4, :],
                                        b[0:NCP, :].rearrange("p (h t) -> p h t", h=4)).then_inc(v_free, 1)
        for u in range(UNITS_P + 3):
            if u < UNITS_P:
                h, i, o, g, s = unit(u)
                st = ST[:, 40 + 4 * (u % 2):44 + 4 * (u % 2)]
                V.wait_ge(v_full, v.filled())
                b = v.take()
                pv = PP[:, u % 3, :].rearrange("p (z s) -> p z s", z=2)[:, :, 0:s]
                dist = C("distp").rearrange("p (i s) -> p i s", i=2)[:, i:i + 1, 0:s].broadcast_to([P, 2, s])
                stt(pv, dist, float(SLOPES[h]), b[:, :].rearrange("p (z s) -> p z s", z=2)[:, :, 0:s],
                    ALU.mult, ALU.add).then_inc(v_free, 1)
                V.wait_ge(v_free, v.emptied())
                V.tensor_reduce(st[:, 0:2], pv, AX_X, ALU.max, negate=True).then_inc(sem("pmax"), 1)
            if 1 <= u < UNITS_P + 1:
                h, i, o, g, s = unit(u - 1)
                st = ST[:, 40 + 4 * ((u - 1) % 2):44 + 4 * ((u - 1) % 2)]
                V.wait_ge(sem("pexp"), nth("DVE", "pexp"))
                V.reciprocal(st[:, 2:4], st[:, 2:4]).then_inc(dve_done, 1)
                V.wait_ge(dve_done, nth("DVE", "dve_done"))
                tt(st[:, 2:4], st[:, 2:4], KV[:, i, 6 * KVW + 3 * h + 1:6 * KVW + 3 * h + 3], ALU.mult).then_inc(dve_done, 1)
                V.wait_ge(dve_done, nth("DVE", "dve_done"))
                pv = PP[:, (u - 1) % 3, :].rearrange("p (z s) -> p z s", z=2)[:, :, 0:s]
                tt(pv, pv, st[:, 2:4].unsqueeze(2).broadcast_to([P, 2, s]), ALU.mult).then_inc(sem("probs"), 1)
            if u >= 3:
                h, i, o, g, s = unit(u - 3)
                V.wait_ge(v_full, v.filled())
                b = v.take()
                V.tensor_copy(MIXT[o:o + DH, h // 2, i * P:(i + 1) * P], b[o:o + DH, 0:P]).then_inc(v_free, 1)

    NS = PAST + 1
    NW = WIN + 1
    S_SEL, S_WIN, S_CMP = slice(0, NS), slice(NS, NS + NW), slice(NS + NW, NS + NW + NCS)

    NOLD = len(OLD)

    def sp_sample():
        nc.sync.wait_ge(sem("ck"), nth("SP", "ck"))
        for n in range(2 * NB):
            s, nm = n % NB, "k" if n < NB else "v"
            if n >= NOLD:
                used = "keys_used" if n - NOLD < NB else "v_used"
                nc.sync.wait_ge(sem(used), nth("SP", used))
            pool = A["cache_sel_" + nm][0].rearrange("n p g d -> n p (g d)")
            for pg in range(NPG):
                page = nc.sync.value_load(PGT[0:1, s * NPG + pg:s * NPG + pg + 1], min_val=0, max_val=79)
                nc.sync.dma_start(OLD[n % NOLD][:, pg, :],
                                  pool[bass.ds(page, 1)].rearrange("n p c -> (n p) c")).then_inc(sem(f"old{n % NOLD}"), 16)
            nc.sync.dma_start(OLD[n % NOLD][:, NPG:NPG + 4, :],
                              A["cache_win_" + nm][0, s].rearrange("(t p) g d -> p t (g d)", p=P)).then_inc(
                                  sem(f"old{n % NOLD}"), 16)

    def pe_sample_scores():
        PE.wait_ge(sem("qbd"), nth("PE", "qbd"))
        PE.wait_ge(v_free, v.room())
        b3 = v.claim()
        for s in range(NB):
            mm(b3[0:RS, 0:NCS], QBD[:, 0, s, :], CKT[:, 0, s, 0:NCS], s == 0, False)
            m = mm(b3[0:RS, 0:NCS], QBD[0:DH, 1, s, :], CKT[0:DH, 1, s, 0:NCS], False, s == NB - 1)
        for z in range(2):
            for s in range(NB):
                mm(b3[0:RS, 64 + z:65 + z], QBD[:, 0, s, :], KNEW[:, z, 0, s:s + 1], s == 0, False)
                m = mm(b3[0:RS, 64 + z:65 + z], QBD[0:DH, 1, s, :], KNEW[0:DH, z, 1, s:s + 1], False, s == NB - 1)
        m.then_inc(v_full, 1)
        bs = []
        for _ in range(3):
            PE.wait_ge(v_free, v.room())
            bs.append(v.claim())
        for s in range(NB + 1):
            if s < NB:
                old = f"old{s % NOLD}"
                PE.wait_ge(sem(old), nth("PE", old, 16 * (NPG + 1)))
                for c in range(2):
                    w = P if c == 0 else DH
                    for q in range(3):
                        PE.wait_ge(a_free, a.room())
                        b = a.claim()
                        for t in range(4):
                            m = tr(b[0:w, t * P:(t + 1) * P], OLD[s % NOLD][:, 4 * q + t, c * P:c * P + w])
                        m.then_inc(a_full, 1)
            if s:
                PE.wait_ge(a_free, a.all_free(6 if s < NB else 0))
                for c in range(2):
                    w = P if c == 0 else DH
                    for q in range(3):
                        m = mm(bs[q][0:RS, :], QBD[0:w, c, s - 1, :], KTS[(s - 1) % 2][0:w, c, q * 512:(q + 1) * 512],
                               s == 1 and c == 0, s == NB and c == 1)
                        if s == NB and c == 1:
                            m.then_inc(v_full, 1)

    def act_sample_scores():
        for s in range(NB):
            for c in range(2):
                w = P if c == 0 else DH
                for q in range(3):
                    AC.wait_ge(a_full, a.filled())
                    b = a.take()
                    AC.copy(KTS[s % 2][0:w, c, q * 512:(q + 1) * 512], b[0:w, :]).then_inc(a_free, 1)
            AC.copy(ST[:, 30:31], ST[:, 31:32]).then_inc(sem("keys_used"), 1)

    def dve_sample_scores():
        V.memset(QBD[:, :, :, :], 0.0).then_inc(dve_done, 1)
        V.wait_ge(dve_done, nth("DVE", "dve_done"))
        for h in range(H):
            g = h // HG
            o, src = 64 * (g % 2), 64 * (h % 2)
            rows = QBD[o:o + DH, g // 2, :, :].rearrange("p b r -> p (b r)")
            V.tensor_copy(rows[:, h:h + (RS + H) * (NB - 1) + 1:RS + H], QT[src:src + DH, h // 2, SEQ:NT])
        V.memset(ST[:, 8:9], 0.0).then_inc(sem("qbd"), 1)
        V.wait_ge(sem("qbd"), nth("DVE", "qbd"))
        sl = C("slope", RS)
        V.wait_ge(v_full, v.filled())
        b3 = v.take()
        stt(SS[0:RS, S_CMP], C("cpos", RS), sl, b3[0:RS, 0:NCS], ALU.mult, ALU.add)
        V.tensor_copy(SS[0:RS, NS - 1:NS], b3[0:RS, 64:65])
        V.tensor_copy(SS[0:RS, NS + NW - 1:NS + NW], b3[0:RS, 65:66]).then_inc(v_free, 1)
        pos = C("pos", RS)
        for q in range(3):
            V.wait_ge(v_full, v.filled())
            b = v.take()
            o, c = (512 * q, 512 * q) if q < 2 else (NS, PAST - WIN)
            stt(SS[0:RS, o:o + 512], pos[:, c:c + 512], sl, b[0:RS, :], ALU.mult, ALU.add).then_inc(v_free, 1)
        V.memset(ST[:, 8:9], 0.0).then_inc(sem("mem_go"), 1)
        V.wait_ge(sem("mem_go"), nth("DVE", "mem_go"))

        sm = SMALL
        soft(S_CMP, 0)
        V.reciprocal(sm[0:RS, 8:9], sm[0:RS, 4:5]).then_inc(dve_done, 1)
        V.wait_ge(dve_done, nth("DVE", "dve_done"))
        ts(SS[0:RS, S_CMP], SS[0:RS, S_CMP], sm[0:RS, 8:9], None, ALU.mult).then_inc(sem("pc"), 1)
        V.wait_ge(sem("pc"), nth("DVE", "pc"))
        V.wait_ge(v_full, v.filled())
        b = v.take()
        V.tensor_copy(SPT[0:NCS, 12, :], b[0:NCS, 0:RS]).then_inc(v_free, 1)
        V.wait_ge(v_full, v.filled())
        b = v.take()
        V.tensor_copy(sm[0:RS, 16:16 + NSEL], b[0:RS, 0:NSEL]).then_inc(v_free, 1)
        V.wait_ge(v_full, v.filled())
        b = v.take()
        V.tensor_copy(sm[0:RS, 40:40 + NSEL], b[0:RS, 0:NSEL]).then_inc(v_free, 1)
        V.wait_ge(v_free, v.emptied())
        nb = NSEL - 3
        imp, eq = sm[0:RS, 41:41 + nb], sm[0:RS, 60:60 + nb]
        V.tensor_reduce(sm[0:RS, 10:11], imp, AX_X, ALU.min).then_inc(dve_done, 1)
        V.wait_ge(dve_done, nth("DVE", "dve_done"))
        ts(eq, imp, sm[0:RS, 10:11], None, ALU.is_le).then_inc(dve_done, 1)
        V.wait_ge(dve_done, nth("DVE", "dve_done"))
        tt(eq, eq, C("blkno", RS), ALU.mult).then_inc(dve_done, 1)
        V.wait_ge(dve_done, nth("DVE", "dve_done"))
        V.tensor_reduce(sm[0:RS, 11:12], eq, AX_X, ALU.max).then_inc(dve_done, 1)
        V.wait_ge(dve_done, nth("DVE", "dve_done"))
        ts(sm[0:RS, 80:80 + nb], C("blkno", RS), sm[0:RS, 11:12], NEG, ALU.is_equal, ALU.mult).then_inc(dve_done, 1)
        V.wait_ge(dve_done, nth("DVE", "dve_done"))
        blocks = SS[0:RS, SEL:SEL * (nb + 1)].rearrange("p (n k) -> p n k", k=SEL)
        tt(blocks, blocks, sm[0:RS, 80:80 + nb].unsqueeze(2).broadcast_to([RS, nb, SEL]), ALU.add).then_inc(dve_done, 1)
        V.wait_ge(dve_done, nth("DVE", "dve_done"))
        soft(S_SEL, 1)
        soft(S_WIN, 2)
        V.reciprocal(sm[0:RS, 8:10], sm[0:RS, 5:7]).then_inc(dve_done, 1)
        V.wait_ge(dve_done, nth("DVE", "dve_done"))
        V.wait_ge(sem("gate_rows"), nth("DVE", "gate_rows", 16 * NB))
        tt(sm[0:RS, 8:10], sm[0:RS, 8:10], sm[0:RS, 13:15], ALU.mult).then_inc(dve_done, 1)
        V.wait_ge(dve_done, nth("DVE", "dve_done"))
        ts(SS[0:RS, S_SEL], SS[0:RS, S_SEL], sm[0:RS, 8:9], None, ALU.mult).then_inc(dve_done, 1)
        V.wait_ge(dve_done, nth("DVE", "dve_done"))
        ts(SS[0:RS, S_WIN], SS[0:RS, S_WIN], sm[0:RS, 9:10], None, ALU.mult).then_inc(dve_done, 1)
        V.wait_ge(dve_done, nth("DVE", "dve_done"))
        ts(SS[0:RS, S_CMP], SS[0:RS, S_CMP], sm[0:RS, 12:13], None, ALU.mult)
        for z, c in enumerate((NS - 1, NS + NW - 1)):
            ts(PDD[0:RS, z, :], ident[0:RS, 0:RS], SS[0:RS, c:c + 1], None, ALU.mult)
        V.memset(ST[:, 8:9], 0.0).then_inc(sem("ps"), 1)
        V.wait_ge(sem("ps"), nth("DVE", "ps"))
        for t in range(4):
            V.wait_ge(v_full, v.filled())
            b = v.take()
            n = min(4, 13 - 4 * t)
            w = P if t < 3 else NCS
            V.tensor_copy(SPT[0:w, 4 * t:4 * t + n, :], b[0:w, 0:n * RS].rearrange("p (a r) -> p a r", r=RS)).then_inc(v_free, 1)
        V.wait_ge(v_full, v.filled())
        b = v.take()
        V.tensor_copy(PD[0:NB, :, :], b[0:NB, 0:2 * RS].rearrange("p (a r) -> p a r", r=RS)).then_inc(v_free, 1)
        for s in range(NB):
            V.wait_ge(v_full, v.filled())
            b = v.take()
            V.tensor_copy(VO[:, s, :], b[:, 0:KVW]).then_inc(v_free, 1)
        V.wait_ge(v_full, v.filled())
        b = v.take()
        o = b[0:DH, 0:RS].rearrange("p (b c two) -> p c b two", b=NB, two=2)
        V.tensor_copy(MIXT[0:DH, 0:6, SEQ:NT], o[:, :, :, 0])
        V.tensor_copy(MIXT[DH:P, 0:6, SEQ:NT], o[:, :, :, 1]).then_inc(v_free, 1)

    def soft(cols, z):
        sm = SMALL
        V.tensor_reduce(sm[0:RS, z:z + 1], SS[0:RS, cols], AX_X, ALU.max).then_inc(dve_done, 1)
        V.wait_ge(dve_done, nth("DVE", "dve_done"))
        ts(sm[0:RS, z:z + 1], sm[0:RS, z:z + 1], -1.0, None, ALU.mult).then_inc(sem("smax"), 1)
        V.wait_ge(sem("smax"), nth("DVE", "smax"))
        V.wait_ge(sem("sexp"), nth("DVE", "sexp"))

    def act_soft(cols, z):
        AC.wait_ge(sem("smax"), nth("ACT", "smax"))
        AC.activation(SS[0:RS, cols], SS[0:RS, cols], ACT.Exp, bias=SMALL[0:RS, z:z + 1],
                                          accum_out=SMALL[0:RS, 4 + z:5 + z]).then_inc(sem("sexp"), 1)
        AC.wait_ge(sem("sexp"), nth("ACT", "sexp"))

    def act_sample():
        act_sample_scores()
        act_soft(S_CMP, 0)
        act_soft(S_SEL, 1)
        act_soft(S_WIN, 2)

    def pool_sample():
        nc.gpsimd.wait_ge(sem("gates"), nth("POOL", "gates"))
        nc.gpsimd.wait_ge(sem("qbd"), nth("POOL", "qbd"))
        g = KV[0:NB, 2, 6 * KVW:KVN].rearrange("b (h z) -> b h z", z=3)
        for s in range(NB):
            nc.gpsimd.dma_start(SMALL[s * H:(s + 1) * H, 12:15], g[s:s + 1, :, :]).then_inc(sem("gate_rows"), 16)

    PDD = place("PDD", 87000 // 32 * 32, [2, RS])

    def pe_sample_values():
        PE.wait_ge(sem("pc"), nth("PE", "pc"))
        PE.wait_ge(v_free, v.room())
        b = v.claim()
        tr(b[0:NCS, 0:RS], SS[0:RS, S_CMP]).then_inc(v_full, 1)
        PE.wait_ge(v_free, v.all_free())
        PE.wait_ge(v_free, v.room())
        b = v.claim()
        mm(b[0:RS, 0:NSEL], SPT[0:NCS, 12, :], C("cmpsel", NCS)).then_inc(v_full, 1)
        PE.wait_ge(v_free, v.all_free())
        PE.wait_ge(v_free, v.room())
        b = v.claim()
        mm(b[0:RS, 0:NSEL], C("samegroup", RS), SMALL[0:RS, 16:16 + NSEL]).then_inc(v_full, 1)
        PE.wait_ge(sem("ps"), nth("PE", "ps"))
        for t in range(4):
            PE.wait_ge(v_free, v.room())
            b = v.claim()
            for j in range(min(4, 13 - 4 * t)):
                k = 4 * t + j
                c0 = P * k if k < 8 else NS + P * (k - 8) if k < 12 else NS + NW
                w = P if k < 12 else NCS
                m = tr(b[0:w, j * RS:(j + 1) * RS], SS[0:RS, c0:c0 + w])
            m.then_inc(v_full, 1)
        PE.wait_ge(v_free, v.room())
        b = v.claim()
        for z in range(2):
            m = mm(b[0:NB, z * RS:(z + 1) * RS], C("rowseq", RS), PDD[0:RS, z, :])
        m.then_inc(v_full, 1)
        PE.wait_ge(v_free, v.all_free())
        PE.wait_ge(v_free, v.room())
        b = v.claim()
        for s in range(NB):
            if s:
                PE.wait_ge(v_free, v.room())
                b = v.claim()
            r = slice(ROW0[s], ROW0[s] + SLOT)
            items = [(SPT[0:NCS, 12, r], CV[0:NCS, s, :])]
            for z in range(2):
                c0 = (3 + 2 * z) * KVW
                items.append((PD[0:NB, z, r], KV[0:NB, 2, c0:c0 + KVW]))
            items += [(SPT[:, t, r], OLD[(NB + s) % NOLD][:, t, :]) for t in range(NPG + 4)]
            old = f"old{(NB + s) % NOLD}"
            for n, (probs, values) in enumerate(items):
                if n == 3:
                    PE.wait_ge(sem(old), nth("PE", old, 16 * (NPG + 1)))
                q = n % 4
                m = PE.matmul(b[q * SLOT:(q + 1) * SLOT, 0:KVW], lhsT=probs, rhs=values, start=n < 4,
                              stop=n >= len(items) - 4, skip_group_check=True)
                if n == 0 and s:
                    m.then_inc(sem("v_used"), 1)
            m.then_inc(v_full, 1)
        PE.wait_ge(v_free, v.all_free())
        PE.wait_ge(v_free, v.room())
        b = v.claim()
        for s in range(NB):
            for g in range(G):
                c = s * H - ROW0[s] + g * HG
                m = mm(b[0:DH, s * H + g * HG:s * H + (g + 1) * HG], VO[:, s, g * DH:(g + 1) * DH], C("fold")[:, c:c + HG])
        m.then_inc(v_full, 1)

    ROW0 = [min(s * H, RS - SLOT) for s in range(NB)]

    def mem_tiles(base):
        return dict(
            MK=place("MK", base, [2, 2, SEQ]), MV=place("MV", base + 4096, [2, 2, SEQ]),
            MQ=place("MQ", base + 8192, [2, NB, NB * MH]), MS=place("MS", base + 10240, [SEQ]),
            MPT=place("MPT", base + 11264, [2, SEQ]), MST=place("MST", base + 13312, [2, NB * MH]),
            MP=place("MP", base + 13568, [2, 2, SEQ]), MKT=place("MKT", base + 17664, [NB, 2, SEQ]))

    MTL = [mem_tiles(58304), mem_tiles(50112)]
    RM = NB * MH

    def sp_memattn(l):
        m = MTL[l]
        nc.sync.wait_ge(sem("mem_go"), nth("SP", "mem_go"))
        for z, nm in enumerate(("k", "v")):
            for s in range(NB):
                if s >= 2:
                    nc.sync.wait_ge(sem(f"m{nm}_used"), nth("SP", f"m{nm}_used"))
                nc.sync.dma_start(m["MK" if z == 0 else "MV"][:, s % 2, :, :],
                    A["cache_mem_" + nm][l, s].rearrange("(t p) h d -> p t (h d)", p=P)).then_inc(sem(f"m{nm}{s % 2}"), 16)
            nth("SP", f"m{nm}_used", 2 - z)

    def pe_memattn(l):
        T, KVM, q0 = MTL[l], KVMS[l], 6 if l == 0 else 0
        PE.wait_ge(sem("mq"), nth("PE", "mq"))
        for u in range(NB):
            if 2 <= u < MH + 2:
                h = u - 2
                o = 64 * (h % 2)
                PE.wait_ge(v_free, v.all_free())
                PE.wait_ge(v_free, v.room())
                b = v.claim()
                for t in range(2):
                    m = mm(b[o:o + DH, 0:SEQ], KVM[:, t, MEMQ + h * DH:MEMQ + (h + 1) * DH], T["MPT"][:, t, :], t == 0, t == 1)
                m.then_inc(v_full, 1)
            if u < MH:
                o = 64 * (u % 2)
                PE.wait_ge(v_free, v.room())
                b = v.claim()
                for i in range(2):
                    m = mm(b[:, i * SEQ:(i + 1) * SEQ], QT[o:o + DH, q0 + u // 2, i * P:(i + 1) * P], KMT[o:o + DH, u // 2, :])
                m.then_inc(v_full, 1)
            PE.wait_ge(sem(f"mk{u % 2}"), nth("PE", f"mk{u % 2}", 16))
            PE.wait_ge(a_free, a.room())
            b = a.claim()
            for c in range(2):
                for t in range(2):
                    m = tr(b[:, c * SEQ + t * P:c * SEQ + (t + 1) * P], T["MK"][:, u % 2, t, c * P:(c + 1) * P])
            m.then_inc(a_full, 1)
            if 1 <= u < MH + 1:
                PE.wait_ge(sem("mprobs"), nth("PE", "mprobs"))
                PE.wait_ge(v_free, v.room())
                b = v.claim()
                for t in range(2):
                    for i in range(2):
                        m = tr(b[:, (2 * t + i) * P:(2 * t + i + 1) * P], T["MP"][:, (u - 1) % 2, i, t * P:(t + 1) * P])
                m.then_inc(v_full, 1)
        PE.wait_ge(a_free, a.all_free())
        PE.wait_ge(v_free, v.room())
        b = v.claim()
        for s in range(NB):
            for c in range(2):
                m = mm(b[0:RM, 0:SEQ], T["MQ"][:, c, s, :], T["MKT"][:, s, c, :], s == 0 and c == 0, s == NB - 1 and c == 1)
        m.then_inc(v_full, 1)
        PE.wait_ge(sem("msprobs"), nth("PE", "msprobs"))
        PE.wait_ge(v_free, v.room())
        b = v.claim()
        for t in range(2):
            m = tr(b[:, t * RM:(t + 1) * RM], T["MS"][0:RM, t * P:(t + 1) * P])
        m.then_inc(v_full, 1)
        PE.wait_ge(v_free, v.all_free())
        PE.wait_ge(v_free, v.room())
        b = v.claim()
        for s in range(NB):
            PE.wait_ge(sem(f"mv{s % 2}"), nth("PE", f"mv{s % 2}", 16))
            for h in range(MH):
                r = s * MH + h
                for t in range(2):
                    m = mm(b[0:DH, r:r + 1], T["MV"][:, s % 2, t, h * DH:(h + 1) * DH], T["MST"][:, t, r:r + 1], t == 0, t == 1)
            if s < NB - 1:
                m.then_inc(sem("mv_used"), 1)
            else:
                m.then_inc(v_full, 1)

    def act_memattn(l):
        T = MTL[l]
        for u in range(NB):
            if u < MH:
                AC.wait_ge(sem("mmax"), nth("ACT", "mmax"))
                st = ST[:, 40 + 4 * (u % 2):44 + 4 * (u % 2)]
                for i in range(2):
                    r = T["MP"][:, u % 2, i, :]
                    ins = AC.activation(r, r, ACT.Exp, bias=st[:, i:i + 1], scale=DH ** -0.5, accum_out=st[:, 2 + i:3 + i])
                ins.then_inc(sem("mexp"), 1)
            AC.wait_ge(a_full, a.filled())
            b = a.take()
            AC.copy(T["MKT"][:, u, :, :].rearrange("p c m -> p (c m)"), b[:, :]).then_inc(a_free, 1)
            AC.wait_ge(a_free, a.emptied())
            AC.copy(ST[:, 30:31], ST[:, 31:32]).then_inc(sem("mk_used"), 1)
        AC.wait_ge(sem("msmax"), nth("ACT", "msmax"))
        AC.activation(T["MS"][0:RM, :], T["MS"][0:RM, :], ACT.Exp, bias=ST[0:RM, 40:41],
                                           accum_out=ST[0:RM, 42:43]).then_inc(sem("msexp"), 1)
        AC.wait_ge(sem("msexp"), nth("ACT", "msexp"))

    def dve_memattn(l):
        T, q0 = MTL[l], 6 if l == 0 else 0
        if l:
            V.memset(ST[:, 8:9], 0.0).then_inc(sem("mem_go"), 1)
            V.wait_ge(sem("mem_go"), nth("DVE", "mem_go"))
        V.memset(T["MQ"][:, :, :, :], 0.0).then_inc(dve_done, 1)
        V.wait_ge(dve_done, nth("DVE", "dve_done"))
        for h in range(MH):
            o = 64 * (h % 2)
            rows = T["MQ"][o:o + DH, h // 2, :, :].rearrange("p b r -> p (b r)")
            V.tensor_copy(rows[:, h:h + (RM + MH) * (NB - 1) + 1:RM + MH], QT[o:o + DH, q0 + h // 2, SEQ:NT])
        V.memset(ST[:, 8:9], 0.0).then_inc(sem("mq"), 1)
        V.wait_ge(sem("mq"), nth("DVE", "mq"))
        for u in range(MH + 2):
            if u >= 2:
                h = u - 2
                o = 64 * (h % 2)
                V.wait_ge(v_full, v.filled())
                b = v.take()
                V.tensor_copy(MIXT[o:o + DH, 6 + h // 2, 0:SEQ], b[o:o + DH, 0:SEQ]).then_inc(v_free, 1)
            if 1 <= u < MH + 1:
                st = ST[:, 40 + 4 * ((u - 1) % 2):44 + 4 * ((u - 1) % 2)]
                mp = T["MP"][:, (u - 1) % 2, :, :]
                V.wait_ge(sem("mexp"), nth("DVE", "mexp"))
                V.reciprocal(st[:, 2:4], st[:, 2:4]).then_inc(dve_done, 1)
                V.wait_ge(dve_done, nth("DVE", "dve_done"))
                tt(mp, mp, st[:, 2:4].unsqueeze(2).broadcast_to([P, 2, SEQ]), ALU.mult).then_inc(sem("mprobs"), 1)
            if u < MH:
                st = ST[:, 40 + 4 * (u % 2):44 + 4 * (u % 2)]
                V.wait_ge(v_full, v.filled())
                b = v.take()
                V.tensor_copy(T["MP"][:, u % 2, :, :].rearrange("p i m -> p (i m)"), b[:, :]).then_inc(v_free, 1)
                V.wait_ge(v_free, v.emptied())
                V.tensor_reduce(st[:, 0:2], T["MP"][:, u % 2, :, :], AX_X, ALU.max).then_inc(dve_done, 1)
                V.wait_ge(dve_done, nth("DVE", "dve_done"))
                ts(st[:, 0:2], st[:, 0:2], -(DH ** -0.5), None, ALU.mult).then_inc(sem("mmax"), 1)
            if 1 <= u < MH + 1:
                V.wait_ge(v_full, v.filled())
                b = v.take()
                V.tensor_copy(T["MPT"][:, :, :].rearrange("p i m -> p (i m)"), b[:, :]).then_inc(v_free, 1)
        V.wait_ge(v_full, v.filled())
        b = v.take()
        MS = T["MS"]
        ts(MS[0:RM, :], b[0:RM, 0:SEQ], DH ** -0.5, None, ALU.mult).then_inc(v_free, 1)
        V.wait_ge(v_free, v.emptied())
        V.tensor_reduce(ST[0:RM, 40:41], MS[0:RM, :], AX_X, ALU.max).then_inc(dve_done, 1)
        V.wait_ge(dve_done, nth("DVE", "dve_done"))
        ts(ST[0:RM, 40:41], ST[0:RM, 40:41], -1.0, None, ALU.mult).then_inc(sem("msmax"), 1)
        V.wait_ge(sem("msmax"), nth("DVE", "msmax"))
        V.wait_ge(sem("msexp"), nth("DVE", "msexp"))
        V.reciprocal(ST[0:RM, 42:43], ST[0:RM, 42:43]).then_inc(dve_done, 1)
        V.wait_ge(dve_done, nth("DVE", "dve_done"))
        ts(MS[0:RM, :], MS[0:RM, :], ST[0:RM, 42:43], None, ALU.mult).then_inc(sem("msprobs"), 1)
        V.wait_ge(sem("msprobs"), nth("DVE", "msprobs"))
        V.wait_ge(v_full, v.filled())
        b = v.take()
        V.tensor_copy(T["MST"][:, :, :].rearrange("p i m -> p (i m)"), b[:, 0:2 * RM]).then_inc(v_free, 1)
        V.wait_ge(v_full, v.filled())
        b = v.take()
        o = b[0:DH, 0:RM].rearrange("p (b c two) -> p c b two", b=NB, two=2)
        V.tensor_copy(MIXT[0:DH, 6:8, SEQ:NT], o[:, :, :, 0])
        V.tensor_copy(MIXT[DH:P, 6:8, SEQ:NT], o[:, :, :, 1]).then_inc(v_free, 1)

    def sp_wo(l):
        nc.sync.wait_ge(sem("v_used"), NB - 1)
        nc.sync.dma_start(WO[:, :, :], A["w_out"][l].rearrange("(k p) n -> p k n", p=P)).then_inc(sem("w_out"), 16)

    def pe_out(l):
        PE.wait_ge(sem("w_out"), nth("PE", "w_out", 16))
        PE.wait_ge(v_free, v.all_free())
        PE.wait_ge(sem("mix"), nth("PE", "mix"))
        for i, (t0, n) in reversed(list(enumerate(TILES))):
            for hf in range(2):
                PE.wait_ge(v_free, v.room())
                b = v.claim()
                if n == NB:
                    pe_few(b, MIXT, WO, slice(hf * 512, (hf + 1) * 512)).then_inc(v_full, 1)
                    continue
                for c in range(KD):
                    m = mm(b[0:n, :], MIXT[:, c, t0:t0 + n], WO[:, c, hf * 512:(hf + 1) * 512], c == 0, c == KD - 1)
                m.then_inc(v_full, 1)

    def dve_out(l):
        V.memset(ST[:, 8:9], 0.0).then_inc(sem("mix"), 1)
        V.wait_ge(sem("mix"), nth("DVE", "mix"))
        V.memset(ST[:, 8:9], 0.0).then_inc(sem("arena_free"), 1)
        V.wait_ge(sem("arena_free"), nth("DVE", "arena_free"))
        for i, (t0, n) in reversed(list(enumerate(TILES))):
            for hf in range(2):
                V.wait_ge(v_full, v.filled())
                b = v.take()
                x = X[0:n, i, hf * 512:(hf + 1) * 512]
                if n == NB:
                    dve_few(x, b, 0)
                    continue
                tt(x, x, b[0:n, :], ALU.add).then_inc(v_free, 1)
            V.wait_ge(v_free, v.emptied())
            dve_squares(i)
        V.memset(ST[:, 8:9], 0.0).then_inc(sem("mixed"), 1)
        V.wait_ge(sem("mixed"), nth("DVE", "mixed"))

    def sp_router(l):
        if l:
            nc.sync.wait_ge(sem("router_used"), nth("SP", "router_used"))
        nc.sync.dma_start(WR[:, :, 0:4],
                          A["moe_w_coarse"][l].rearrange("(k p) n -> p k n", p=P)).then_inc(sem("router"), 16)
        nc.sync.dma_start(WR[:, :, 4:36],
                          A["moe_w_fine"][l].rearrange("(k p) n -> p k n", p=P)).then_inc(sem("router"), 16)
        nc.sync.dma_start(BR[:, 0:4], A["moe_b_coarse"][l:l + 1, :].broadcast_to([P, 4])).then_inc(sem("router"), 16)
        nc.sync.dma_start(BR[:, 4:36], A["moe_b_fine"][l:l + 1, :].broadcast_to([P, NE])).then_inc(sem("router"), 16)

    def pe_router():
        PE.wait_ge(sem("router"), nth("PE", "router", 16 * 4))
        PE.wait_ge(v_free, v.room())
        b = v.claim()
        for i, (t0, n) in enumerate(TILES):
            for k in range(KD):
                m = mm(b[0:n, i * 36:(i + 1) * 36], HT[:, k, t0:t0 + n], WR[:, k, :], k == 0, k == KD - 1)
        m.then_inc(v_full, 1)
        PE.wait_ge(sem("assigned"), nth("PE", "assigned"))
        PE.wait_ge(v_free, v.room())
        b = v.claim()
        for i in range(3):
            for j in range(i + 1):
                m = mm(b[:, i * NE:(i + 1) * NE], C("before") if j == i else C("ones"), RTMP[:, 15, j, 0:NE], j == 0, j == i)
        m.then_inc(v_full, 1)
        PE.wait_ge(v_free, v.room())
        b = v.claim()
        for j in range(3):
            m = mm(b[0:1, 0:NE], C("ones")[:, 0:1], RTMP[:, 15, j, 0:NE], j == 0, j == 2)
        m.then_inc(v_full, 1)

    def act_router():
        AC.wait_ge(sem("r_exp_in"), nth("ACT", "r_exp_in"))
        AC.activation(RTMP[:, 2, :, 0:4], RTMP[:, 1, :, 0:4], ACT.Exp).then_inc(sem("r_exp"), 1)
        AC.wait_ge(sem("r_exp"), nth("ACT", "r_exp"))
        AC.wait_ge(sem("r_exp_in"), nth("ACT", "r_exp_in"))
        AC.activation(RTMP[:, 13, :, 0:1], RTMP[:, 12, :, 0:1], ACT.Exp).then_inc(sem("r_exp"), 1)
        AC.wait_ge(sem("r_exp"), nth("ACT", "r_exp"))

    def dve_router():
        T = RTMP
        V.wait_ge(sem("router"), nth("DVE", "router", 16 * 4))
        bc = lambda ap, n: ap.broadcast_to([P, 3, n])
        col = lambda k: T[:, k, :, 0:1]
        V.memset(T[:, :, :, :], 0.0).then_inc(dve_done, 1)
        V.wait_ge(dve_done, nth("DVE", "dve_done"))
        V.wait_ge(v_full, v.filled())
        b = v.take()
        tt(T[:, 0, 0:2, :], b[:, 0:72].rearrange("p (i n) -> p i n", i=2),
           BR[:, :].unsqueeze(1).broadcast_to([P, 2, 36]), ALU.add).then_inc(dve_done, 1)
        V.wait_ge(dve_done, nth("DVE", "dve_done"))
        tt(T[0:NB, 0, 2, :], b[0:NB, 72:108], BR[0:NB, :], ALU.add).then_inc(v_free, 1)
        V.wait_ge(v_free, v.emptied())
        lg, lf = T[:, 0, :, 0:4], T[:, 0, :, 4:36]
        V.tensor_reduce(T[:, 3, :, 0], lg, AX_X, ALU.max).then_inc(dve_done, 1)
        V.wait_ge(dve_done, nth("DVE", "dve_done"))
        tt(T[:, 1, :, 0:4], lg, bc(col(3), 4), ALU.subtract)
        tt(T[:, 4, :, 0:4], lg, bc(col(3), 4), ALU.is_ge).then_inc(sem("r_exp_in"), 1)
        V.wait_ge(sem("r_exp_in"), nth("DVE", "r_exp_in"))
        go = C("gorder").unsqueeze(1).broadcast_to([P, 3, 4])
        tt(T[:, 4, :, 0:4], T[:, 4, :, 0:4], go, ALU.mult).then_inc(dve_done, 1)
        V.wait_ge(dve_done, nth("DVE", "dve_done"))
        V.tensor_reduce(T[:, 5, :, 0], T[:, 4, :, 0:4], AX_X, ALU.max).then_inc(dve_done, 1)
        V.wait_ge(dve_done, nth("DVE", "dve_done"))
        tt(T[:, 4, :, 0:4], go, bc(col(5), 4), ALU.is_equal)
        V.wait_ge(sem("r_exp"), nth("DVE", "r_exp"))
        V.tensor_reduce(T[:, 6, :, 0], T[:, 2, :, 0:4], AX_X, ALU.add).then_inc(dve_done, 1)
        V.wait_ge(dve_done, nth("DVE", "dve_done"))
        V.reciprocal(col(6), col(6))
        for i in range(3):
            g4 = T[:, 4, i, 0:4].unsqueeze(2).broadcast_to([P, 4, 8])
            f4 = T[:, 0, i, 4:36].rearrange("p (g e) -> p g e", g=4)
            o4 = T[:, 7, i, 0:32].rearrange("p (g e) -> p g e", g=4)
            q4 = T[:, 8, i, 0:32].rearrange("p (g e) -> p g e", g=4)
            tt(o4, f4, g4, ALU.mult)
            ts(q4, g4, -1.0, -NEG, ALU.add, ALU.mult).then_inc(dve_done, 1)
            V.wait_ge(dve_done, nth("DVE", "dve_done"))
            tt(o4, o4, q4, ALU.add).then_inc(dve_done, 1)
            V.wait_ge(dve_done, nth("DVE", "dve_done"))
        lf = T[:, 7, :, 0:32]
        order = C("order").unsqueeze(1).broadcast_to([P, 3, NE])
        for k, (hot, val) in enumerate(((9, 3), (10, 5))):
            V.tensor_reduce(T[:, val, :, 0], lf, AX_X, ALU.max).then_inc(dve_done, 1)
            V.wait_ge(dve_done, nth("DVE", "dve_done"))
            tt(T[:, 8, :, 0:32], lf, bc(col(val), NE), ALU.is_ge).then_inc(dve_done, 1)
            V.wait_ge(dve_done, nth("DVE", "dve_done"))
            tt(T[:, 8, :, 0:32], T[:, 8, :, 0:32], order, ALU.mult).then_inc(dve_done, 1)
            V.wait_ge(dve_done, nth("DVE", "dve_done"))
            V.tensor_reduce(T[:, 11, :, 0], T[:, 8, :, 0:32], AX_X, ALU.max).then_inc(dve_done, 1)
            V.wait_ge(dve_done, nth("DVE", "dve_done"))
            tt(T[:, hot, :, 0:32], order, bc(col(11), NE), ALU.is_equal).then_inc(dve_done, 1)
            V.wait_ge(dve_done, nth("DVE", "dve_done"))
            if k == 0:
                ts(T[:, 8, :, 0:32], T[:, hot, :, 0:32], 2 * NEG, None, ALU.mult).then_inc(dve_done, 1)
                V.wait_ge(dve_done, nth("DVE", "dve_done"))
                tt(lf, lf, T[:, 8, :, 0:32], ALU.add).then_inc(dve_done, 1)
                V.wait_ge(dve_done, nth("DVE", "dve_done"))
        tt(col(12), col(5), col(3), ALU.subtract).then_inc(sem("r_exp_in"), 1)
        V.wait_ge(sem("r_exp_in"), nth("DVE", "r_exp_in"))
        V.wait_ge(sem("r_exp"), nth("DVE", "r_exp"))
        ts(T[:, 14, :, 0:1], col(13), 1.0, None, ALU.add).then_inc(dve_done, 1)
        V.wait_ge(dve_done, nth("DVE", "dve_done"))
        V.reciprocal(col(14), col(14)).then_inc(dve_done, 1)
        V.wait_ge(dve_done, nth("DVE", "dve_done"))
        tt(col(14), col(14), col(6), ALU.mult).then_inc(dve_done, 1)
        V.wait_ge(dve_done, nth("DVE", "dve_done"))
        tt(col(13), col(13), col(14), ALU.mult).then_inc(dve_done, 1)
        V.wait_ge(dve_done, nth("DVE", "dve_done"))
        real = C("real").unsqueeze(2).broadcast_to([P, 3, NE])
        tt(T[:, 9, :, 0:32], T[:, 9, :, 0:32], real, ALU.mult).then_inc(dve_done, 1)
        V.wait_ge(dve_done, nth("DVE", "dve_done"))
        tt(T[:, 10, :, 0:32], T[:, 10, :, 0:32], real, ALU.mult).then_inc(dve_done, 1)
        V.wait_ge(dve_done, nth("DVE", "dve_done"))
        tt(T[:, 15, :, 0:32], T[:, 9, :, 0:32], T[:, 10, :, 0:32], ALU.add)
        V.memset(ST[:, 8:9], 0.0).then_inc(sem("assigned"), 1)
        V.wait_ge(sem("assigned"), nth("DVE", "assigned"))
        tt(T[:, 9, :, 0:32], T[:, 9, :, 0:32], bc(col(14), NE), ALU.mult).then_inc(dve_done, 1)
        V.wait_ge(dve_done, nth("DVE", "dve_done"))
        tt(T[:, 10, :, 0:32], T[:, 10, :, 0:32], bc(col(13), NE), ALU.mult).then_inc(dve_done, 1)
        V.wait_ge(dve_done, nth("DVE", "dve_done"))
        tt(RW[:, :, :], T[:, 9, :, 0:32], T[:, 10, :, 0:32], ALU.add)
        V.wait_ge(v_full, v.filled())
        b = v.take()
        stt(RT[:, :, :], b[:, 0:96].rearrange("p (i n) -> p i n", i=3), 1.0, T[:, 15, :, 0:32],
            ALU.add, ALU.mult).then_inc(v_free, 1)
        V.wait_ge(v_free, v.emptied())
        ts(RT[:, :, :], RT[:, :, :], -1.0, None, ALU.add)
        V.wait_ge(v_full, v.filled())
        b = v.take()
        V.tensor_reduce(T[0:1, 8, 0, 0:1], b[0:1, 0:NE], AX_X, ALU.max).then_inc(dve_done, 1)
        V.wait_ge(dve_done, nth("DVE", "dve_done"))
        V.tensor_copy(T[0:1, 8, 1, 0:1], b[0:1, 0:1]).then_inc(v_free, 1)
        V.tensor_copy(CNT[0:1, 0:1], T[0:1, 8, 0, 0:1])
        V.memset(ST[:, 8:9], 0.0).then_inc(sem("counted"), 1)
        V.wait_ge(sem("counted"), nth("DVE", "counted"))
        V.memset(ST[:, 8:9], 0.0).then_inc(sem("router_used"), 1)
        V.wait_ge(sem("router_used"), nth("DVE", "router_used"))

    def sp_step(l, it, g):
        wg = A["moe_w_gate"][l].rearrange("(q e) (k p) f -> q k p e f", e=GE, p=P)
        wu = A["moe_w_up"][l].rearrange("(q e) (k p) f -> q k p e f", e=GE, p=P)
        wd = A["moe_w_down"][l].rearrange("(q e) (k p) d -> q k p e d", e=GE, p=P)
        for u in range(UNITS):
            s = u % RING
            n, i = it
            if n or u >= RING:
                nc.sync.wait_ge(w_used, i * UNITS + (n * UNITS + u - RING + 1))
            dst = RINGW[:, s, :]
            if u < 8:
                d4 = dst.rearrange("p (z e f) -> p z e f", z=2, e=GE)
                for z, w in enumerate((wg, wu)):
                    nc.sync.dma_start(d4[:, z, :, :], w[bass.ds(g, 1), u].rearrange("q p e f -> (q p) e f")).then_inc(
                        w_in_ring[s], 16)
            else:
                d3 = dst.rearrange("p (e d) -> p e d", e=GE)
                for z in range(2):
                    nc.sync.dma_start(d3[:, 2 * z:2 * z + 2, :],
                                      wd[bass.ds(g, 1), u - 8, :, 2 * z:2 * z + 2].rearrange("q p e d -> (q p) e d")).then_inc(
                        w_in_ring[s], 16)

    def pe_step(it):
        PE.wait_ge(sem("sel"), it + 1)
        for q in range(4):
            PE.wait_ge(v_free, v.room())
            b = v.claim()
            for c in range(2):
                for i, (t0, n) in enumerate(TILES):
                    m = mm(b[:, c * P:(c + 1) * P], XN[0:n, i, (2 * q + c) * P:(2 * q + c + 1) * P], SELT[0:n, i, :], i == 0, i == 2)
            m.then_inc(v_full, 1)
        PE.wait_ge(v_free, v.all_free())
        PE.wait_ge(a_free, a.room())
        gate = a.claim()
        PE.wait_ge(v_free, v.room())
        up = v.claim()
        for u in range(8):
            PE.wait_ge(w_in_ring[u % RING], 32 * (2 * it + u // RING + 1))
            w = RINGW[:, u % RING, :].rearrange("p (z e f) -> p z e f", z=2, e=GE)
            for z, out in enumerate((gate, up)):
                for e in range(GE):
                    m = mm(out[e * SLOT:(e + 1) * SLOT, :], HG_T[:, u, e * SLOT:(e + 1) * SLOT], w[:, z, e, :], u == 0, u == 7)
                if u == 7 and z == 0:
                    m.then_inc(a_full, 1)
            if u < 7:
                m.then_inc(w_used, 1)
        m.then_inc(v_full, 1)
        PE.wait_ge(v_free, v.all_free())
        PE.wait_ge(v_free, v.room())
        b = v.claim()
        for f in range(4):
            m = tr(b[:, f * P:(f + 1) * P], AV[:, f * P:(f + 1) * P])
            if f == 0:
                m.then_inc(w_used, 1)
        m.then_inc(v_full, 1)
        PE.wait_ge(v_free, v.all_free())
        outs = []
        for _ in range(2):
            PE.wait_ge(a_free, a.room())
            outs.append(a.claim())
        for f in range(4):
            u = 8 + f
            PE.wait_ge(w_in_ring[u % RING], 32 * (2 * it + u // RING + 1))
            w = RINGW[:, u % RING, :].rearrange("p (e d) -> p e d", e=GE)
            for hf in range(2):
                for e in range(GE):
                    m = mm(outs[hf][e * SLOT:(e + 1) * SLOT, :], AVT[:, f, e * SLOT:(e + 1) * SLOT],
                           w[:, e, hf * 512:(hf + 1) * 512], f == 0, f == 3)
                if f == 3:
                    m.then_inc(a_full, 1)
            if f < 3:
                m.then_inc(w_used, 1)
        PE.wait_ge(a_free, a.room())
        b = a.claim()
        for i, (t0, n) in enumerate(TILES):
            m = tr(b[:, t0:t0 + n], SELW[0:n, i, :])
            if i == 0:
                m.then_inc(w_used, 1)
        m.then_inc(a_full, 1)
        PE.wait_ge(a_free, a.all_free())
        for i, (t0, n) in enumerate(TILES):
            for hf in range(2):
                PE.wait_ge(v_free, v.room())
                b = v.claim()
                m = mm(b[0:n, :], SWT[:, t0:t0 + n], OUT4[:, hf * 512:(hf + 1) * 512])
                m.then_inc(v_full, 1)

    def act_step():
        AC.wait_ge(a_full, a.filled())
        b = a.take()
        AC.activation(SG[:, :], b[:, :], ACT.Silu).then_inc(sem("silu"), 1)
        AC.wait_ge(sem("silu"), nth("ACT", "silu"))
        AC.copy(ST[:, 30:31], ST[:, 31:32]).then_inc(a_free, 1)
        AC.wait_ge(a_free, a.emptied())
        for hf in range(2):
            AC.wait_ge(a_full, a.filled())
            b = a.take()
            AC.copy(OUT4[:, hf * 512:(hf + 1) * 512], b[:, :]).then_inc(a_free, 1)
            AC.wait_ge(a_free, a.emptied())
        AC.wait_ge(a_full, a.filled())
        b = a.take()
        AC.copy(SWT[:, :], b[:, 0:NT]).then_inc(a_free, 1)
        AC.wait_ge(a_free, a.emptied())

    def dve_step(g, r, gain):
        rt = RT[:, :, bass.ds(g * GE, GE)].unsqueeze(3).broadcast_to([P, 3, GE, SLOT])
        rw = RW[:, :, bass.ds(g * GE, GE)].unsqueeze(3).broadcast_to([P, 3, GE, SLOT])
        o = at["slotno"][0]
        slot = CONST[:, o:o + SLOT] if isinstance(r, int) else CONST[:, bass.ds(r * SLOT + o, SLOT)]
        slot = slot.unsqueeze(1).unsqueeze(1).broadcast_to([P, 3, GE, SLOT])
        st = SELT[:, :, :].rearrange("p i (e s) -> p i e s", e=GE)
        sw = SELW[:, :, :].rearrange("p i (e s) -> p i e s", e=GE)
        for i in range(3):
            tt(st[:, i], rt[:, i], slot[:, i], ALU.is_equal).then_inc(dve_done, 1)
            V.wait_ge(dve_done, nth("DVE", "dve_done"))
            ins = tt(sw[:, i], st[:, i], rw[:, i], ALU.mult)
            if i < 2:
                ins.then_inc(dve_done, 1)
                V.wait_ge(dve_done, nth("DVE", "dve_done"))
            else:
                ins.then_inc(sem("sel"), 1)
                V.wait_ge(sem("sel"), nth("DVE", "sel"))
        for q in range(4):
            V.wait_ge(v_full, v.filled())
            b = v.take()
            gc = PAR[:, gain + 2 * q:gain + 2 * q + 2].unsqueeze(2).broadcast_to([P, 2, P])
            tt(HG_T[:, 2 * q:2 * q + 2, :], b[:, 0:256].rearrange("p (c s) -> p c s", c=2), gc, ALU.mult).then_inc(v_free, 1)
            V.wait_ge(v_free, v.emptied())
        V.wait_ge(v_full, v.filled())
        b = v.take()
        V.wait_ge(sem("silu"), nth("DVE", "silu"))
        tt(AV[:, :], SG[:, :], b[:, :], ALU.mult).then_inc(v_free, 1)
        V.wait_ge(v_free, v.emptied())
        V.wait_ge(v_full, v.filled())
        b = v.take()
        V.tensor_copy(AVT[:, :, :].rearrange("p f s -> p (f s)"), b[:, :]).then_inc(v_free, 1)
        V.wait_ge(v_free, v.emptied())
        for i, (t0, n) in enumerate(TILES):
            for hf in range(2):
                V.wait_ge(v_full, v.filled())
                b = v.take()
                x = X[0:n, i, hf * 512:(hf + 1) * 512]
                tt(x, x, b[0:n, :], ALU.add).then_inc(v_free, 1)
                V.wait_ge(v_free, v.emptied())


    def counts(who):
        if who == "PE":
            return [(v.claimed, 12), (a.claimed, 4)]
        if who == "ACT":
            return [(a.taken, 4), (count("ACT", "silu"), 1)]
        if who == "DVE":
            return [(v.taken, 12), (count("DVE", "dve_done"), 5), (count("DVE", "sel"), 1),
                    (count("DVE", "silu"), 1)]
        return []

    def increments(who):
        if who == "PE":
            return [(v_full, 12), (a_full, 4), (w_used, UNITS)]
        if who == "ACT":
            return [(a_free, 4), (sem("silu"), 1)]
        if who == "DVE":
            return [(v_free, 12), (dve_done, 5), (sem("sel"), 1)]
        return [(w_in_ring[s], 32 * UNITS // RING) for s in range(RING)]

    def moe(who, l):
        n0 = l * NGRP * (1 + OVER)
        eng = NM[who]
        gain = FFNG + 8 * l

        def step(n, i, g, r):
            if who == "SP":
                sp_step(l, (n, i), g)
            elif who == "PE":
                pe_step(i + n)
            elif who == "ACT":
                act_step()
            else:
                dve_step(g, r, gain)

        if who == "SP":
            nc.sync.wait_ge(sem("arena_free"), nth("SP", "arena_free"))
            if l == 0:
                sp_step(l, (0, 0), 0)
                with eng.Fori(0, NGRP - 1) as i:
                    step(1, i, i + 1, 0)
        if who != "SP" or l:
            with eng.Fori(0, NGRP) as i:
                for c, per in counts(who):
                    c.loop(i, per)
                step(n0, i, i, 0)
            for c, per in counts(who):
                c.end(NGRP)
        eng.wait_ge(sem("counted"), l + 1)
        most = eng.value_load(CNT[0:1, 0:1], min_val=0, max_val=NT)
        with eng.Fori(0, OVER) as r:
            with eng.If(most > r * SLOT + SLOT):
                with eng.Fori(0, NGRP) as g:
                    i = r * NGRP + g
                    for c, per in counts(who):
                        c.loop(i, per)
                    step(n0 + NGRP, i, g, r + 1)
            with eng.Else():
                if who == "SP":
                    eng.wait_ge(w_used, r * (UNITS * NGRP) + (n0 + NGRP) * UNITS)
                if who == "PE":
                    eng.wait_ge(v_free, r * (12 * NGRP) + v.claimed.n + 4)
                    eng.wait_ge(a_free, r * (4 * NGRP) + a.claimed.n + 4)
                for s, n in increments(who):
                    eng.sem_inc(s, n * NGRP)
        for c, per in counts(who):
            c.end(OVER * NGRP)

    NC = 6
    E_HALF = float(np.exp(-0.5))
    NCK = SEQ // CH
    PR, PK, PV_, PWA, PG = slice(0, 6), slice(6, 12), slice(12, 18), 18, 19
    SQ_B = place("SQ_B", 84160, [2, NT])
    RS_B = place("RS_B", 86272, [2, NT])
    HROW = MIXT[0:H, 0:3, :].rearrange("p c t -> p (c t)")[:, 0:QA]
    BON = place("BON", 0, [NC, NT], base=XNoff)[:, :, :]
    RSM = place("RSM", 91968, [NT])
    SHF = place("SHF", 0, [SHIFT_W])
    SSH = place("SSH", 12672, [SHIFT_W])
    PREVS = place("PREVS", 25344, [NCH, NB])
    DIF = place("DIF", 25984, [NCH, NT])
    AQ, QL, BT, KL = (place(n, 6336 * i, [NC, NT]) for i, n in enumerate(("AQ", "QL", "BT", "KL")))
    BTOK, KTOK, VTOK = (place(n, 25344 + 6144 * i, [2, QA]) for i, n in enumerate(("BTOK", "KTOK", "VTOK")))
    GG = place("GG", 43776, [NC, NT])
    AA = place("AA", 50112, [NC, NT])
    KN = place("KN", 56448, [NC, NT])
    LWP = place("LWP", 62784, [NC, SEQ])
    CC = place("CC", 68928, [NC, SEQ])
    EX = place("EX", 75072, [NC, SEQ])
    SCM = place("SCM", 25984, [NC, SEQ])
    EXI = place("EXI", 32128, [NC, SEQ])
    KAF = place("KAF", 19008, [NC, NT])
    T1 = place("T1", 81216, [NC, NT])
    LWS = place("LWS", 87584, [NC, NB])
    WUP = place("WUP", 93120, [QA])
    GUP = place("GUP", 96192, [QA])
    MATS = [place(f"MAT{i}", 50112 + 3072 * i, [H, CH]) for i in range(14)]
    VRAW = [place("VRAW", 16384 + 3072 * q, [QA], base=U1) for q in range(5)] + [place("VRAW", 90048, [QA])]
    YT = place("YT", 0, [NC, NT], base=XNoff + 12288)
    STT = place("STT", 6336, [NC, CH], base=XNoff + 12288)
    LAMK = place("LAMK", 6336 + 1536, [NC, NCK], base=XNoff + 12288)
    SST = place("SST", 0, [DH, DH], base=U1)
    STMP = place("STMP", 16384, [DH, DH], base=U1)
    VEC = place("VEC", 10496, [6, DH], base=XNoff)
    SAV = place("SAV", 10496 + 1536, [DH], base=XNoff)
    YS = place("YS", 0, [QA], base=U1)
    SOUT = place("SOUT", 4096, [H, DH], base=U1)

    def sp_layer_b():
        nc.sync.wait_ge(sem("moe_done"), nth("SP", "moe_done"))
        w = A["w_in_b"][0].rearrange("(k p) n -> p k n", p=P)
        for k in range(KD):
            nc.sync.dma_start(WIN_B[:, k, :], w[:, k, :]).then_inc(sem("w_in"), 16)
        sp_router(1)
        nc.sync.wait_ge(sem("proj_b"), nth("SP", "proj_b"))
        nc.sync.dma_start(SSH[0:NB, :], A["state_shift"][0]).then_inc(sem("b_w"), 16)
        nc.sync.dma_start(WUP[0:64, :], A["rwkv_w_up"][0]).then_inc(sem("b_w"), 16)
        nc.sync.dma_start(WUP[64:P, :], A["rwkv_a_up"][0]).then_inc(sem("b_w"), 16)
        nc.sync.dma_start(GUP[:, :], A["rwkv_g_up"][0]).then_inc(sem("b_w"), 16)
        sp_memattn(1)
        nc.sync.wait_ge(sem("u1_used"), nth("SP", "u1_used"))
        nc.sync.dma_start(SST[0:RS, :, :],
                          A["state_rwkv"][0].rearrange("b h v k -> (b h) v k")).then_inc(sem("s_state"), 16)

        nc.sync.wait_ge(sem("u1_ys"), nth("SP", "u1_ys"))
        nc.sync.dma_start(WO[:, :, :], A["w_out"][1].rearrange("(k p) n -> p k n", p=P)).then_inc(sem("w_out"), 16)

    def pool_layer_b():
        nc.gpsimd.wait_ge(sem("mixed"), nth("POOL", "mixed"))
        load_mem(nc.gpsimd, 1)
        nc.gpsimd.dma_start(HROW, A["head_rows"]).then_inc(sem("head_rows"), 16)
        pool_mem(1)
        nc.gpsimd.wait_ge(sem("shf"), nth("POOL", "shf"))
        nc.gpsimd.dma_start(O["p_shift"][0], SHF[0:1, :]).then_inc(sem("shf_stored"), 16)
        nc.gpsimd.dma_start(O["s_shift"][0], SHF[1:9, :]).then_inc(sem("shf_stored"), 16)
        pool_shift()
        pool_bonus()
        nc.gpsimd.wait_ge(sem("vraw"), nth("POOL", "vraw"))
        for q in range(6):
            for s in range(NB):
                nc.gpsimd.dma_start(VEC[s * H:(s + 1) * H, q, :],
                                    VRAW[q][s:s + 1, :].rearrange("b (h d) -> b h d", h=H)).then_inc(sem("vecs"), 16)
        pool_sample_step()
        nc.gpsimd.wait_ge(sem("s_stored"), nth("POOL", "s_stored", 16))
        for s in range(NB):
            nc.gpsimd.dma_start(YS[s:s + 1, :].rearrange("b (h d) -> b h d", h=H),
                                SAV[s * H:(s + 1) * H, :]).then_inc(sem("y_rows8"), 16)
        nc.gpsimd.wait_ge(sem("sout"), nth("POOL", "sout"))
        nc.gpsimd.dma_start(O["p_rwkv"][0, 0].rearrange("h v k -> v h k"),
                            SOUT[0:DH, :, :]).then_inc(sem("sout_stored"), 16)

    def pe_layer_b():
        pe_norm()
        pe_mem(1)
        PE.wait_ge(sem("w_in"), nth("PE", "w_in", 16 * KD))
        pe_channels(WIN_B, [P * c for c in range(22)])
        pe_last_rows()
        pe_headnorm(SQ_B, 2)
        pe_rows_before()
        pe_memattn(1)
        pe_rwkv()

    def act_layer_b():
        act_norm()
        act_mem(1)
        act_headnorm(RS_B)
        act_memattn(1)
        act_rwkv()

    def dve_layer_b():
        dve_norm(MIXG + 8)
        dve_mem(1)
        for c in range(22):
            V.wait_ge(v_full, v.filled())
            b = v.take()
            V.tensor_copy(PRT[:, c, :] if c < NCH else QT[:, c - NCH, :], b[:, 0:NT]).then_inc(v_free, 1)
            V.wait_ge(v_free, v.emptied())
        V.memset(ST[:, 8:9], 0.0).then_inc(sem("proj_b"), 1)
        V.wait_ge(sem("proj_b"), nth("DVE", "proj_b"))
        for q in range(5):
            V.wait_ge(v_full, v.filled())
            b = v.take()
            V.tensor_copy(SHF[0:9, q * 512:(q + 1) * 512], b[0:9, :]).then_inc(v_free, 1)
        V.memset(ST[:, 8:9], 0.0).then_inc(sem("shf"), 1)
        V.wait_ge(sem("shf"), nth("DVE", "shf"))
        dve_headnorm(QT[:, 0:2, :], SQ_B, RS_B, 2, [MQG + 1] * 2)
        V.wait_ge(v_full, v.filled())
        b = v.take()
        V.tensor_copy(PREVS[:, :, :].rearrange("p c b -> p (c b)"), b[:, 0:NCH * NB]).then_inc(v_free, 1)
        ts(ST[:, 56:62], PAR[:, KA:KA + 6], -1.0, 1.0, ALU.mult, ALU.add)
        V.memset(ST[:, 8:9], 0.0).then_inc(sem("prevs"), 1)
        V.wait_ge(sem("prevs"), nth("DVE", "prevs"))
        dve_memattn(1)
        V.memset(ST[:, 8:9], 0.0).then_inc(sem("mem_done"), 1)
        V.wait_ge(sem("mem_done"), nth("DVE", "mem_done"))
        dve_rwkv()

    COLS = ((0, 4), (4, 6))

    def pe_last_rows():
        for q in range(5):
            PE.wait_ge(v_free, v.room())
            b = v.claim()
            for c in range(4):
                m = tr(b[0:9, c * P:(c + 1) * P], PRT[:, 4 * q + c, SEQ - 1:NT])
            m.then_inc(v_full, 1)

    def pe_rows_before():
        PE.wait_ge(sem("b_w"), nth("PE", "b_w", 16 * 4))
        PE.wait_ge(v_free, v.room())
        b = v.claim()
        for c in range(NCH):
            m = tr(b[:, c * NB:(c + 1) * NB], SSH[0:NB, c * P:(c + 1) * P])
        m.then_inc(v_full, 1)

    def pe_rwkv():
        PE.wait_ge(sem("mem_done"), nth("PE", "mem_done"))
        PE.wait_ge(sem("gates_b"), nth("PE", "gates_b"))
        for c in range(NC):
            PE.wait_ge(a_free, a.room())
            b = a.claim()
            mm(b[:, 0:NT], WUP[0:64, c * P:(c + 1) * P], PRT[0:64, PWA, :]).then_inc(a_full, 1)
        for c in range(NC):
            PE.wait_ge(a_free, a.room())
            b = a.claim()
            mm(b[:, 0:NT], WUP[64:P, c * P:(c + 1) * P], PRT[64:P, PWA, :]).then_inc(a_full, 1)
        for c in range(NC):
            PE.wait_ge(v_free, v.room())
            b = v.claim()
            mm(b[:, 0:NT], GUP[:, c * P:(c + 1) * P], PRT[:, PG, :]).then_inc(v_full, 1)
        PE.wait_ge(sem("head_rows"), 16)
        pe_headroots()
        PE.wait_ge(sem("scaled"), nth("PE", "scaled"))
        for src in (lambda c: BT[:, c, :], lambda c: KL[:, c, :], lambda c: PRT[:, 12 + c, :]):
            for j in range(2):
                for c0, c1 in COLS:
                    PE.wait_ge(v_free, v.room())
                    b = v.claim()
                    for c in range(c0, c1):
                        m = tr(b[:, (c - c0) * P:(c - c0 + 1) * P], src(c)[:, j * P:(j + 1) * P])
                    m.then_inc(v_full, 1)
        for src in sample_vectors():
            for c0, c1 in COLS:
                PE.wait_ge(v_free, v.room())
                b = v.claim()
                for c in range(c0, c1):
                    m = tr(b[0:NB, (c - c0) * P:(c - c0 + 1) * P], src(c))
                m.then_inc(v_full, 1)
        PE.wait_ge(v_free, v.all_free())
        PE.wait_ge(sem("state0"), nth("PE", "state0"))
        for j in range(2):
            pe_inverse(j)
            if j == 0:
                PE.wait_ge(sem("bonus_in"), nth("PE", "bonus_in"))
                pe_headsums(BON)
                PE.wait_ge(v_free, v.all_free())
            for c in range(2 * j, 2 * j + 2):
                pe_chunk(j, c)
        PE.wait_ge(sem("state"), nth("PE", "state"))
        for c0, c1 in COLS:
            PE.wait_ge(v_free, v.room())
            b = v.claim()
            for c in range(c0, c1):
                m = tr(b[0:DH, (c - c0) * P:(c - c0 + 1) * P], STT[:, c, :])
            m.then_inc(v_full, 1)
        PE.wait_ge(sem("y_rows8"), 16 * NB)
        PE.wait_ge(v_free, v.room())
        b = v.claim()
        for c in range(NC):
            m = tr(b[:, c * NB:(c + 1) * NB], YS[0:NB, c * P:(c + 1) * P])
        m.then_inc(v_full, 1)
        PE.wait_ge(sem("sq"), nth("PE", "sq"))
        pe_headsums(YT)
        pe_headroots()

    def pe_headsums(x):
        for c in range(NC):
            PE.wait_ge(v_free, v.room())
            b = v.claim()
            mm(b[:, 0:NT], C("headones"), x[:, c, :]).then_inc(v_full, 1)

    def pe_headroots():
        PE.wait_ge(sem("sq"), nth("PE", "sq"))
        PE.wait_ge(v_free, v.room())
        b = v.claim()
        for c in range(NC):
            m = mm(b[0:H, 0:NT], C("headcol")[:, H - 2 - 2 * c:2 * H - 2 - 2 * c], T1[:, c, :], c == 0, c == NC - 1)
        m.then_inc(v_full, 1)
        PE.wait_ge(sem("roots"), nth("PE", "roots"))
        for c in range(NC):
            PE.wait_ge(v_free, v.room())
            b = v.claim()
            mm(b[:, 0:NT], HROW[:, c * P:(c + 1) * P], RSM[0:H, :]).then_inc(v_full, 1)

    def sample_vectors():
        return (lambda c: LWS[:, c, :], lambda c: PRT[:, 6 + c, SEQ:NT], lambda c: PRT[:, 12 + c, SEQ:NT],
                lambda c: KN[:, c, SEQ:NT], lambda c: AA[:, c, SEQ:NT], lambda c: PRT[:, c, SEQ:NT])

    def pe_pairs(f):
        for odd in range(2):
            PE.wait_ge(v_free, v.room())
            b = v.claim()
            for q in range(NC):
                for cp in range(2):
                    l, r = f(2 * q + odd, cp)
                    m = mm(b[64 * cp:64 * cp + 64, q * CH:(q + 1) * CH], l, r)
            m.then_inc(v_full, 1)

    def pe_square(l, r):
        for q in range(2):
            PE.wait_ge(v_free, v.all_free(1))
            b = v.claim()
            for h in range(6 * q, 6 * q + 6):
                for cp in range(2):
                    o = slice(64 * cp, 64 * cp + 64)
                    m = mm(b[o, (h % 6) * CH:(h % 6 + 1) * CH], l[o, h, :], r[o, h, :])
            m.then_inc(v_full, 1)

    P0, Q0, P1, Q1, TI, TT_, LO32, LO64, ZZ, LKT, QBT, QKT, SAM, X1M = MATS

    def pe_inverse(j):
        def at_(x, h, cp):
            o = 64 * (h % 2)
            return x[o:o + DH, h // 2, j * P + cp * CH:j * P + (cp + 1) * CH]
        for l, r in ((AQ, BT), (BT, AQ), (KL, AQ), (BT, QL), (KL, QL)):
            pe_pairs(lambda h, cp: (at_(l, h, cp), at_(r, h, cp)))
        p, q, p2, q2 = P0, Q0, P1, Q1
        for k in range(3):
            if k < 2:
                pe_square(q, p)
            pe_square(p, q)
            p, q, p2, q2 = p2, q2, p, q
            pe_square(q, TI)
        for hf in range(2):
            PE.wait_ge(v_free, v.all_free(1))
            b = v.claim()
            for h in range(6 * hf, 6 * hf + 6):
                for cp in range(2):
                    o = slice(64 * cp, 64 * cp + 64)
                    m = mm(b[o, (h % 6) * CH:(h % 6 + 1) * CH], TI[o, h, :], C("ident64")[o, :])
            m.then_inc(v_full, 1)
        for lo in (LO32, LO64):
            pe_square(lo, TT_)
            for hf in range(2):
                if hf == 0:
                    PE.wait_ge(v_free, v.all_free(1))
                else:
                    PE.wait_ge(v_free, v.all_free(2 if lo is LO32 else 1))
                for l, r in ((ZZ, TI), (TI, ZZ)) if lo is LO32 else ((TI, ZZ),):
                    PE.wait_ge(v_free, v.room())
                    b = v.claim()
                    for h in range(6 * hf, 6 * hf + 6):
                        for cp in range(2):
                            o = slice(64 * cp, 64 * cp + 64)
                            m = mm(b[o, (h % 6) * CH:(h % 6 + 1) * CH], l[o, h, :], r[o, h, :])
                    m.then_inc(v_full, 1)

    def pe_chunk(j, c):
        cp = c % 2
        o = slice(64 * cp, 64 * cp + 64)
        t = slice(c * CH, (c + 1) * CH)
        PE.wait_ge(sem("state"), nth("PE", "state"))
        for odd in range(2):
            PE.wait_ge(v_free, v.room())
            b = v.claim()
            hp = slice(64 * odd, 64 * odd + 64)
            for q in range(NC):
                m = mm(b[o, q * CH:(q + 1) * CH], AQ[hp, q, t], STT[hp, q, :])
            m.then_inc(v_full, 1)
        for q in range(2):
            PE.wait_ge(v_free, v.room())
            b = v.claim()
            for h in range(6 * q, 6 * q + 6):
                m = mm(b[o, (h % 6) * CH:(h % 6 + 1) * CH], LKT[o, HX(h), :], VTOK[o, j, h * DH:(h + 1) * DH])
            m.then_inc(v_full, 1)
        PE.wait_ge(v_free, v.all_free())
        for q in range(2):
            PE.wait_ge(v_free, v.room())
            b = v.claim()
            for h in range(6 * q, 6 * q + 6):
                m = mm(b[o, (h % 6) * CH:(h % 6 + 1) * CH], TT_[o, HX(h), :], X1M[o, h, :])
            m.then_inc(v_full, 1)
        PE.wait_ge(v_free, v.room())
        b = v.claim()
        for h in range(H):
            hp = slice(64 * (h % 2), 64 * (h % 2) + 64)
            m = mm(b[hp, h // 2 * CH:(h // 2 + 1) * CH], STT[hp, h // 2, :], QL[hp, h // 2, t])
        m.then_inc(v_full, 1)
        PE.wait_ge(v_free, v.all_free())
        PE.wait_ge(v_free, v.room())
        b = v.claim()
        for h in range(H):
            hp = slice(64 * (h % 2), 64 * (h % 2) + 64)
            out = b[hp, h // 2 * CH:(h // 2 + 1) * CH]
            mm(out, SAM[o, h, :], QBT[o, HX(h), :], True, False)
            m = mm(out, VTOK[o, j, h * DH:(h + 1) * DH], QKT[o, HX(h), :], False, True)
        m.then_inc(v_full, 1)
        PE.wait_ge(v_free, v.room())
        b = v.claim()
        for h in range(H):
            hp = slice(64 * (h % 2), 64 * (h % 2) + 64)
            out = b[hp, h // 2 * CH:(h // 2 + 1) * CH]
            hd = slice(h * DH, (h + 1) * DH)
            mm(out, BTOK[o, j, hd], SAM[o, h, :], True, False)
            m = mm(out, KTOK[o, j, hd], VTOK[o, j, hd], False, True)
        m.then_inc(v_full, 1)

    def HX(h):
        return (h % 2) * 6 + h // 2

    def act_rwkv():
        AC.wait_ge(sem("mixed_x"), nth("ACT", "mixed_x"))
        AC.activation(PRT[0:64, PWA, :], PRT[0:64, PWA, :], ACT.Tanh)
        AC.activation(PRT[:, PG, :], PRT[:, PG, :], ACT.Sigmoid).then_inc(sem("gates_b"), 1)
        AC.wait_ge(sem("gates_b"), nth("ACT", "gates_b"))
        for c in range(NC):
            AC.wait_ge(a_full, a.filled())
            b = a.take()
            AC.activation(LWP[:, c, :], b[:, 0:SEQ], ACT.Sigmoid, bias=PAR[:, W0 + c:W0 + c + 1])
            AC.activation(LWS[:, c, :], b[:, SEQ:NT], ACT.Sigmoid, bias=PAR[:, W0 + c:W0 + c + 1]).then_inc(a_free, 1)
        for c in range(NC):
            AC.wait_ge(a_full, a.filled())
            b = a.take()
            AC.activation(AA[:, c, :], b[:, 0:NT], ACT.Sigmoid, bias=PAR[:, A0 + c:A0 + c + 1]).then_inc(a_free, 1)
            AC.wait_ge(a_free, a.emptied())
        AC.copy(ST[:, 30:31], ST[:, 31:32]).then_inc(sem("sigmoids"), 1)
        for c in range(NC):
            AC.activation(KAF[:, c, :], AA[:, c, :], ACT.Identity, scale=PAR[:, KA + c:KA + c + 1], bias=ST[:, 56 + c:57 + c])
        AC.wait_ge(sem("cum"), nth("ACT", "cum"))
        AC.activation(EX[:, :, :], CC[:, :, :], ACT.Exp, scale=-E_HALF).then_inc(sem("lam"), 1)
        AC.activation(EXI[:, :, :], CC[:, :, :], ACT.Exp, scale=E_HALF).then_inc(sem("lam"), 1)
        AC.activation(LWS[:, :, :], LWS[:, :, :], ACT.Exp, scale=-E_HALF)
        rsqrt_act(RSM[0:H, :])
        AC.wait_ge(sem("cum"), nth("ACT", "cum"))
        AC.activation(LWP[:, :, :], LWP[:, :, :], ACT.Exp, scale=-E_HALF).then_inc(sem("lam"), 1)
        rsqrt_act(RSM[0:H, :])

    def dve_headroots(x, scale, eps, op):
        V.wait_ge(v_full, v.filled())
        b = v.take()
        ts(RSM[0:H, :], b[0:H, 0:NT], scale, eps, ALU.mult, op).then_inc(v_free, 1)
        V.memset(ST[:, 8:9], 0.0).then_inc(sem("var"), 1)
        V.wait_ge(sem("var"), nth("DVE", "var"))
        V.wait_ge(sem("std"), nth("DVE", "std"))
        V.reciprocal(RSM[0:H, :], RSM[0:H, :]).then_inc(sem("roots"), 1)
        for c in range(NC):
            V.wait_ge(v_full, v.filled())
            b = v.take()
            tt(x[:, c, :], x[:, c, :], b[:, 0:NT], ALU.mult).then_inc(v_free, 1)
        V.wait_ge(v_free, v.emptied())

    def dve_rwkv():
        V.wait_ge(sem("mixed_x"), nth("DVE", "mixed_x"))
        for c in range(NC):
            ts(KN[:, c, :], PRT[:, 6 + c, :], PAR[:, KK + c:KK + c + 1], None, ALU.mult).then_inc(dve_done, 1)
        V.wait_ge(dve_done, nth("DVE", "dve_done", NC))
        tt(T1[:, :, :], KN[:, :, :], KN[:, :, :], ALU.mult).then_inc(sem("sq"), 1)
        for c in range(NC):
            V.wait_ge(v_full, v.filled())
            b = v.take()
            V.tensor_copy(GG[:, c, :], b[:, 0:NT]).then_inc(v_free, 1)
        V.wait_ge(sem("sigmoids"), nth("DVE", "sigmoids"))
        V.wait_ge(sem("scan_mask"), 1)
        flat = lambda x: x[:, :, :].rearrange("p c t -> p (c t)")
        V.tensor_tensor_scan(flat(CC), flat(SCM), flat(LWP), 0.0, ALU.mult, ALU.add).then_inc(sem("cum"), 1)
        V.wait_ge(sem("cum"), 1)
        dve_headroots(KN, 1.0, 1e-24, ALU.max)
        tt(LWP[:, :, :], CC[:, :, :], LWP[:, :, :], ALU.subtract).then_inc(sem("cum"), 1)
        pr = slice(0, SEQ)
        V.wait_ge(sem("lam"), 2)
        V.wait_ge(sem("shf_stored"), nth("DVE", "shf_stored", 16 * 2))
        V.tensor_copy(LAMK[:, :, :], EX[:, :, CH - 1:SEQ:CH])
        tt(QL[:, :, pr], PRT[:, PR, pr], EX[:, :, :], ALU.mult)
        tt(PRT[:, PK, :], PRT[:, PK, :], KAF[:, :, :], ALU.mult).then_inc(dve_done, 1)
        tt(AA[:, :, :], AA[:, :, :], KN[:, :, :], ALU.mult).then_inc(dve_done, 1)
        V.wait_ge(dve_done, nth("DVE", "dve_done", 2))
        tt(KL[:, :, pr], PRT[:, PK, pr], EXI[:, :, :], ALU.mult)
        tt(BT[:, :, pr], AA[:, :, pr], EXI[:, :, :], ALU.mult)
        V.wait_ge(sem("lam"), 3)
        tt(AQ[:, :, pr], KN[:, :, pr], LWP[:, :, :], ALU.mult)
        V.memset(ST[:, 8:9], 0.0).then_inc(sem("scaled"), 1)
        V.wait_ge(sem("scaled"), nth("DVE", "scaled"))
        for tok in (BTOK, KTOK, VTOK):
            for j in range(2):
                for c0, c1 in COLS:
                    V.wait_ge(v_full, v.filled())
                    b = v.take()
                    V.tensor_copy(tok[:, j, c0 * P:c1 * P], b[:, 0:(c1 - c0) * P]).then_inc(v_free, 1)
        for q in range(6):
            for c0, c1 in COLS:
                V.wait_ge(v_full, v.filled())
                b = v.take()
                V.tensor_copy(VRAW[q][0:NB, c0 * P:c1 * P], b[0:NB, 0:(c1 - c0) * P]).then_inc(v_free, 1)
        V.memset(ST[:, 8:9], 0.0).then_inc(sem("vraw"), 1)
        V.wait_ge(sem("vraw"), nth("DVE", "vraw"))
        V.memset(STT[:, :, :], 0.0)
        V.memset(ST[:, 8:9], 0.0).then_inc(sem("state0"), 1)
        V.wait_ge(sem("state0"), nth("DVE", "state0"))
        for j in range(2):
            dve_inverse(j)
            if j == 0:
                for c in range(NC):
                    V.wait_ge(v_full, v.filled())
                    b = v.take()
                    tt(BON[:, c, :], b[:, 0:NT], PRT[:, 12 + c, :], ALU.mult).then_inc(v_free, 1)
                    V.wait_ge(v_free, v.emptied())
                    ts(BON[:, c, :], BON[:, c, :], PAR[:, LNB + c:LNB + c + 1], None, ALU.add)
                V.wait_ge(sem("vecs"), 16 * 6 * NB)
            for c in range(2 * j, 2 * j + 2):
                dve_chunk(j, c)
        for c0, c1 in COLS:
            V.wait_ge(v_full, v.filled())
            b = v.take()
            if c0 == 0:
                V.wait_ge(sem("y_rows8"), 16 * NB)
            V.tensor_copy(SOUT[0:DH, 2 * c0:2 * c1, :].rearrange("p h k -> p (h k)"),
                          b[0:DH, 0:(c1 - c0) * P]).then_inc(v_free, 1)
        V.wait_ge(v_full, v.filled())
        b = v.take()
        V.tensor_copy(YT[:, :, SEQ:NT], b[:, 0:NC * NB].rearrange("p (c b) -> p c b", b=NB)).then_inc(v_free, 1)
        V.memset(ST[:, 8:9], 0.0).then_inc(sem("sout"), 1)
        V.wait_ge(sem("sout"), nth("DVE", "sout"))
        V.memset(ST[:, 8:9], 0.0).then_inc(sem("sq"), 1)
        V.wait_ge(sem("sq"), nth("DVE", "sq"))
        for c in range(NC):
            V.wait_ge(v_full, v.filled())
            b = v.take()
            stt(YT[:, c, :], b[:, 0:NT], -1.0 / DH, YT[:, c, :], ALU.mult, ALU.add).then_inc(v_free, 1)
        V.wait_ge(v_free, v.emptied())
        tt(T1[:, :, :], YT[:, :, :], YT[:, :, :], ALU.mult).then_inc(sem("sq"), 1)
        dve_headroots(YT, 1.0 / DH, 64e-5, ALU.add)
        for c in range(NC):
            stt(YT[:, c, :], YT[:, c, :], PAR[:, LNW + c:LNW + c + 1], BON[:, c, :], ALU.mult, ALU.add).then_inc(dve_done, 1)
        V.wait_ge(dve_done, nth("DVE", "dve_done", NC))
        tt(MIXT[:, 0:NC, :], YT[:, :, :], GG[:, :, :], ALU.mult)
        V.wait_ge(sem("sout_stored"), 16)
        V.memset(ST[:, 8:9], 0.0).then_inc(sem("u1_ys"), 1)
        V.wait_ge(sem("u1_ys"), nth("DVE", "u1_ys"))

    def pool_shift():
        nc.gpsimd.wait_ge(sem("prevs"), nth("POOL", "prevs"))
        nc.gpsimd.tensor_tensor(DIF[:, :, 1:SEQ], PRT[:, :, 0:SEQ - 1], PRT[:, :, 1:SEQ], ALU.subtract)
        nc.gpsimd.tensor_scalar(DIF[:, :, 0:1], PRT[:, :, 0:1], -1.0, None, ALU.mult)
        nc.gpsimd.tensor_tensor(DIF[:, :, SEQ:NT], PREVS[:, :, :], PRT[:, :, SEQ:NT], ALU.subtract).then_inc(sem("shift"), 1)
        nc.gpsimd.wait_ge(sem("shift"), 1)
        mu = PAR[:, MU:MU + NCH].unsqueeze(2).broadcast_to([P, NCH, NT])
        nc.gpsimd.tensor_tensor(DIF[:, :, :], DIF[:, :, :], mu, ALU.mult).then_inc(sem("shift"), 1)
        nc.gpsimd.wait_ge(sem("shift"), 2)
        nc.gpsimd.tensor_tensor(PRT[:, :, :], PRT[:, :, :], DIF[:, :, :], ALU.add).then_inc(sem("mixed_x"), 1)
        nc.gpsimd.wait_ge(sem("mixed_x"), 1)
        nc.gpsimd.memset(SCM[:, :, :], 1.0).then_inc(sem("shift"), 1)
        nc.gpsimd.wait_ge(sem("shift"), 3)
        nc.gpsimd.memset(SCM[:, :, 0:SEQ:CH], 0.0).then_inc(sem("scan_mask"), 1)

    def pool_bonus():
        nc.gpsimd.wait_ge(sem("scaled"), nth("POOL", "scaled"))
        nc.gpsimd.tensor_tensor(BON, PRT[:, PR, :], PRT[:, PK, :], ALU.mult).then_inc(sem("shift"), 1)
        nc.gpsimd.wait_ge(sem("shift"), 4)
        rk = PAR[:, RK:RK + NC].unsqueeze(2).broadcast_to([P, NC, NT])
        nc.gpsimd.tensor_tensor(BON, BON, rk, ALU.mult).then_inc(sem("bonus_in"), 1)

    def pool_sample_step():
        nc.gpsimd.wait_ge(sem("s_state"), 16)
        nc.gpsimd.wait_ge(sem("vecs"), 16 * 6 * NB)
        s, t = SST[0:RS, :, :], STMP[0:RS, :, :]
        row = lambda q: VEC[0:RS, q:q + 1, :].broadcast_to([RS, DH, DH])
        colv = lambda ap: ap.unsqueeze(2).broadcast_to([RS, DH, DH])
        sa = SAV[0:RS, :]
        G_ = nc.gpsimd
        G_.tensor_tensor(t, s, row(3), ALU.mult).then_inc(sem("s_step"), 1)
        G_.wait_ge(sem("s_step"), 1)
        pool_sum(t, 1)
        G_.tensor_scalar(sa, t[:, :, 0], -1.0, None, ALU.mult).then_inc(sem("s_step"), 1)
        G_.tensor_tensor(s, s, row(0), ALU.mult).then_inc(sem("s_step"), 1)
        G_.wait_ge(sem("s_step"), 9)
        G_.tensor_tensor(t, colv(sa), row(4), ALU.mult).then_inc(sem("s_step"), 1)
        G_.wait_ge(sem("s_step"), 10)
        G_.tensor_tensor(s, s, t, ALU.add).then_inc(sem("s_step"), 1)
        G_.wait_ge(sem("s_step"), 11)
        G_.tensor_tensor(t, colv(VEC[0:RS, 2, :]), row(1), ALU.mult).then_inc(sem("s_step"), 1)
        G_.wait_ge(sem("s_step"), 12)
        G_.tensor_tensor(s, s, t, ALU.add).then_inc(sem("s_step"), 1)
        G_.wait_ge(sem("s_step"), 13)
        G_.dma_start(O["s_rwkv"][0].rearrange("b h v k -> (b h) v k"), s).then_inc(sem("s_stored"), 16)
        G_.tensor_tensor(t, s, row(5), ALU.mult).then_inc(sem("s_step"), 1)
        G_.wait_ge(sem("s_step"), 14)
        pool_sum(t, 14)
        G_.tensor_copy(sa, t[:, :, 0]).then_inc(sem("s_step"), 1)
        G_.wait_ge(sem("s_step"), 21)

    def pool_sum(t, n):
        w = DH // 2
        while w:
            nc.gpsimd.tensor_tensor(t[:, :, 0:w], t[:, :, 0:w], t[:, :, w:2 * w], ALU.add).then_inc(sem("s_step"), 1)
            n, w = n + 1, w // 2
            nc.gpsimd.wait_ge(sem("s_step"), n)

    def dve_inverse(j):
        msk = lambda k: C(k).unsqueeze(1).broadcast_to([P, 6, CH])
        bank = lambda b: b[:, 0:6 * CH].rearrange("p (h t) -> p h t", h=6)
        half = lambda m, q: m[:, 6 * q:6 * q + 6, :]
        for q in range(2):
            V.wait_ge(v_full, v.filled())
            b = bank(v.take())
            stt(half(P0, q), b, -1.0, msk("m16l"), ALU.mult, ALU.mult)
            tt(half(LO32, q), b, msk("off32"), ALU.mult)
            tt(half(LO64, q), b, msk("off64"), ALU.mult).then_inc(v_free, 1)
            V.wait_ge(v_free, v.emptied())
            tt(half(TI, q), half(P0, q), msk("ident64"), ALU.add)
        for q in range(2):
            V.wait_ge(v_full, v.filled())
            b = bank(v.take())
            stt(half(Q0, q), b, -1.0, msk("m16u"), ALU.mult, ALU.mult).then_inc(v_free, 1)
        for m, k in ((LKT, "m_iu"), (QBT, "m_ieu"), (QKT, "m_ieu")):
            for q in range(2):
                V.wait_ge(v_full, v.filled())
                b = bank(v.take())
                tt(half(m, q), b, msk(k), ALU.mult).then_inc(v_free, 1)
        p, q_, p2, q2 = P0, Q0, P1, Q1
        for k in range(3):
            for m in (p2, q2) if k < 2 else (q2,):
                for q in range(2):
                    V.wait_ge(v_full, v.filled())
                    b = bank(v.take())
                    V.tensor_copy(half(m, q), b).then_inc(v_free, 1)
            p, q_, p2, q2 = p2, q2, p, q_
            for q in range(2):
                V.wait_ge(v_full, v.filled())
                b = bank(v.take())
                tt(half(TI, q), half(TI, q), b, ALU.add).then_inc(v_free, 1)
        for q in range(2):
            V.wait_ge(v_full, v.filled())
            b = bank(v.take())
            V.tensor_copy(half(TT_, q), b).then_inc(v_free, 1)
        for lo in (LO32, LO64):
            for q in range(2):
                V.wait_ge(v_full, v.filled())
                b = bank(v.take())
                V.tensor_copy(half(ZZ, q), b).then_inc(v_free, 1)
            for q in range(2):
                held = []
                for m in (TI, TT_) if lo is LO32 else (TT_,):
                    V.wait_ge(v_full, v.filled())
                    held.append((m, v.take()))
                for m, bk in held:
                    tt(half(m, q), half(m, q), bank(bk), ALU.subtract).then_inc(v_free, 1)
        V.memset(ST[:, 8:9], 0.0).then_inc(sem("state"), 1)
        V.wait_ge(sem("state"), nth("DVE", "state"))

    def dve_chunk(j, c):
        cp = c % 2
        o = slice(64 * cp, 64 * cp + 64)
        t = slice(c * CH, (c + 1) * CH)
        x = X1M[o, :, :]
        for odd in range(2):
            V.wait_ge(v_full, v.filled())
            b = v.take()
            V.tensor_copy(x[:, odd:H:2, :], b[o, 0:6 * CH].rearrange("p (h v) -> p h v", h=6)).then_inc(v_free, 1)
            V.wait_ge(v_free, v.emptied())
        for q in range(2):
            V.wait_ge(v_full, v.filled())
            b = v.take()
            xq = x[:, 6 * q:6 * q + 6, :]
            stt(xq, b[o, 0:6 * CH].rearrange("p (h v) -> p h v", h=6), -1.0, xq, ALU.mult, ALU.subtract).then_inc(v_free, 1)
        for q in range(2):
            V.wait_ge(v_full, v.filled())
            b = v.take()
            V.tensor_copy(SAM[o, 6 * q:6 * q + 6, :], b[o, 0:6 * CH].rearrange("p (h v) -> p h v", h=6)).then_inc(v_free, 1)
        V.wait_ge(v_full, v.filled())
        b = v.take()
        yt = YT[:, :, t]
        V.tensor_copy(yt, b[:, 0:6 * CH].rearrange("p (h v) -> p h v", h=6)).then_inc(v_free, 1)
        V.wait_ge(v_full, v.filled())
        b = v.take()
        tt(yt, yt, b[:, 0:6 * CH].rearrange("p (h v) -> p h v", h=6), ALU.add).then_inc(v_free, 1)
        V.wait_ge(v_full, v.filled())
        b = v.take()
        tt(STT[:, :, :], STT[:, :, :], b[:, 0:6 * CH].rearrange("p (h v) -> p h v", h=6), ALU.add).then_inc(v_free, 1)
        V.wait_ge(v_free, v.emptied())
        tt(STT[:, :, :], STT[:, :, :], LAMK[:, :, c:c + 1].broadcast_to([P, NC, CH]), ALU.mult)
        if c % 2 == 0 or c == NCK - 1:
            V.memset(ST[:, 8:9], 0.0).then_inc(sem("state"), 1)
            V.wait_ge(sem("state"), nth("DVE", "state"))

    with nc.Block() as block:

        @block.sync
        def _(sp):
            nc.sync.wait_ge(sem("x_zero"), nth("SP", "x_zero"))
            sp_params()
            sp.wait_ge(sem("pages"), 16)
            load_mem(sp, 0)
            sp_more_params()
            sp_win(0, "w_in_a", WIN_A, C_A)
            sp_router(0)
            sp_cmp()
            sp_sample()
            sp_wo(0)
            sp_memattn(0)
            moe("SP", 0)
            sp_layer_b()
            moe("SP", 1)

        @block.gpsimd
        def _(pool):
            pool.memset(X[:, 2, :], 0.0).then_inc(sem("x_zero"), 1)
            nc.gpsimd.wait_ge(sem("x_zero"), nth("POOL", "x_zero"))
            pool_mem(0)
            pool_proj_a()
            pool_sample()
            pool_layer_b()
            nc.gpsimd.wait_ge(sem("y"), nth("POOL", "y"))
            nc.gpsimd.dma_start(O["y_prompt"].rearrange("o (i p) d -> p (o i) d", p=P),
                                X[:, 0:2, :]).then_inc(stored, 16)
            nc.gpsimd.dma_start(O["y_sample"].rearrange("b o d -> (b o) d"), X[0:NB, 2, :]).then_inc(stored, 16)
            pool.wait_ge(stored, 16 * STORES)

        @block.scalar
        def _(act):
            AC.wait_ge(sem("st_zero"), nth("ACT", "st_zero"))
            AC.copy(ST[:, 29:30], ST[:, 31:32]).then_inc(a_free, 4)
            act_norm()
            act_mem(0)
            act_proj_a()
            act_cmp()
            act_prompt()
            act_sample()
            act_memattn(0)
            act_norm()
            act_router()
            moe("ACT", 0)
            act_layer_b()
            act_norm()
            act_router()
            moe("ACT", 1)

        @block.vector
        def _(dve):
            V.memset(ST[:, :], 0.0).then_inc(sem("st_zero"), 1)
            V.wait_ge(sem("st_zero"), nth("DVE", "st_zero"))
            V.memset(ST[:, 9:10], 0.0).then_inc(v_free, 4)
            V.wait_ge(sem("x"), nth("DVE", "x", 16 * 2))
            dve_norm(MIXG, True)
            dve_mem(0)
            dve_proj_a()
            dve_cmp()
            dve_prompt()
            dve_sample_scores()
            dve_memattn(0)
            dve_out(0)
            dve_norm(FFNG, squares=False)
            dve_router()
            moe("DVE", 0)
            V.memset(ST[:, 8:9], 0.0).then_inc(sem("moe_done"), 1)
            V.wait_ge(sem("moe_done"), nth("DVE", "moe_done"))
            dve_layer_b()
            dve_out(1)
            dve_norm(FFNG + 8, squares=False)
            dve_router()
            moe("DVE", 1)
            V.memset(ST[:, 8:9], 0.0).then_inc(sem("y"), 1)
            V.wait_ge(sem("y"), nth("DVE", "y"))

        @block.tensor
        def _(pe):
            PE.wait_ge(sem("consts"), nth("PE", "consts", 16))
            pe_norm()
            pe_mem(0)
            pe_proj_a()
            pe_cmp()
            pe_prompt()
            pe_sample_scores()
            pe_sample_values()
            pe_memattn(0)
            pe_out(0)
            pe_norm()
            pe_router()
            moe("PE", 0)
            pe_layer_b()
            pe_out(1)
            pe_norm()
            pe_router()
            moe("PE", 1)
    ctx.close()


INS = ("x_prompt", "x_sample", "cache_cmp_k", "cache_cmp_v", "cache_sel_k", "cache_sel_v", "cache_win_k",
       "cache_win_v", "cache_mem_k", "cache_mem_v", "state_rwkv", "state_shift", "page_table", "mem_prompt",
       "norm_mix", "norm_ffn", "norm_mem", "w_mem_kv", "mem_q_gain", "mem_k_gain", "w_in_a", "nsa_q_gain",
       "nsa_k_gain", "cmp_pe", "cmp_w1", "cmp_b1", "cmp_w2", "w_in_b", "rwkv_mu", "rwkv_w0", "rwkv_w_up",
       "rwkv_a0", "rwkv_a_up", "rwkv_g_up", "rwkv_k_k", "rwkv_k_a", "rwkv_r_k", "rwkv_ln_w", "rwkv_ln_b",
       "w_out", "moe_w_coarse", "moe_b_coarse", "moe_w_fine", "moe_b_fine", "moe_w_gate", "moe_w_up", "moe_w_down")
ROW = (1, 1, SEQ, G, DH)
SROW = (1, NB, 1, G, DH)
OUTS = (("y_prompt", (1, SEQ, D)), ("y_sample", (NB, 1, D)),
        ("p_cmp_k", ROW), ("p_cmp_v", ROW), ("p_sel_k", ROW), ("p_sel_v", ROW), ("p_win_k", ROW), ("p_win_v", ROW),
        ("p_mem_k", (2, 1, SEQ, MH, DH)), ("p_mem_v", (2, 1, SEQ, MH, DH)),
        ("p_rwkv", (1, 1, H, DH, DH)), ("p_shift", (1, 1, SHIFT_W)),
        ("s_cmp_k", SROW), ("s_cmp_v", SROW), ("s_sel_k", SROW), ("s_sel_v", SROW),
        ("s_win_k", (1, NB, WIN, G, DH)), ("s_win_v", (1, NB, WIN, G, DH)),
        ("s_rwkv", (1, NB, H, DH, DH)), ("s_shift", (1, NB, SHIFT_W)))

def kernel(**inputs):
    import concourse.bacc as bacc
    from concourse.bass_utils import run_bass_kernel_spmd

    nc = bacc.Bacc("TRN2", target_bir_lowering=False, num_devices=1)
    at, consts = constants()
    arrays = {name: np.ascontiguousarray(inputs[name]) for name in INS}
    arrays["consts"] = consts
    arrays["head_rows"] = np.ascontiguousarray(np.repeat(np.eye(H, dtype=np.float32), DH, axis=1))
    A = {n: nc.dram_tensor(f"in_{n}", x.shape, mybir.dt.from_np(x.dtype), kind="ExternalInput").ap()
         for n, x in arrays.items()}
    O = {n: nc.dram_tensor(f"out_{n}", shape, F32, kind="ExternalOutput").ap() for n, shape in OUTS}
    build(nc, A, O, at)
    r = run_bass_kernel_spmd(nc, [{f"in_{n}": x for n, x in arrays.items()}], core_ids=[0])
    return tuple(r.results[0][f"out_{n}"] for n, _ in OUTS)
```
